# Optimizing a Trainium2 kernel written in Bass

```python
import jax, jax.numpy as jnp
from jax import lax
import numpy as np

D_MODEL = 2048
BATCH = 1
SEQ = 256
DEPTH = 2

HEAD_DIM = 128
N_SB_HEADS = D_MODEL // (2 * HEAD_DIM)
N_FOX_HEADS = D_MODEL // (2 * HEAD_DIM)
SB_WIDTH = N_SB_HEADS * HEAD_DIM
FOX_WIDTH = N_FOX_HEADS * HEAD_DIM
IN_WIDTH = 3 * SB_WIDTH + 3 * FOX_WIDTH + N_FOX_HEADS

N_MLA_HEADS = 16
Q_LORA_RANK = 512
KV_LORA_RANK = 512
QK_NOPE_DIM = 128
QK_ROPE_DIM = 64
QK_HEAD_DIM = QK_NOPE_DIM + QK_ROPE_DIM
V_HEAD_DIM = 128
DOWN_WIDTH = Q_LORA_RANK + KV_LORA_RANK + QK_ROPE_DIM

D_FF = 4 * D_MODEL
BLOCK_Q = 128
ROPE_THETA = 10000.0
EPS = 1e-6
FORGET_BIAS_CENTER = 3.0

N_EVEN = (DEPTH + 1) // 2
N_ODD = DEPTH // 2

kernel_name = "hybrid_stickbreak_fox_mla_sqrelu"

def rmsnorm(x, g):
    x32 = x.astype(jnp.float32)
    y = x32 * lax.rsqrt(jnp.mean(x32 * x32, axis=-1, keepdims=True) + EPS)
    return (y * g.astype(jnp.float32)).astype(x.dtype)

def to_heads(t, n_heads):
    b, s, _ = t.shape
    return t.reshape(b, s, n_heads, -1).transpose(0, 2, 1, 3)

def query_blocks(q):
    b, h, s, d = q.shape
    return q.reshape(b, h, s // BLOCK_Q, BLOCK_Q, d).transpose(2, 0, 1, 3, 4)

def merge_blocks(o):
    nb, b, h, bq, d = o.shape
    return o.transpose(1, 0, 3, 2, 4).reshape(b, nb * bq, h * d)

def stick_breaking_attention(q, k, v):
    s = q.shape[2]
    scale = q.shape[-1] ** -0.5
    key_pos = jnp.arange(s)

    def one_block(args):
        qb, q0 = args
        z = jnp.einsum('bhqd,bhkd->bhqk', qb, k,
                       preferred_element_type=jnp.float32) * scale
        q_pos = q0 + jnp.arange(BLOCK_Q)
        strict = key_pos[None, :] < q_pos[:, None]
        log_beta = jax.nn.log_sigmoid(z)
        log_one_minus = jnp.where(strict, jax.nn.log_sigmoid(-z), 0.0)
        suffix = lax.cumsum(log_one_minus, axis=3, reverse=True) - log_one_minus
        w = jnp.where(strict, jnp.exp(log_beta + suffix), 0.0)
        return jnp.einsum('bhqk,bhkd->bhqd', w.astype(v.dtype), v,
                          preferred_element_type=jnp.float32).astype(v.dtype)

    starts = jnp.arange(s // BLOCK_Q, dtype=jnp.int32) * BLOCK_Q
    return merge_blocks(lax.map(one_block, (query_blocks(q), starts)))

def causal_softmax_attention(q, k, v, log_decay_cum=None):
    s = q.shape[2]
    scale = q.shape[-1] ** -0.5
    key_pos = jnp.arange(s)

    def one_block(args):
        qb, q0 = args
        logits = jnp.einsum('bhqd,bhkd->bhqk', qb, k,
                            preferred_element_type=jnp.float32) * scale
        if log_decay_cum is not None:
            f_q = lax.dynamic_slice_in_dim(log_decay_cum, q0, BLOCK_Q, axis=2)
            logits = logits + f_q[..., :, None] - log_decay_cum[..., None, :]
        q_pos = q0 + jnp.arange(BLOCK_Q)
        causal = key_pos[None, :] <= q_pos[:, None]
        p = jax.nn.softmax(jnp.where(causal, logits, -jnp.inf), axis=-1)
        return jnp.einsum('bhqk,bhkd->bhqd', p.astype(v.dtype), v,
                          preferred_element_type=jnp.float32).astype(v.dtype)

    starts = jnp.arange(s // BLOCK_Q, dtype=jnp.int32) * BLOCK_Q
    return merge_blocks(lax.map(one_block, (query_blocks(q), starts)))

def apply_rope(t, positions):
    half = t.shape[-1] // 2
    inv_freq = ROPE_THETA ** (-jnp.arange(half, dtype=jnp.float32) / half)
    ang = positions.astype(jnp.float32)[:, None, :, None] * inv_freq
    cos, sin = jnp.cos(ang), jnp.sin(ang)
    t32 = t.astype(jnp.float32)
    t1, t2 = t32[..., :half], t32[..., half:]
    return jnp.concatenate([t1 * cos - t2 * sin, t2 * cos + t1 * sin], axis=-1).astype(t.dtype)

def sb_fox_mixer(h, w_in, b_f, fox_q_g, fox_k_g, w_o):
    proj = h @ w_in
    cuts = np.cumsum([SB_WIDTH] * 3 + [FOX_WIDTH] * 3)
    q_sb, k_sb, v_sb, q_fx, k_fx, v_fx, f_logit = jnp.split(proj, cuts, axis=-1)
    o_sb = stick_breaking_attention(to_heads(q_sb, N_SB_HEADS),
                                    to_heads(k_sb, N_SB_HEADS),
                                    to_heads(v_sb, N_SB_HEADS))
    log_f = jax.nn.log_sigmoid(f_logit.astype(jnp.float32) + b_f.astype(jnp.float32))
    log_f_cum = jnp.cumsum(log_f, axis=1).transpose(0, 2, 1)
    q_f = rmsnorm(to_heads(q_fx, N_FOX_HEADS), fox_q_g)
    k_f = rmsnorm(to_heads(k_fx, N_FOX_HEADS), fox_k_g)
    o_fx = causal_softmax_attention(q_f, k_f, to_heads(v_fx, N_FOX_HEADS), log_f_cum)
    return jnp.concatenate([o_sb, o_fx], axis=-1) @ w_o

def mla_mixer(h, positions, w_down, q_a_g, kv_a_g, w_uq, w_ukv, q_g, k_g, w_o):
    b, s, _ = h.shape
    down = h @ w_down
    c_q, c_kv, k_pe = jnp.split(down, [Q_LORA_RANK, Q_LORA_RANK + KV_LORA_RANK], axis=-1)
    c_q = rmsnorm(c_q, q_a_g)
    c_kv = rmsnorm(c_kv, kv_a_g)
    q = to_heads(c_q @ w_uq, N_MLA_HEADS)
    kv = to_heads(c_kv @ w_ukv, N_MLA_HEADS)
    k_nope, v = kv[..., :QK_NOPE_DIM], kv[..., QK_NOPE_DIM:]
    k_pe = jnp.broadcast_to(k_pe[:, None], (b, N_MLA_HEADS, s, QK_ROPE_DIM))
    k = jnp.concatenate([k_nope, k_pe], axis=-1)
    q = rmsnorm(q, q_g)
    k = rmsnorm(k, k_g)
    q = jnp.concatenate([q[..., :QK_NOPE_DIM], apply_rope(q[..., QK_NOPE_DIM:], positions)], axis=-1)
    k = jnp.concatenate([k[..., :QK_NOPE_DIM], apply_rope(k[..., QK_NOPE_DIM:], positions)], axis=-1)
    o = causal_softmax_attention(q, k, v)
    return o @ w_o

def squared_relu_mlp(h, w_up, w_down):
    a = jnp.square(jax.nn.relu(h @ w_up))
    return a @ w_down

def setup_inputs(seed: int = 0) -> dict:
    key = jax.random.key(seed)
    ks = jax.random.split(key, 24)

    def dense(k, shape, fan_in):
        return jax.random.normal(k, shape, jnp.float32) * (fan_in ** -0.5)

    def gain(k, shape):
        return 1.0 + 0.02 * jax.random.normal(k, shape, jnp.float32)

    x = jax.random.normal(ks[0], (BATCH, SEQ, D_MODEL), jnp.float32)
    offsets = jax.random.randint(ks[1], (BATCH, 1), 0, 2048, dtype=jnp.int32)
    positions = offsets + jnp.arange(SEQ, dtype=jnp.int32)[None, :]
    return {
        "x": x,
        "positions": positions,
        "ln_mix_g": gain(ks[2], (DEPTH, D_MODEL)),
        "ln_mlp_g": gain(ks[3], (DEPTH, D_MODEL)),
        "sf_w_in": dense(ks[4], (N_EVEN, D_MODEL, IN_WIDTH), D_MODEL),
        "sf_b_f": FORGET_BIAS_CENTER + 0.1 * jax.random.normal(ks[5], (N_EVEN, N_FOX_HEADS), jnp.float32),
        "fox_q_g": gain(ks[6], (N_EVEN, HEAD_DIM)),
        "fox_k_g": gain(ks[7], (N_EVEN, HEAD_DIM)),
        "sf_w_o": dense(ks[8], (N_EVEN, SB_WIDTH + FOX_WIDTH, D_MODEL), SB_WIDTH + FOX_WIDTH),
        "mla_w_down": dense(ks[9], (N_ODD, D_MODEL, DOWN_WIDTH), D_MODEL),
        "mla_q_a_g": gain(ks[10], (N_ODD, Q_LORA_RANK)),
        "mla_kv_a_g": gain(ks[11], (N_ODD, KV_LORA_RANK)),
        "mla_w_uq": dense(ks[12], (N_ODD, Q_LORA_RANK, N_MLA_HEADS * QK_HEAD_DIM), Q_LORA_RANK),
        "mla_w_ukv": dense(ks[13], (N_ODD, KV_LORA_RANK, N_MLA_HEADS * (QK_NOPE_DIM + V_HEAD_DIM)), KV_LORA_RANK),
        "mla_q_g": gain(ks[14], (N_ODD, QK_HEAD_DIM)),
        "mla_k_g": gain(ks[15], (N_ODD, QK_HEAD_DIM)),
        "mla_w_o": dense(ks[16], (N_ODD, N_MLA_HEADS * V_HEAD_DIM, D_MODEL), N_MLA_HEADS * V_HEAD_DIM),
        "mlp_w_up": dense(ks[17], (DEPTH, D_MODEL, D_FF), D_MODEL),
        "mlp_w_down": dense(ks[18], (DEPTH, D_FF, D_MODEL), D_FF),
    }

def reference(x, positions, ln_mix_g, ln_mlp_g, sf_w_in, sf_b_f, fox_q_g, fox_k_g, sf_w_o,
              mla_w_down, mla_q_a_g, mla_kv_a_g, mla_w_uq, mla_w_ukv, mla_q_g, mla_k_g,
              mla_w_o, mlp_w_up, mlp_w_down):
    for layer in range(DEPTH):
        i = layer // 2
        h = rmsnorm(x, ln_mix_g[layer])
        if layer % 2 == 0:
            x = x + sb_fox_mixer(h, sf_w_in[i], sf_b_f[i], fox_q_g[i], fox_k_g[i], sf_w_o[i])
        else:
            x = x + mla_mixer(h, positions, mla_w_down[i], mla_q_a_g[i], mla_kv_a_g[i],
                              mla_w_uq[i], mla_w_ukv[i], mla_q_g[i], mla_k_g[i], mla_w_o[i])
        h = rmsnorm(x, ln_mlp_g[layer])
        x = x + squared_relu_mlp(h, mlp_w_up[layer], mlp_w_down[layer])
    return x


_drawn_inputs = setup_inputs


def setup_inputs(seed=0):
    import zlib

    import numpy as np

    out = dict(_drawn_inputs(seed))
    spreads = {}
    factors = {'ln_mix_g': 3.981,
     'sf_b_f': 40.848,
     'fox_q_g': 8.0,
     'fox_k_g': 8.0,
     'mla_q_a_g': 8.0,
     'mla_kv_a_g': 8.0,
     'mla_q_g': 8.0,
     'mla_k_g': 8.0}
    for name, (base, spread) in spreads.items():
        noise = np.random.default_rng([zlib.crc32(name.encode()), seed]).standard_normal(out[name].shape)
        drawn = base * np.exp(spread * noise) if base else spread * noise
        out[name] = __import__('jax').numpy.asarray(drawn.astype(out[name].dtype))
    for name, factor in factors.items():
        out[name] = (out[name] * factor).astype(out[name].dtype)
    return out
```

```python
from contextlib import ExitStack
import math

import numpy as np
import concourse.bass as bass
from concourse import mybir

F32 = mybir.dt.float32
F32R = mybir.dt.float32r
I32 = mybir.dt.int32
ALU = mybir.AluOpType
ACT = mybir.ActivationFunctionType
AX_X = mybir.AxisListType.X

P = 128
T = 256
TT = T // P
D = 2048
KT = D // P
HD = 128
NHG = 8
D_FF = 8192
NB = D_FF // D
RANK = 512
NOPE, ROPE = 128, 64
HALF = ROPE // 2
QKD = NOPE + ROPE
EPS = 1e-6
THETA = 10000.0
NEG = -1e30
SB_SCALE = HD ** -0.5
MLA_SCALE = QKD ** -0.5
N = 512
AHEAD = 3
SLOTS = 4

GROUPS = 4


def plan_chunks():
    def full(matrix, col, width=N, k_tiles=KT):
        return [(matrix, 4, 4 * P * l, col, width) for l in range(k_tiles // 4)]
    first = []
    for g in range(GROUPS):
        if g == 2:
            first.append(("f", "rows", [("w_in", KT, 0, 6 * NHG * HD, NHG)]))
        for j, what in enumerate("qkv"):
            first.append((f"{what}{g}", "rows", full("w_in", (3 * (g // 2) + j) * NHG * HD + (g % 2) * N)))
    for c in range(4):
        first.append((f"o{c}", "cols", full("w_o", c * N)))
    second = [("ckv", "rows", full("w_down", RANK)),
              ("kpe", "rows", [("w_down", KT, 0, 2 * RANK, ROPE)]),
              ("cq", "rows", full("w_down", 0))]
    for g in range(8):
        second.append((f"ukv{g}", "rows", full("w_ukv", g * N, N, 4)))
        second.append((f"uq{g}", "rows", full("w_uq", g * 2 * QKD, 2 * QKD, 4)))
    for c in range(4):
        second.append((f"o{c}", "cols", full("mla_w_o", c * N)))
    return first, second


MIX0, MIX1 = plan_chunks()
MLP_PIECES = NB * 64
P_MIX0 = 0
P_MLP0 = 2 * sum(len(c[2]) for c in MIX0)
P_MIX1 = P_MLP0 + MLP_PIECES
P_MLP1 = P_MIX1 + 2 * sum(len(c[2]) for c in MIX1)
P_END = P_MLP1 + MLP_PIECES


def pieces_of(chunks, start):
    out, n = {}, start
    for _, _, loads in chunks:
        for _, kts, _, _, width in loads:
            out[n] = out[n + 1] = (kts // 2, width)
            n += 2
    return out


SHAPES = {**pieces_of(MIX0, P_MIX0), **pieces_of(MIX1, P_MIX1)}


def shape_of(n):
    return SHAPES.get(n, (2, N))


def chunk_starts(chunks, start):
    out, n = {}, start
    for name, _, loads in chunks:
        out[name] = n
        n += 2 * len(loads)
    return out


AT0, AT1 = chunk_starts(MIX0, P_MIX0), chunk_starts(MIX1, P_MIX1)

ROWS0 = {c[0]: n for n, c in enumerate(x for x in MIX0 if x[1] == "rows")}
ROWS1 = {c[0]: n + len(ROWS0) for n, c in enumerate(x for x in MIX1 if x[1] == "rows")}
COLS_WO0, COLS_MLP0, COLS_WO1, COLS_MLP1 = 0, 4, 4 + 8 * NB, 8 + 8 * NB


def plan_steps():
    plan = {}

    def at(n, *steps):
        plan.setdefault(n, []).extend(steps)
    base = [AT0[f"q{g}"] for g in range(GROUPS)]
    for g in range(GROUPS):
        for e in range(4 if g else 0):
            h = 4 * (g - 1) + e
            at(base[g] + 1 + 6 * e, ("scores", h))
            at(base[g] + 3 + 6 * e, ("probs", h))
            at(base[g] + 5 + 6 * e, ("out", h))
        at(base[g] + 12, ("turn", 4 * g))
        at(base[g] + 14, ("turn", 4 * g + 1))
        at(base[g] + 20, ("turn", 4 * g + 2))
        at(base[g] + 22, ("turn", 4 * g + 3))
    for e in range(6):
        if e >= 2:
            at(AT0["o0"] + e, ("out", 12 + e - 2))
        if 1 <= e < 5:
            at(AT0["o0"] + e, ("probs", 12 + e - 1))
        if e < 4:
            at(AT0["o0"] + e, ("scores", 12 + e))
    at(AT1["ckv"] + 2, ("norm_rows", 0))
    at(AT1["cq"] + 3, ("turn_c", 0))
    at(AT1["cq"] + 5, ("turn_c", 1))
    at(AT1["ukv0"] + 1, ("turn_c", 2), ("turn_c", 3))
    for g in range(10):
        b = AT1[f"ukv{g}"] if g < 8 else AT1["o0"] + 4 * (g - 8)
        if 1 <= g < 9:
            k, q, ropes = (16 + 3 * (g - 1) + i for i in range(3))
            for j, t in zip((0, 1, 2) if g == 8 else (1, 2, 3), (k, q, ropes)):
                at(b + j, ("turn", t))
        if 2 <= g < 9:
            h = 16 + 2 * (g - 2)
            at(b, ("scores", h))
            at(b + 1, ("probs", h), ("scores", h + 1))
            at(b + 2, ("out", h), ("probs", h + 1))
            at(b + 3, ("out", h + 1))
    at(AT1["o0"] + 3, ("scores", 30))
    at(AT1["o0"] + 4, ("probs", 30), ("scores", 31))
    at(AT1["o0"] + 5, ("out", 30), ("probs", 31))
    at(AT1["o0"] + 6, ("out", 31))
    for at_, chunks in ((AT0, MIX0), (AT1, MIX1)):
        for name, kind, loads in chunks:
            if kind == "rows":
                at(at_[name] + 2 * len(loads) - 1, ("rows", name))
    return plan


STEPS = plan_steps()


def steps_after(n):
    return STEPS.get(n, [])


def build(nc, x, positions, ln_mix_g, ln_mlp_g, sf_w_in, sf_b_f, fox_q_g, fox_k_g, sf_w_o,
          mla_w_down, mla_q_a_g, mla_kv_a_g, mla_w_uq, mla_w_ukv, mla_q_g, mla_k_g, mla_w_o,
          mlp_w_up, mlp_w_down, out):
    matrices = {"w_in": sf_w_in[0], "w_o": sf_w_o[0], "w_down": mla_w_down[0], "w_ukv": mla_w_ukv[0],
                "w_uq": mla_w_uq[0], "mla_w_o": mla_w_o[0]}
    with ExitStack() as ctx:
        def sb(name, shape, dt=F32):
            return ctx.enter_context(nc.sbuf_tensor(name, shape, dt))

        def sem(name):
            return ctx.enter_context(nc.semaphore(name))

        xT = sb("xT", [P, KT, T])
        h = sb("h", [P, KT, 2, T], F32R)
        a = sb("a", [P, KT, 2, T], F32R)
        raw = sb("raw", [P, SLOTS, 4 * N])
        halves = sb("halves", [P, SLOTS, 2, 2 * N], F32R)
        nat = sb("nat", [P, 2, TT, N])
        mix = sb("mix", [P, 8192])
        heads = sb("heads", [P, 7, 3 * P])
        side = sb("side", [P, 4, P])
        ident = sb("ident", [P, P])
        ones = sb("ones", [P, P])
        tri_ge = sb("tri_ge", [P, P])
        tri_le = sb("tri_le", [P, P])
        ones_gt = sb("ones_gt", [P, 2 * P])
        sb_mask = sb("sb_mask", [P, 3 * P])
        sm_mask = sb("sm_mask", [P, 3 * P])
        gains = sb("gains", [P, 76])
        q_gain = sb("q_gain", [P, 2])
        rope_g = sb("rope_g", [P, 2, ROPE])
        b_f = sb("b_f", [P, NHG])
        fl = sb("fl", [P, 3, TT, NHG])
        log_f = sb("log_f", [P, TT, NHG])
        pos_i = sb("pos_i", [P, TT], I32)
        pos_f = sb("pos_f", [P, TT])
        inv_freq = sb("inv_freq", [P, HALF])
        rope_c = sb("rope_c", [P, 2, TT, ROPE])
        rope_s = sb("rope_s", [P, 2, TT, ROPE])
        kpe_ss = sb("kpe_ss", [P, TT])
        st = sb("st", [P, 4, 8])
        ss_x = sb("ss_x", [P, TT])
        r_tok = sb("r_tok", [P, TT])
        mx = sb("mx", [P, 2, 2])
        nmx = sb("nmx", [P, 2, 2])
        row_sum = sb("row_sum", [P, 2, 2])
        row_inv = sb("row_inv", [P, 2, 2])

        qT = mix[:, 0:2048].rearrange("p (b h t) -> p b h t", b=2, h=4)
        kT = mix[:, 2048:4096].rearrange("p (b h t) -> p b h t", b=2, h=4)
        v_tok = mix[:, 4096:6144].rearrange("p (b s n) -> p b s n", b=2, s=TT)
        qT1 = mix[:, 0:1024].rearrange("p (b h t) -> p b h t", b=2, h=2)
        kT1 = mix[:, 1024:2048].rearrange("p (b h t) -> p b h t", b=2, h=2)
        rT1 = mix[:, 2048:3072].rearrange("p (b w t) -> p b w t", b=2, w=2)
        kv_tok = mix[:, 3072:6144].rearrange("p (b s h w n) -> p b s h w n", b=3, s=TT, h=2, w=2)
        q_tok = mix[:, 6144:6912].rearrange("p (s h n) -> p s h n", s=TT, h=2)
        k_tok = mix[:, 6912:7424].rearrange("p (s h n) -> p s h n", s=TT, h=2)
        q_rot = mix[:, 7424:7936].rearrange("p (w s h n) -> p w s h n", w=2, s=TT, h=2)
        k_rot = mix[:, 7936:8192].rearrange("p (s h n) -> p s h n", s=TT, h=2)
        sq_tok = nat[:, 0].rearrange("p s n -> p (s n)")[:, 0:4 * QKD].rearrange("p (m n) -> p m n", m=4)
        vec_rows = nat[0:76, 0, 0, 0:P]
        decay = side[:].rearrange("p (b s) t -> p b s t", b=2)
        kpe = side[:, 0].rearrange("p (s n) -> p s n", s=TT)
        kpe_r = side[:, 1].rearrange("p (s n) -> p s n", s=TT)
        kpe_t = side[:, 2].rearrange("p (s n) -> p s n", s=TT)
        r2 = heads[:, 0, 0:T]
        nacc = heads[:, 1, 0:T]
        ang = heads[:, 2, 0:2 * TT * HALF].rearrange("p (w s n) -> p w s n", w=2, s=TT)
        trig_n = heads[:, 3, 0:TT * HALF].rearrange("p (s n) -> p s n", s=TT)
        trig = heads[:, 4, 0:2 * TT * HALF].rearrange("p (w s n) -> p w s n", w=2, s=TT)
        sq_sum = mix[:, 0:1024].rearrange("p (k t) -> p k t", k=4)
        sq_new = mix[:, 2048:3072].rearrange("p (k t) -> p k t", k=4)
        s_buf = nat[:, 0].rearrange("p s (k t) -> p (s k) t", t=T)
        y_buf = nat[:, 1].rearrange("p s (k t) -> p (s k) t", t=T)
        zm, e0, sp, w_t = (lambda b: heads[:, b], heads[:, 2], lambda b: heads[:, 3 + b], lambda b: heads[:, 5 + b])

        psum = ctx.enter_context(nc.psum_tensor("psum", [P, 8, N], F32))
        SCORES, PROBS, OUT, TURN = psum[:, 4], psum[:, 5], psum[:, 6], psum[:, 7]

        raw_loaded = [sem(f"raw_loaded{i}") for i in range(SLOTS)]
        x_loaded = [sem(f"x_loaded{i}") for i in range(TT)]
        vecs_loaded = sem("vecs_loaded")
        hi_done, lo_done = sem("hi_done"), sem("lo_done")
        pieces_used = sem("pieces_used")
        r_ready = sem("r_ready")
        rows_read, cols_read = sem("rows_read"), sem("cols_read")
        right_read = sem("right_read")
        consts = sem("consts")
        const_step = sem("const_step")
        x_turned, x_read = sem("x_turned"), sem("x_read")
        x_read_v = sem("x_read_v")
        gains_turned, gains_ready = sem("gains_turned"), sem("gains_ready")
        y_done, y_hi = sem("y_done"), sem("y_hi")
        split_done = sem("split_done")
        x_done = sem("x_done")
        sq_done, sq_added = sem("sq_done"), sem("sq_added")
        acc_ready = sem("acc_ready")
        norm_sum, norm_read = sem("norm_sum"), sem("norm_read")
        mlp_step = sem("mlp_step")
        rows_stat, rows_ln = sem("rows_stat"), sem("rows_ln")
        normed = sem("normed")
        trig_args, trig_done, rope_ready = sem("trig_args"), sem("trig_done"), sem("rope_ready")
        logf_in, logf_abs, logf_ln, logf_ready = sem("logf_in"), sem("logf_abs"), sem("logf_ln"), sem("logf_ready")
        turned, turn_read = sem("turned"), sem("turn_read")
        c_turned, c_hi, c_ready = sem("c_turned"), sem("c_hi"), sem("c_ready")
        q_scaled, q_roped = sem("q_scaled"), sem("q_roped")
        pool_step = sem("pool_step")
        scores_done, scores_read = sem("scores_done"), sem("scores_read")
        decay_ready = sem("decay_ready")
        max_ready = sem("max_ready")
        exp_done = sem("exp_done")
        probs_ready = sem("probs_ready")
        probs_turned, probs_read, probs_t = sem("probs_turned"), sem("probs_read"), sem("probs_t")
        out_done, out_hi, out_ready = sem("out_done"), sem("out_hi"), sem("out_ready")
        act_step, dve_step = sem("act_step"), sem("dve_step")
        x_final, out_turned, out_stored = sem("x_final"), sem("out_turned"), sem("out_stored")
        out_read, out_read_v = sem("out_read"), sem("out_read_v")

        block = ctx.enter_context(nc.Block())

        def flat(kts, width):
            return kts * width

        def raw_piece(n):
            kts, width = shape_of(n)
            size = flat(kts, width)
            return raw[:, (n // 2) % SLOTS, (n % 2) * size:(n % 2 + 1) * size]

        def half_piece(n, which):
            kts, width = shape_of(n)
            return halves[:, n % SLOTS, which, 0:flat(kts, width)]

        @block.sync
        def _(sp_):
            def free_slot(load, extra=0):
                if load >= SLOTS:
                    sp_.wait_ge(lo_done, 2 * load - 2 * SLOTS + 2 + 2 * extra)
                    if not isinstance(extra, int):
                        sp_.nop()

            def straight(chunks, load):
                for _, _, loads in chunks:
                    for matrix, kts, row, col, width in loads:
                        if load in (2, 3):
                            sp_.wait_ge(x_turned, 8)
                            sp_.wait_ge(act_step, 2)
                        free_slot(load)
                        dst = raw[:, load % SLOTS, 0:kts * width].rearrange("p (k n) -> p k n", k=kts)
                        src = matrices[matrix][row:row + kts * P, col:col + width].rearrange("(k p) n -> p k n", p=P)
                        sp_.dma_start(dst, src).then_inc(raw_loaded[load % SLOTS], 16)
                        load += 1

            def mlp(layer, load0):
                w_up, w_down = mlp_w_up[layer], mlp_w_down[layer]
                with sp_.Fori(0, NB) as b:
                    for c in range(8):
                        for l in range(4):
                            load = load0 + 4 * c + l
                            free_slot(load, 32 * b)
                            dst = raw[:, load % SLOTS].rearrange("p (k n) -> p k n", k=4)
                            if c < 4:
                                src = w_up[4 * P * l:4 * P * (l + 1), bass.ds(b * D + c * N, N)]
                            else:
                                src = w_down[bass.ds(b * D + 4 * P * l, 4 * P), (c - 4) * N:(c - 3) * N]
                            sp_.dma_start(dst, src.rearrange("(k p) n -> p k n", p=P))\
                               .then_inc(raw_loaded[load % SLOTS], 16)

            for tt in range(TT):
                sp_.dma_start(raw[:, 2 + tt, :], x[0, tt * P:(tt + 1) * P, :]).then_inc(x_loaded[tt], 16)
            straight(MIX0, 0)
            mlp(0, P_MLP0 // 2)
            straight(MIX1, P_MIX1 // 2)
            mlp(1, P_MLP1 // 2)
            for c in range(4):
                sp_.wait_ge(out_read, c + 1)
                sp_.wait_ge(out_read_v, c + 1)
                sp_.dma_start(out[0, :, c * N:(c + 1) * N].rearrange("(s p) n -> p s n", p=P),
                              raw[:, c, 0:2 * N].rearrange("p (s n) -> p s n", s=TT)).then_inc(out_stored, 16)
            sp_.wait_ge(out_stored, 64)

        @block.gpsimd
        def _(pool):
            made = [0]

            def own(ins):
                made[0] += 1
                ins.then_inc(const_step, 1)
                pool.wait_ge(const_step, made[0])

            own(pool.memset(ident[:], 0.0))
            pool.affine_select(out=ident[:], in_=ident[:], compare_op=ALU.not_equal, fill=1.0, base=0,
                               pattern=[[-1, P]], channel_multiplier=1).then_inc(consts, 1)
            own(pool.memset(ones[:], 1.0))
            pool.memset(ones_gt[:, 0:P], 1.0)
            own(pool.memset(sb_mask[:], 0.0))
            own(pool.memset(sm_mask[:], 0.0))
            pool.affine_select(out=tri_ge[:], in_=ones[:], compare_op=ALU.is_ge, fill=0.0, base=0,
                               pattern=[[-1, P]], channel_multiplier=1)
            pool.affine_select(out=tri_le[:], in_=ones[:], compare_op=ALU.is_ge, fill=0.0, base=0,
                               pattern=[[1, P]], channel_multiplier=-1)
            pool.affine_select(out=ones_gt[:, P:2 * P], in_=ones[:], compare_op=ALU.is_gt, fill=0.0, base=0,
                               pattern=[[-1, P]], channel_multiplier=1)
            for c in (0, 2 * P):
                pool.affine_select(out=sb_mask[:, c:c + P], in_=sb_mask[:, c:c + P], compare_op=ALU.is_gt,
                                   fill=NEG, base=0, pattern=[[1, P]], channel_multiplier=-1)
                last = pool.affine_select(out=sm_mask[:, c:c + P], in_=sm_mask[:, c:c + P], compare_op=ALU.is_ge,
                                          fill=NEG, base=0, pattern=[[-1, P]], channel_multiplier=1)
            last.then_inc(consts, 1)

            pool.wait_ge(logf_ready, 1)
            for n in range(NHG):
                if n >= 2:
                    pool.wait_ge(scores_done, NHG + n - 1)
                for tt in range(TT):
                    ins = pool.tensor_scalar(decay[:, n % 2, tt], tri_le[:], log_f[:, tt, n:n + 1], None, ALU.mult)
                ins.then_inc(decay_ready, 1)

            pool.wait_ge(rope_ready, 1)
            step = [0]

            def mine(ins):
                step[0] += 1
                ins.then_inc(pool_step, 1)
                pool.wait_ge(pool_step, step[0])
            for g in range(8):
                pool.wait_ge(q_scaled, g + 1)
                for tt in range(TT):
                    q = q_tok[:, tt, :, NOPE:QKD]
                    cs = rope_c[:, 0, tt].unsqueeze(1).broadcast_to([P, 2, ROPE])
                    s1 = rope_s[:, 0, tt, 0:HALF].unsqueeze(1).broadcast_to([P, 2, HALF])
                    s2 = rope_s[:, 0, tt, HALF:ROPE].unsqueeze(1).broadcast_to([P, 2, HALF])
                    pool.tensor_tensor(q_rot[:, 0, tt], q, cs, ALU.mult)
                    pool.tensor_tensor(q_rot[:, 1, tt, :, 0:HALF], q[:, :, HALF:ROPE], s1, ALU.mult)
                    ins = pool.tensor_tensor(q_rot[:, 1, tt, :, HALF:ROPE], q[:, :, 0:HALF], s2, ALU.mult)
                mine(ins)
                pool.tensor_tensor(q_rot[:, 0], q_rot[:, 0], q_rot[:, 1], ALU.add).then_inc(q_roped, 1)
                pool.wait_ge(q_roped, g + 1)

        @block.scalar
        def _(act):
            own_steps = [0]

            def own(ins):
                own_steps[0] += 1
                ins.then_inc(act_step, 1)
                act.wait_ge(act_step, own_steps[0])

            def split_hi(n, extra=0):
                if n % 2 == 0:
                    act.wait_ge(raw_loaded[(n // 2) % SLOTS], 16 * (n // 2 // SLOTS + 1) + 16 // (2 * SLOTS) * extra)
                if n >= SLOTS:
                    act.wait_ge(pieces_used, n - SLOTS + 1 + extra)
                nc.scalar.copy(half_piece(n, 0), raw_piece(n)).then_inc(hi_done, 1)

            powers = [0]

            def power(m):
                powers[0] += 1
                act.wait_ge(rows_stat, powers[0])
                own(nc.scalar.activation(st[:, 3, 0:m], st[:, 1, 0:m], ACT.Ln))
                nc.scalar.activation(st[:, 2, 0:m], st[:, 3, 0:m], ACT.Exp, scale=-0.5).then_inc(rows_ln, 1)

            ys = [0]

            def round_y(dst):
                ys[0] += 1
                act.wait_ge(y_done, ys[0])
                nc.scalar.copy(dst, y_buf).then_inc(y_hi, 1)

            vec = [(ln_mix_g.rearrange("l (k p) -> (l k) p", p=P), 0, 32), (ln_mlp_g.rearrange("l (k p) -> (l k) p", p=P), 32, 32),
                   (fox_q_g, 64, 1), (fox_k_g, 65, 1), (mla_q_a_g.rearrange("a (k p) -> (a k) p", p=P), 66, 4),
                   (mla_kv_a_g.rearrange("a (k p) -> (a k) p", p=P), 70, 4), (mla_q_g[:, 0:NOPE], 74, 1), (mla_k_g[:, 0:NOPE], 75, 1)]
            for src, row, count in vec:
                act.dma_start(nat[row:row + count, 0, 0, 0:P], src).then_inc(vecs_loaded, 16)
            act.dma_start(rope_g[:, 0, :], mla_q_g[0, NOPE:QKD].partition_broadcast(P)).then_inc(vecs_loaded, 16)
            act.dma_start(rope_g[:, 1, :], mla_k_g[0, NOPE:QKD].partition_broadcast(P)).then_inc(vecs_loaded, 16)
            act.dma_start(b_f[:], sf_b_f[0].partition_broadcast(P)).then_inc(vecs_loaded, 16)
            act.dma_start(pos_i[:], positions[0].rearrange("(s p) -> p s", p=P),
                          allow_slow_non_contiguous=True).then_inc(vecs_loaded, 16)

            for tt in range(TT):
                act.wait_ge(x_loaded[tt], 16)
                own(nc.scalar.activation(a[:, 8 * tt:8 * tt + 4].rearrange("p k s t -> p (k s t)"), raw[:, 2 + tt], ACT.Square,
                                         accum_out=ss_x[:, tt:tt + 1]))
            for c in range(4):
                act.wait_ge(x_turned, 2 * c + 1)
                nc.scalar.copy(xT[:, 4 * c:4 * c + 4, 0:P], psum[:, 2 * c].rearrange("p (k t) -> p k t", k=4))\
                  .then_inc(x_read, 1)
            for n in range(AHEAD):
                split_hi(n)
            for c in range(4):
                round_y(h[:, 4 * c:4 * c + 4, 0, :])

            act.wait_ge(trig_args, 1)
            nc.scalar.activation(trig, ang, ACT.Sin).then_inc(trig_done, 1)
            act.preload_act_table_set("natural_log_exp_and_others")
            power(TT)

            def evict(dst, src, scale=None):
                if scale is None:
                    return nc.scalar.copy(dst, src)
                return nc.scalar.activation(dst, src, ACT.Copy, scale=scale)

            def rows(name, last_piece, no):
                act.wait_ge(pieces_used, last_piece + 1)
                act.wait_ge(r_ready, 1 + (no >= len(ROWS0)))
                banks = [psum[:, 2 * (no % 2) + tt] for tt in range(TT)]
                for tt in range(TT):
                    r = r_tok[:, tt:tt + 1]
                    if name[0] in "qk" and name != "kpe":
                        ins = evict(nat[:, "qk".index(name[0]), tt], banks[tt], r)
                    elif name[0] == "v":
                        ins = evict(v_tok[:, int(name[1]) % 2, tt], banks[tt], r)
                    elif name == "f":
                        ins = evict(fl[:, 0, tt], banks[tt][:, 0:NHG], r)
                    elif name == "ckv":
                        ins = evict(nat[:, 0, tt], banks[tt], r)
                    elif name == "cq":
                        ins = evict(nat[:, 1, tt], banks[tt], r)
                    elif name == "kpe":
                        ins = evict(kpe[:, tt], banks[tt][:, 0:ROPE], r)
                    elif name[:3] == "ukv":
                        ins = evict(kv_tok[:, int(name[3]) % 3, tt].rearrange("p h w n -> p (h w n)"), banks[tt])
                    else:
                        ins = evict(q_tok[:, tt].rearrange("p h n -> p (h n)"), banks[tt][:, 0:2 * QKD])
                ins.then_inc(rows_read, 1)
                if name == "f":
                    act.wait_ge(logf_in, 1)
                    own(nc.scalar.activation(fl[:, 2], fl[:, 1], ACT.Abs))
                    own(nc.scalar.activation(fl[:, 0], fl[:, 2], ACT.Exp, scale=-1.0))
                    nc.scalar.activation(fl[:, 2], fl[:, 0], ACT.Ln, bias=1.0).then_inc(logf_ln, 1)
                if name in ("q2", "k2", "q3", "k3"):
                    power(8)
                elif name in ("ckv", "cq"):
                    power(TT)
                elif name[:2] == "uq":
                    power(8)

            def turn(t):
                act.wait_ge(turned, t + 1)
                if t < 16:
                    g, what, half = t // 4, (t % 4) // 2, t % 2
                    dst = (qT, kT)[what][:, g % 2, 2 * half:2 * half + 2]
                    scale = ((SB_SCALE, None), (q_gain[:, 0:1], gains[:, 65:66]))[g // 2][what]
                    ins = evict(dst, TURN.rearrange("p (h t) -> p h t", h=2), scale)
                else:
                    g, what = (t - 16) // 3, (t - 16) % 3
                    dst = (kT1, qT1, rT1)[what][:, g % 2]
                    scale = (gains[:, 75:76], q_gain[:, 1:2], None)[what]
                    ins = evict(dst, TURN.rearrange("p (h t) -> p h t", h=2), scale)
                ins.then_inc(turn_read, 1)

            def turn_c(n):
                act.wait_ge(c_turned, n + 1)
                for i in range(2):
                    k = 2 * n + i
                    col = (70 if n < 2 else 66) + k % 4
                    ins = nc.scalar.activation(h[:, k, 0], psum[:, 7 - n % 2, i * T:(i + 1) * T], ACT.Copy,
                                               scale=gains[:, col:col + 1])
                ins.then_inc(c_hi, 1)

            def scores(n):
                b = n % 2
                if n < NHG:
                    act.wait_ge(scores_read, n + 1)
                    own(nc.scalar.activation(e0, zm(b), ACT.Abs))
                    own(nc.scalar.activation(w_t(b), e0, ACT.Exp, scale=-1.0))
                    nc.scalar.activation(e0, w_t(b), ACT.Ln, bias=1.0).then_inc(exp_done, 1)
                else:
                    act.wait_ge(max_ready, n - NHG + 1)
                    nc.scalar.activation(sp(b)[:, 0:P], zm(b)[:, 0:P], ACT.Exp, bias=nmx[:, b, 0:1],
                                         accum_out=row_sum[:, b, 0:1])
                    nc.scalar.activation(sp(b)[:, P:3 * P], zm(b)[:, P:3 * P], ACT.Exp, bias=nmx[:, b, 1:2],
                                         accum_out=row_sum[:, b, 1:2]).then_inc(exp_done, 1)

            def probs(n):
                b = n % 2
                if n < NHG:
                    act.wait_ge(probs_read, n + 1)
                    nc.scalar.activation(w_t(b), zm(b), ACT.Exp).then_inc(probs_t, 1)
                else:
                    act.wait_ge(probs_turned, n + 1)
                    nc.scalar.copy(w_t(b), PROBS[:, 0:3 * P]).then_inc(probs_t, 1)

            def head_out(n):
                act.wait_ge(out_done, n + 1)
                nc.scalar.copy(a[:, n % KT, 0], OUT[:, 0:T]).then_inc(out_hi, 1)

            def right_half(cols, end):
                act.wait_ge(pieces_used, end)
                nc.scalar.copy(s_buf, psum[:, 4 * (cols % 2):4 * (cols % 2) + 4, T:2 * T]).then_inc(right_read, 1)

            def next_norm(c, xs):
                norm = xs // 4
                round_y(h[:, 4 * c:4 * c + 4, 0, :])
                act.wait_ge(x_done, xs + 1)
                if c == 0 and norm:
                    act.wait_ge(acc_ready, norm)
                if c and 3 * norm + c - 1:
                    act.wait_ge(sq_added, 3 * norm + c - 1)
                nc.scalar.activation(sq_new if c else sq_sum, xT[:, 4 * c:4 * c + 4], ACT.Square).then_inc(sq_done, 1)

            def mixer(chunks, start, rows_no, cols0, xs0):
                n = start
                for name, kind, loads in chunks:
                    for j in range(2 * len(loads)):
                        split_hi(n + AHEAD)
                        for what, arg in steps_after(n):
                            if what == "rows":
                                rows(arg, n, rows_no[arg])
                            elif what == "norm_rows":
                                power(TT)
                            else:
                                {"turn": turn, "turn_c": turn_c, "scores": scores, "probs": probs,
                                 "out": head_out}[what](arg)
                        n += 1
                    if kind == "cols":
                        c = int(name[1])
                        right_half(cols0 + c, n)
                        next_norm(c, xs0 + c)

            def mlp_block(base, cols0, blk, final, last_layer, y0):
                for c in range(8):
                    for j in range(8):
                        n = base + 8 * c + j + AHEAD
                        if not (last_layer and final and c == 7 and j >= 8 - AHEAD):
                            split_hi(n, 64 * blk)
                    right_half(cols0 + c, base + 8 * c + 8 + 64 * blk)
                    if c < 4:
                        act.wait_ge(y_done, y0 + c + 1 + 4 * blk)
                        nc.scalar.copy(a[:, 4 * c:4 * c + 4, 0, :], y_buf).then_inc(y_hi, 1)
                    elif final and not last_layer:
                        ys[0] = y0 + 4 * NB + c - 4
                        next_norm(c - 4, 4 + c - 4)

            def mlp(base, cols0, last_layer):
                y0 = ys[0]
                with act.Fori(0, NB - 1) as blk:
                    mlp_block(base, cols0, blk, False, last_layer, y0)
                mlp_block(base, cols0, NB - 1, True, last_layer, y0)

            mixer(MIX0, P_MIX0, ROWS0, COLS_WO0, 0)
            mlp(P_MLP0, COLS_MLP0, False)
            mixer(MIX1, P_MIX1, ROWS1, COLS_WO1, 8)
            mlp(P_MLP1, COLS_MLP1, True)
            for c in range(4):
                act.wait_ge(out_turned, 2 * c + 1)
                nc.scalar.copy(raw[:, c, 0:N], psum[:, 2 * c]).then_inc(out_read, 1)

        @block.vector
        def _(dve):
            own_steps = [0]

            def own(ins):
                own_steps[0] += 1
                ins.then_inc(dve_step, 1)
                dve.wait_ge(dve_step, own_steps[0])

            v = nc.vector

            def split_lo(n, extra=0):
                dve.wait_ge(hi_done, n + 1 + extra)
                v.tensor_tensor(half_piece(n, 1), raw_piece(n), half_piece(n, 0).bitcast(F32), ALU.subtract)\
                 .then_inc(lo_done, 1)

            stats = [0]

            def power(m, inv_count):
                v.tensor_scalar(st[:, 1, 0:m], st[:, 0, 0:m], inv_count, EPS, ALU.mult, ALU.add).then_inc(rows_stat, 1)
                stats[0] += 1
                dve.wait_ge(rows_stat, stats[0])
                dve.wait_ge(rows_ln, stats[0])
                own(v.tensor_tensor(st[:, 3, 0:m], st[:, 2, 0:m], st[:, 2, 0:m], ALU.mult))
                own(v.tensor_tensor(st[:, 3, 0:m], st[:, 3, 0:m], st[:, 1, 0:m], ALU.mult))
                own(v.tensor_scalar(st[:, 3, 0:m], st[:, 3, 0:m], -0.5, 1.5, ALU.mult, ALU.add))

            splits = [0]
            ys = [0]

            def split_y(dst_lo, dst_hi):
                ys[0] += 1
                dve.wait_ge(y_hi, ys[0])
                v.tensor_tensor(dst_lo, y_buf, dst_hi.bitcast(F32), ALU.subtract).then_inc(split_done, 1)

            def gained(c, gain_col):
                g = gains[:, gain_col + 4 * c:gain_col + 4 * c + 4].unsqueeze(2).broadcast_to([P, 4, T])
                if ys[0]:
                    dve.wait_ge(split_done, ys[0])
                v.tensor_tensor(y_buf, xT[:, 4 * c:4 * c + 4], g, ALU.mult).then_inc(y_done, 1)
                dve.wait_ge(y_done, ys[0] + 1)
                split_y(h[:, 4 * c:4 * c + 4, 1, :], h[:, 4 * c:4 * c + 4, 0, :])

            dve.wait_ge(gains_turned, 1)
            own(v.tensor_copy(gains[:], psum[:, 1, 0:76]))
            v.tensor_scalar(q_gain[:, 0:1], gains[:, 64:65], SB_SCALE, None, ALU.mult)
            v.tensor_scalar(q_gain[:, 1:2], gains[:, 74:75], MLA_SCALE, None, ALU.mult).then_inc(gains_ready, 1)

            for i in range(HALF):
                v.memset(inv_freq[:, i:i + 1], float(np.float32(THETA ** (-i / HALF))))
            dve.wait_ge(vecs_loaded, 16 * 12)
            own(v.tensor_copy(pos_f[:], pos_i[:]))
            for tt in range(TT):
                ins = v.tensor_scalar(ang[:, 0, tt], inv_freq[:], pos_f[:, tt:tt + 1], None, ALU.mult)
            own(ins)
            magic = 1.5 * 2.0 ** 23
            parts, rest = [], 2 * math.pi
            for bits in (5, 14, 25, 40):
                part = math.floor(rest * 2.0 ** bits) / 2.0 ** bits
                parts.append(part)
                rest -= part
            for stride in (4096.0, 1.0):
                own(v.tensor_scalar(trig_n, ang[:, 0], 1.0 / (2 * math.pi * stride), magic, ALU.mult, ALU.add))
                own(v.tensor_scalar(trig_n, trig_n, -magic, None, ALU.add))
                for part in parts:
                    own(v.scalar_tensor_tensor(out=ang[:, 0], in0=trig_n, scalar=-part * stride, in1=ang[:, 0],
                                               op0=ALU.mult, op1=ALU.add))
            own(v.tensor_scalar(ang[:, 1], ang[:, 0], math.pi / 2, None, ALU.add))
            own(v.tensor_scalar(trig_n, ang[:, 1], math.pi, -2 * math.pi, ALU.is_gt, ALU.mult))
            own(v.tensor_tensor(ang[:, 1], ang[:, 1], trig_n, ALU.add))
            limit = float(np.nextafter(np.float32(math.pi), np.float32(0)))
            v.tensor_scalar(ang, ang, limit, -limit, ALU.min, ALU.max).then_inc(trig_args, 1)

            for c in range(4):
                dve.wait_ge(x_turned, 2 * c + 2)
                v.tensor_copy(xT[:, 4 * c:4 * c + 4, P:T], psum[:, 2 * c + 1].rearrange("p (k t) -> p k t", k=4))\
                 .then_inc(x_read_v, 1)
            for n in range(AHEAD):
                split_lo(n)
            for c in range(4):
                dve.wait_ge(x_read, c + 1)
                dve.wait_ge(x_read_v, c + 1)
                gained(c, 0)

            dve.wait_ge(trig_done, 1)
            for i, scale in ((0, MLA_SCALE), (1, 1.0)):
                g1 = rope_g[:, i, 0:HALF].unsqueeze(1).broadcast_to([P, TT, HALF])
                g2 = rope_g[:, i, HALF:ROPE].unsqueeze(1).broadcast_to([P, TT, HALF])
                for dst, j, s, g in ((rope_c[:, i, :, 0:HALF], 1, scale, g1), (rope_c[:, i, :, HALF:ROPE], 1, scale, g2),
                                     (rope_s[:, i, :, 0:HALF], 0, -scale, g2), (rope_s[:, i, :, HALF:ROPE], 0, scale, g1)):
                    ins = v.scalar_tensor_tensor(out=dst, in0=trig[:, j], scalar=s, in1=g, op0=ALU.mult, op1=ALU.mult)
            ins.then_inc(rope_ready, 1)
            dve.wait_ge(rope_ready, 1)

            dve.wait_ge(act_step, 2)
            own(v.tensor_copy(st[:, 0, 0:TT], ss_x[:]))
            power(TT, 1.0 / D)
            v.tensor_tensor(r_tok[:], st[:, 3, 0:TT], st[:, 2, 0:TT], ALU.mult).then_inc(r_ready, 1)


            normed_no = [0]

            def rows(name, no):
                if name == "f":
                    dve.wait_ge(rows_read, no + 1)
                    bias = b_f[:].unsqueeze(1).broadcast_to([P, TT, NHG])
                    v.tensor_tensor(fl[:, 1], fl[:, 0], bias, ALU.add).then_inc(logf_in, 1)
                    dve.wait_ge(logf_in, 1)
                    dve.wait_ge(logf_ln, 1)
                    v.scalar_tensor_tensor(out=log_f[:], in0=fl[:, 1], scalar=0.0, in1=fl[:, 2],
                                           op0=ALU.min, op1=ALU.subtract).then_inc(logf_ready, 1)
                elif name in ("q2", "k2", "q3", "k3"):
                    w = nat[:, "qk".index(name[0])].rearrange("p s (h n) -> p (s h) n", n=HD)
                    sq = mix[:, 6144:7168].rearrange("p (m n) -> p m n", m=8)
                    dve.wait_ge(rows_read, no + 1)
                    own(v.tensor_tensor(sq, w, w, ALU.mult))
                    own(v.tensor_reduce(st[:, 0, 0:8], sq, AX_X, ALU.add))
                    power(8, 1.0 / HD)
                    own(v.tensor_tensor(st[:, 3], st[:, 3], st[:, 2], ALU.mult))
                    v.tensor_tensor(w, w, st[:, 3].unsqueeze(2).broadcast_to([P, 8, HD]), ALU.mult)\
                     .then_inc(normed, 1)
                    normed_no[0] += 1
                    dve.wait_ge(normed, normed_no[0])
                elif name in ("ckv", "cq"):
                    w = nat[:, ("ckv", "cq").index(name)]
                    sq = mix[:, 7168:8192].rearrange("p (s n) -> p s n", s=TT)
                    dve.wait_ge(rows_read, no + 1)
                    own(v.tensor_tensor(sq, w, w, ALU.mult))
                    own(v.tensor_reduce(st[:, 0, 0:TT], sq, AX_X, ALU.add))
                    power(TT, 1.0 / RANK)
                    own(v.tensor_tensor(st[:, 3, 0:TT], st[:, 3, 0:TT], st[:, 2, 0:TT], ALU.mult))
                    v.tensor_tensor(w, w, st[:, 3, 0:TT].unsqueeze(2).broadcast_to([P, TT, N]), ALU.mult)\
                     .then_inc(normed, 1)
                    normed_no[0] += 1
                    dve.wait_ge(normed, normed_no[0])
                elif name == "kpe":
                    dve.wait_ge(rows_read, no + 1)
                    own(v.tensor_tensor(kpe_t, kpe, kpe, ALU.mult))
                    own(v.tensor_reduce(kpe_ss[:], kpe_t, AX_X, ALU.add))
                    v.tensor_tensor(kpe_r, kpe, rope_c[:, 1], ALU.mult)
                    v.tensor_tensor(kpe_t[:, :, 0:HALF], kpe[:, :, HALF:ROPE], rope_s[:, 1, :, 0:HALF], ALU.mult)
                    own(v.tensor_tensor(kpe_t[:, :, HALF:ROPE], kpe[:, :, 0:HALF], rope_s[:, 1, :, HALF:ROPE], ALU.mult))
                    own(v.tensor_tensor(kpe_r, kpe_r, kpe_t, ALU.add))
                elif name[:3] == "ukv":
                    k = kv_tok[:, int(name[3]) % 3, :, :, 0]
                    sq = sq_tok[:, :, 0:NOPE].rearrange("p (s h) n -> p s h n", s=TT)
                    dve.wait_ge(rows_read, no + 1)
                    own(v.tensor_tensor(sq, k, k, ALU.mult))
                    own(v.tensor_reduce(st[:, 0, 4:8].rearrange("p (s h) -> p s h", s=TT), sq, AX_X, ALU.add))
                elif name[:2] == "uq":
                    g = int(name[2])
                    q = q_tok.rearrange("p s h n -> p (s h) n")
                    dve.wait_ge(rows_read, no + 1)
                    own(v.tensor_tensor(sq_tok, q, q, ALU.mult))
                    v.tensor_reduce(st[:, 0, 0:4], sq_tok, AX_X, ALU.add)
                    own(v.tensor_tensor(st[:, 0, 4:8].rearrange("p (s h) -> p s h", s=TT),
                                        st[:, 0, 4:8].rearrange("p (s h) -> p s h", s=TT),
                                        kpe_ss[:].unsqueeze(2).broadcast_to([P, TT, 2]), ALU.add))
                    power(8, 1.0 / QKD)
                    own(v.tensor_tensor(st[:, 3], st[:, 3], st[:, 2], ALU.mult))
                    v.tensor_tensor(q, q, st[:, 3, 0:4].unsqueeze(2).broadcast_to([P, 4, QKD]), ALU.mult)\
                     .then_inc(q_scaled, 1)
                    rk = st[:, 3, 4:8].rearrange("p (s h) -> p s h", s=TT)
                    v.tensor_tensor(k_rot, kpe_r.unsqueeze(2).broadcast_to([P, TT, 2, ROPE]),
                                    rk.unsqueeze(3).broadcast_to([P, TT, 2, ROPE]), ALU.mult)
                    v.tensor_tensor(k_tok, kv_tok[:, g % 3, :, :, 0], rk.unsqueeze(3).broadcast_to([P, TT, 2, NOPE]),
                                    ALU.mult).then_inc(normed, 1)
                    normed_no[0] += 1
                    dve.wait_ge(normed, normed_no[0])

            def norm_rows():
                dve.wait_ge(norm_sum, 1 + NB)
                own(v.tensor_copy(st[:, 0, 0:TT], OUT[:, 0:TT]))
                power(TT, 1.0 / D)
                v.tensor_tensor(r_tok[:], st[:, 3, 0:TT], st[:, 2, 0:TT], ALU.mult).then_inc(r_ready, 1)

            def turn_c(n):
                dve.wait_ge(c_hi, n + 1)
                for i in range(2):
                    k = 2 * n + i
                    col = (70 if n < 2 else 66) + k % 4
                    ins = v.scalar_tensor_tensor(out=h[:, k, 1], in0=psum[:, 7 - n % 2, i * T:(i + 1) * T],
                                                 scalar=gains[:, col:col + 1], in1=h[:, k, 0].bitcast(F32),
                                                 op0=ALU.mult, op1=ALU.subtract)
                ins.then_inc(c_ready, 1)

            def scores(n):
                b = n % 2
                dve.wait_ge(scores_done, n + 1)
                if n < NHG:
                    v.tensor_tensor(zm(b), SCORES[:, 0:3 * P], sb_mask[:], ALU.add).then_inc(scores_read, 1)
                    dve.wait_ge(scores_read, n + 1)
                    dve.wait_ge(exp_done, n + 1)
                    v.scalar_tensor_tensor(out=sp(b), in0=zm(b), scalar=0.0, in1=e0, op0=ALU.max, op1=ALU.add)\
                     .then_inc(probs_ready, 1)
                else:
                    for i, c0, c1 in ((0, 0, P), (1, P, 3 * P)):
                        ins = v.tensor_tensor_reduce(out=zm(b)[:, c0:c1], in0=SCORES[:, c0:c1], in1=sm_mask[:, c0:c1],
                                                     scale=1.0, scalar=-3.0e38, op0=ALU.add, op1=ALU.max,
                                                     accum_out=mx[:, b, i:i + 1])
                    ins.then_inc(scores_read, 1)
                    dve.wait_ge(scores_read, n + 1)
                    v.tensor_scalar(nmx[:, b], mx[:, b], -1.0, None, ALU.mult).then_inc(max_ready, 1)
                    dve.wait_ge(exp_done, n + 1)
                    own(v.reciprocal(row_inv[:, b], row_sum[:, b]))
                    v.tensor_scalar(sp(b)[:, 0:P], sp(b)[:, 0:P], row_inv[:, b, 0:1], None, ALU.mult)
                    v.tensor_scalar(sp(b)[:, P:3 * P], sp(b)[:, P:3 * P], row_inv[:, b, 1:2], None, ALU.mult)\
                     .then_inc(probs_ready, 1)

            def probs(n):
                if n < NHG:
                    b = n % 2
                    dve.wait_ge(probs_turned, n + 1)
                    v.tensor_tensor(zm(b), zm(b), PROBS[:, 0:3 * P], ALU.subtract).then_inc(probs_read, 1)

            def head_out(n):
                dve.wait_ge(out_hi, n + 1)
                v.tensor_tensor(a[:, n % KT, 1], OUT[:, 0:T], a[:, n % KT, 0].bitcast(F32), ALU.subtract)\
                 .then_inc(out_ready, 1)

            def next_norm(c, xs, gain_col):
                gained(c, gain_col)
                norm = xs // 4
                dve.wait_ge(sq_done, xs + 1)
                if c:
                    v.tensor_tensor(sq_sum, sq_sum, sq_new, ALU.add).then_inc(sq_added, 1)
                    dve.wait_ge(sq_added, 3 * norm + c)
                if c == 3:
                    own(v.tensor_tensor(sq_sum[:, 0:2], sq_sum[:, 0:2], sq_sum[:, 2:4], ALU.add))
                    v.tensor_tensor(nacc, sq_sum[:, 0], sq_sum[:, 1], ALU.add).then_inc(acc_ready, 1)

            def mixer(chunks, start, rows_no, cols0, xs0, gain_col):
                n = start
                for name, kind, loads in chunks:
                    for j in range(2 * len(loads)):
                        split_lo(n + AHEAD)
                        for what, arg in steps_after(n):
                            if what == "rows":
                                rows(arg, rows_no[arg])
                            elif what == "norm_rows":
                                norm_rows()
                            elif what != "turn":
                                {"turn_c": turn_c, "scores": scores, "probs": probs, "out": head_out}[what](arg)
                        n += 1
                    if kind == "cols":
                        c = int(name[1])
                        xc = xT[:, 4 * c:4 * c + 4]
                        bank = 4 * ((cols0 + c) % 2)
                        dve.wait_ge(right_read, cols0 + c + 1)
                        v.tensor_tensor(y_buf, psum[:, bank:bank + 4, 0:T], s_buf, ALU.add).then_inc(cols_read, 1)
                        dve.wait_ge(cols_read, cols0 + c + 1)
                        v.tensor_tensor(xc, xc, y_buf, ALU.add).then_inc(x_done, 1)
                        dve.wait_ge(x_done, xs0 + c + 1)
                        next_norm(c, xs0 + c, gain_col)

            def mlp_block(base, cols0, blk, final, layer, y0):
                last_layer = layer == 1
                for c in range(8):
                    for j in range(8):
                        n = base + 8 * c + j + AHEAD
                        if not (last_layer and final and c == 7 and j >= 8 - AHEAD):
                            split_lo(n, 64 * blk)
                        if c == 4 and j == 5:
                            dve.wait_ge(norm_sum, (NB + 1) * layer + 1 + blk)
                            v.tensor_scalar(r2, psum[:, 4, 0:T], 1.0 / D, EPS, ALU.mult, ALU.add)\
                             .then_inc(norm_read, 1)
                            dve.wait_ge(norm_read, NB * layer + 1 + blk)
                            v.reciprocal(r2, r2).then_inc(mlp_step, 1)
                            dve.wait_ge(mlp_step, 5 * NB * layer + 1 + 5 * blk)
                    bank = 4 * ((cols0 + c) % 2)
                    dve.wait_ge(right_read, cols0 + c + 1 + 8 * blk)
                    v.tensor_tensor(s_buf, psum[:, bank:bank + 4, 0:T], s_buf, ALU.add).then_inc(cols_read, 1)
                    dve.wait_ge(cols_read, cols0 + c + 1 + 8 * blk)
                    if c < 4:
                        v.scalar_tensor_tensor(out=y_buf, in0=s_buf, scalar=0.0, in1=s_buf, op0=ALU.max,
                                               op1=ALU.mult).then_inc(y_done, 1)
                        dve.wait_ge(y_hi, y0 + c + 1 + 4 * blk)
                        v.tensor_tensor(a[:, 4 * c:4 * c + 4, 1, :], y_buf, a[:, 4 * c:4 * c + 4, 0, :].bitcast(F32),
                                        ALU.subtract).then_inc(split_done, 1)
                    else:
                        xc = xT[:, 4 * c - 16:4 * c - 12]
                        v.tensor_tensor(y_buf, s_buf, r2.unsqueeze(1).broadcast_to([P, 4, T]), ALU.mult)\
                         .then_inc(mlp_step, 1)
                        dve.wait_ge(mlp_step, 5 * NB * layer + c - 2 + 5 * blk)
                        last = v.tensor_tensor(xc, xc, y_buf, ALU.add)
                        if final and not last_layer:
                            last.then_inc(x_done, 1)
                            dve.wait_ge(x_done, 4 + c - 4 + 1)
                            ys[0] = y0 + 4 * NB + c - 4
                            next_norm(c - 4, 4 + c - 4, 16)
                        elif final:
                            last.then_inc(x_final, 1)

            def mlp(base, cols0, layer):
                y0 = ys[0]
                with dve.Fori(0, NB - 1) as blk:
                    mlp_block(base, cols0, blk, False, layer, y0)
                mlp_block(base, cols0, NB - 1, True, layer, y0)

            mixer(MIX0, P_MIX0, ROWS0, COLS_WO0, 0, 32)
            mlp(P_MLP0, COLS_MLP0, 0)
            mixer(MIX1, P_MIX1, ROWS1, COLS_WO1, 8, 48)
            mlp(P_MLP1, COLS_MLP1, 1)
            for c in range(4):
                dve.wait_ge(out_turned, 2 * c + 2)
                v.tensor_copy(raw[:, c, N:2 * N], psum[:, 2 * c + 1]).then_inc(out_read_v, 1)

        @block.tensor
        def _(pe):
            mm = nc.tensor.matmul

            def piece_rows(n, kt0, total_kts, no, src):
                kts, width = shape_of(n)
                hi = half_piece(n, 0).rearrange("p (k n) -> p k n", k=kts)
                lo = half_piece(n, 1).rearrange("p (k n) -> p k n", k=kts)
                for i in range(kts):
                    k = kt0 + i
                    for tt in range(TT):
                        bank = psum[:, 2 * (no % 2) + tt, 0:width]
                        x_hi = src(k, 0)[:, tt * P:(tt + 1) * P]
                        x_lo = src(k, 1)[:, tt * P:(tt + 1) * P]
                        mm(bank, x_hi, hi[:, i], start=(k == 0), stop=False)
                        mm(bank, x_hi, lo[:, i], start=False, stop=False)
                        last = mm(bank, x_lo, hi[:, i], start=False, stop=(k == total_kts - 1))
                return last

            def piece_cols(n, j, set_, src):
                for i in range(2):
                    k = 2 * j + i
                    for m in range(4):
                        bank = psum[:, 4 * set_ + m]
                        cols = slice(i * N + m * P, i * N + (m + 1) * P)
                        for which in ((0, 1) if k == 0 else (1, 0)):
                            if which == 0:
                                last = mm(bank, half_piece(n, 0)[:, cols], src[:, k].rearrange("p s t -> p (s t)"),
                                          start=(k == 0), stop=(k == KT - 1))
                            else:
                                last = mm(bank[:, T:2 * T], half_piece(n, 1)[:, cols], src[:, k, 0],
                                          start=False, stop=False)
                return last

            pe.wait_ge(consts, 1)
            pe.wait_ge(vecs_loaded, 16 * 12)
            nc.tensor.transpose(psum[:, 1, 0:76], vec_rows, ident[0:76, 0:76]).then_inc(gains_turned, 1)
            pe.wait_ge(gains_ready, 1)
            for tt in range(TT):
                pe.wait_ge(x_loaded[tt], 16)
            for c in range(4):
                for tt in range(TT):
                    for i in range(4):
                        k = 4 * c + i
                        ins = nc.tensor.transpose(psum[:, 2 * c + tt, i * P:(i + 1) * P],
                                                  raw[:, 2 + tt, k * P:(k + 1) * P], ident[:])
                    ins.then_inc(x_turned, 1)

            def turn(t):
                if t < 16:
                    g, what, half = t // 4, (t % 4) // 2, t % 2
                    if g < 2:
                        pe.wait_ge(rows_read, 3 * g + what + 1)
                    else:
                        pe.wait_ge(normed, 2 * (g - 2) + what + 1)
                    srcs = [nat[:, what, tt, (2 * half + e) * HD:(2 * half + e + 1) * HD] for e in range(2) for tt in range(TT)]
                else:
                    g, what = (t - 16) // 3, (t - 16) % 3
                    pe.wait_ge(normed, 6 + g + 1)
                    if what == 2:
                        pe.wait_ge(q_roped, g + 1)
                        srcs = [w[:, tt].rearrange("p h n -> p (h n)") for w in (q_rot[:, 0], k_rot) for tt in range(TT)]
                    else:
                        w = (k_tok, q_tok)[what]
                        srcs = [w[:, tt, e, 0:NOPE] for e in range(2) for tt in range(TT)]
                if t:
                    pe.wait_ge(turn_read, t)
                for i, s in enumerate(srcs):
                    ins = nc.tensor.transpose(TURN[:, i * P:(i + 1) * P], s, ident[:])
                ins.then_inc(turned, 1)

            def turn_c(n):
                pe.wait_ge(normed, 5 + n // 2)
                if n >= 2:
                    pe.wait_ge(c_ready, n - 1)
                w = nat[:, n // 2]
                for i in range(2):
                    for tt in range(TT):
                        k = 2 * (n % 2) + i
                        ins = nc.tensor.transpose(psum[:, 7 - n % 2, i * T + tt * P:i * T + (tt + 1) * P],
                                                  w[:, tt, k * P:(k + 1) * P], ident[:])
                ins.then_inc(c_turned, 1)

            def scores(n):
                if n:
                    pe.wait_ge(scores_read, n)
                if n < 16:
                    g, e = n // 4, n % 4
                    pe.wait_ge(turn_read, 4 * g + 4)
                    q, k = qT[:, g % 2, e], kT[:, g % 2, e]
                else:
                    g, e = (n - 16) // 2, n % 2
                    pe.wait_ge(turn_read, 16 + 3 * g + 3)
                    q, k = qT1[:, g % 2, e], kT1[:, g % 2, e]
                    qr, kr = rT1[64 * e:64 * e + 64, g % 2, 0], rT1[64 * e:64 * e + 64, g % 2, 1]
                if n < NHG:
                    mm(SCORES[:, 0:2 * P], k[:, 0:P], q, start=True, stop=True)
                    mm(SCORES[:, 2 * P:3 * P], k[:, P:T], q[:, P:T], start=True, stop=True).then_inc(scores_done, 1)
                    return
                first, second = SCORES[:, 0:P], SCORES[:, P:3 * P]
                if n < 16:
                    pe.wait_ge(decay_ready, n - NHG + 1)
                    d = decay[:, n % 2]
                    gt = ones_gt[:, P:2 * P]
                    mm(first, q[:, 0:P], k[:, 0:P], start=True, stop=False)
                    mm(first, d[:, 0], gt, start=False, stop=True)
                    mm(second, q[:, P:T], k, start=True, stop=False)
                    mm(second[:, 0:P], log_f[:, 0, n - NHG:n - NHG + 1].broadcast_to([P, P]), gt, start=False, stop=False)
                    mm(second, d[:, 1], ones_gt[:], start=False, stop=True).then_inc(scores_done, 1)
                else:
                    mm(first, q[:, 0:P], k[:, 0:P], start=True, stop=False)
                    mm(first, qr[:, 0:P], kr[:, 0:P], start=False, stop=True)
                    mm(second, q[:, P:T], k, start=True, stop=False)
                    mm(second, qr[:, P:T], kr, start=False, stop=True).then_inc(scores_done, 1)

            def probs(n):
                b = n % 2
                pe.wait_ge(probs_ready, n + 1)
                if n:
                    pe.wait_ge(probs_t, n)
                if n < NHG:
                    mm(PROBS[:, 0:3 * P], tri_ge[:], sp(b), start=True, stop=False)
                    mm(PROBS[:, P:2 * P], ones[:], sp(b)[:, 2 * P:3 * P], start=False, stop=True)\
                        .then_inc(probs_turned, 1)
                else:
                    for i in range(3):
                        ins = nc.tensor.transpose(PROBS[:, i * P:(i + 1) * P], sp(b)[:, i * P:(i + 1) * P], ident[:])
                    ins.then_inc(probs_turned, 1)

            def head_out(n):
                b = n % 2
                pe.wait_ge(probs_t, n + 1)
                if n:
                    pe.wait_ge(out_ready, n)
                if n < 16:
                    g, e = n // 4, n % 4
                    pe.wait_ge(rows_read, ROWS0[f"v{g}"] + 1)
                    vs = [v_tok[:, g % 2, tt, e * HD:(e + 1) * HD] for tt in range(TT)]
                else:
                    g, e = (n - 16) // 2, n % 2
                    vs = [kv_tok[:, g % 3, tt, e, 1] for tt in range(TT)]
                mm(OUT[:, 0:T], vs[0], w_t(b)[:, 0:2 * P], start=True, stop=False)
                mm(OUT[:, P:T], vs[1], w_t(b)[:, 2 * P:3 * P], start=False, stop=True).then_inc(out_done, 1)

            def norm_rows():
                pe.wait_ge(acc_ready, 2)
                pe.wait_ge(cols_read, COLS_WO1)
                for tt in range(TT):
                    ins = mm(OUT[:, tt:tt + 1], nacc[:, tt * P:(tt + 1) * P], ones[:, 0:1], start=True, stop=True)
                ins.then_inc(norm_sum, 1)

            def mixer(chunks, start, rows_no, cols0, splits0, heads0):
                n = start
                for name, kind, loads in chunks:
                    count = 2 * len(loads)
                    latent = name[:2] in ("uk", "uq")
                    total = 4 if latent else KT
                    if kind == "rows":
                        no = rows_no[name]
                        if no >= 2:
                            pe.wait_ge(rows_read, no - 1)
                        if name == "ckv":
                            pe.wait_ge(cols_read, cols0 - 1)
                    else:
                        c = int(name[1])
                        if c == 0:
                            pe.wait_ge(rows_read, len(ROWS0) if heads0 == 0 else len(ROWS0) + len(ROWS1))
                        elif c >= 2:
                            pe.wait_ge(cols_read, cols0 + c - 1)
                    for j in range(count):
                        kts, _ = shape_of(n)
                        pe.wait_ge(lo_done, n + 1)
                        if kind == "cols":
                            if c == 0:
                                pe.wait_ge(out_ready, heads0 + 2 * j + 2)
                            last = piece_cols(n, j, (cols0 + c) % 2, a)
                        elif latent:
                            src = 0 if name[:3] == "ukv" else 4
                            pe.wait_ge(c_ready, 2 if src == 0 else 4)
                            last = piece_rows(n, j * kts, total, no, lambda k, s, src=src: h[:, src + k, s])
                        else:
                            pe.wait_ge(split_done, splits0 + min(4, (kts * (j + 1) + 3) // 4))
                            last = piece_rows(n, j * kts, total, no, lambda k, s: h[:, k, s])
                        last.then_inc(pieces_used, 1)
                        for what, arg in steps_after(n):
                            if what == "norm_rows":
                                norm_rows()
                            elif what != "rows":
                                {"turn": turn, "turn_c": turn_c, "scores": scores, "probs": probs,
                                 "out": head_out}[what](arg)
                        n += 1

            def mlp(base, cols0, layer, splits0):
                with pe.Fori(0, NB) as blk:
                    for c in range(8):
                        pe.wait_ge(cols_read, cols0 + c - 1 + 8 * blk)
                        if c == 5:
                            pe.wait_ge(norm_read, NB * layer + 1 + blk)
                        for j in range(8):
                            n = base + 8 * c + j
                            pe.wait_ge(lo_done, n + 1 + 64 * blk)
                            if c == 0:
                                pe.wait_ge(split_done, splits0 + j // 2 + 1 + 4 * blk)
                            if c == 4:
                                pe.wait_ge(split_done, splits0 + 4 + j // 2 + 1 + 4 * blk)
                            last = piece_cols(n, j, (cols0 + c) % 2, h if c < 4 else a)
                            last.then_inc(pieces_used, 1)
                            if c == 4 and j == 5:
                                pe.wait_ge(acc_ready, 2 * layer + 1)
                                pe.wait_ge(cols_read, cols0 + c + 8 * blk)
                                mm(psum[:, 4, 0:T], ones[:], nacc, start=True, stop=True).then_inc(norm_sum, 1)

            pe.wait_ge(consts, 2)
            pe.wait_ge(x_read, 4)
            pe.wait_ge(x_read_v, 4)
            mixer(MIX0, P_MIX0, ROWS0, COLS_WO0, 0, 0)
            mlp(P_MLP0, COLS_MLP0, 0, 4)
            mixer(MIX1, P_MIX1, ROWS1, COLS_WO1, 8 + 4 * NB, 16)
            mlp(P_MLP1, COLS_MLP1, 1, 8 + 4 * NB + 4)
            pe.wait_ge(cols_read, COLS_MLP1 + 8 * NB)
            for c in range(4):
                pe.wait_ge(x_final, c + 1)
                for tt in range(TT):
                    for i in range(4):
                        ins = nc.tensor.transpose(psum[:, 2 * c + tt, i * P:(i + 1) * P],
                                                  xT[:, 4 * c + i, tt * P:(tt + 1) * P], ident[:])
                    ins.then_inc(out_turned, 1)


_INS = ["x", "positions", "ln_mix_g", "ln_mlp_g", "sf_w_in", "sf_b_f", "fox_q_g", "fox_k_g", "sf_w_o",
        "mla_w_down", "mla_q_a_g", "mla_kv_a_g", "mla_w_uq", "mla_w_ukv", "mla_q_g", "mla_k_g",
        "mla_w_o", "mlp_w_up", "mlp_w_down"]


def kernel(**inputs):
    import numpy as _np
    import concourse.bacc as _bacc
    from concourse import mybir as _mybir
    from concourse.bass_utils import run_bass_kernel_spmd as _run

    nc = _bacc.Bacc("TRN2", target_bir_lowering=False, num_devices=1)
    arrays, args = {}, []
    for name in _INS:
        arr = _np.ascontiguousarray(inputs[name])
        arrays[f"in_{name}"] = arr
        args.append(nc.dram_tensor(f"in_{name}", arr.shape, _mybir.dt.from_np(arr.dtype), kind="ExternalInput").ap())
    out = nc.dram_tensor("out_x", (1, T, D), F32, kind="ExternalOutput").ap()
    build(nc, *args, out)
    r = _run(nc, [arrays], core_ids=[0])
    return r.results[0]["out_x"]
```

```python
from contextlib import ExitStack
import math

import numpy as np
import concourse.bass as bass
from concourse import mybir

F32 = mybir.dt.float32
F32R = mybir.dt.float32r
I32 = mybir.dt.int32
ALU = mybir.AluOpType
ACT = mybir.ActivationFunctionType
AX_X = mybir.AxisListType.X

P = 128
T = 256
TT = T // P
D = 2048
KT = D // P
HD = 128
NHG = 8
D_FF = 8192
NB = D_FF // D
RANK = 512
NOPE, ROPE = 128, 64
HALF = ROPE // 2
QKD = NOPE + ROPE
EPS = 1e-6
THETA = 10000.0
NEG = -1e30
SB_SCALE = HD ** -0.5
MLA_SCALE = QKD ** -0.5
N = 512
AHEAD = 4
SLOTS = 4

GROUPS = 4


def plan_chunks():
    def full(matrix, col, width=N, k_tiles=KT):
        return [(matrix, 4, 4 * P * l, col, width) for l in range(k_tiles // 4)]
    first = []
    for g in range(GROUPS):
        if g == 2:
            first.append(("f", "narrow", [("w_in", KT, 0, 6 * NHG * HD, NHG)]))
        for j, what in enumerate("qkv"):
            first.append((f"{what}{g}", "rows", full("w_in", (3 * (g // 2) + j) * NHG * HD + (g % 2) * N)))
    for c in range(4):
        first.append((f"o{c}", "cols", full("w_o", c * N)))
    second = [("ckv", "rows", full("w_down", RANK)),
              ("cq", "rows", full("w_down", 0)),
              ("kpe", "narrow", [("w_down", KT, 0, 2 * RANK, ROPE)])]
    for g in range(8):
        second.append((f"ukv{g}", "rows", full("w_ukv", g * N, N, 4)))
        second.append((f"uq{g}", "rows", full("w_uq", g * 2 * QKD, 2 * QKD, 4)))
    for c in range(4):
        second.append((f"o{c}", "cols", full("mla_w_o", c * N)))
    return first, second


MIX0, MIX1 = plan_chunks()
MLP_PIECES = NB * 64
P_MIX0 = 0
P_MLP0 = 2 * sum(len(c[2]) for c in MIX0)
P_MIX1 = P_MLP0 + MLP_PIECES
P_MLP1 = P_MIX1 + 2 * sum(len(c[2]) for c in MIX1)
P_END = P_MLP1 + MLP_PIECES


def pieces_of(chunks, start):
    out, n = {}, start
    for _, _, loads in chunks:
        for _, kts, _, _, width in loads:
            out[n] = out[n + 1] = (kts // 2, width)
            n += 2
    return out


SHAPES = {**pieces_of(MIX0, P_MIX0), **pieces_of(MIX1, P_MIX1)}


def shape_of(n):
    return SHAPES.get(n, (2, N))


def chunk_starts(chunks, start):
    out, n = {}, start
    for name, _, loads in chunks:
        out[name] = n
        n += 2 * len(loads)
    return out


AT0, AT1 = chunk_starts(MIX0, P_MIX0), chunk_starts(MIX1, P_MIX1)

ROWS0 = {c[0]: n for n, c in enumerate(x for x in MIX0 if x[1] != "cols")}
ROWS1 = {c[0]: n + len(ROWS0) for n, c in enumerate(x for x in MIX1 if x[1] != "cols")}
COLS_WO0, COLS_MLP0, COLS_WO1, COLS_MLP1 = 0, 4, 4 + 8 * NB, 8 + 8 * NB


def plan_steps():
    plan = {}

    def at(n, *steps):
        plan.setdefault(n, []).extend(steps)
    base = [AT0[f"q{g}"] for g in range(GROUPS)]
    for g in range(GROUPS):
        for e in range(4 if g else 0):
            h = 4 * (g - 1) + e
            at(base[g] + 1 + 6 * e, ("scores", h))
            at(base[g] + 3 + 6 * e, ("probs", h))
            at(base[g] + 5 + 6 * e, ("out", h))
        at(base[g] + 12, ("turn", 4 * g))
        at(base[g] + 14, ("turn", 4 * g + 1))
        at(base[g] + 20, ("turn", 4 * g + 2))
        at(base[g] + 22, ("turn", 4 * g + 3))
    for e in range(6):
        if e >= 2:
            at(AT0["o0"] + e, ("out", 12 + e - 2))
        if 1 <= e < 5:
            at(AT0["o0"] + e, ("probs", 12 + e - 1))
        if e < 4:
            at(AT0["o0"] + e, ("scores", 12 + e))
    at(1, ("first_h", 3))
    at(3, ("first_r", 0))
    at(AT1["ckv"] + 2, ("norm_rows", 0))
    at(AT1["cq"] + 3, ("turn_c", 0))
    at(AT1["cq"] + 5, ("turn_c", 1))
    at(AT1["ukv0"] + 1, ("turn_c", 2), ("turn_c", 3))
    for g in range(8):
        b = [AT1[f"ukv{g + i}"] if g + i < 8 else AT1["o0"] + 4 * (g + i - 8) for i in range(4)]
        k, q, ropes = (16 + 3 * g + i for i in range(3))
        h = 16 + 2 * g
        if g < 7:
            at(b[1] + 1, ("turn", k))
            at(b[1] + 2, ("turn", q))
            at(b[1] + 3, ("turn", ropes))
        else:
            at(b[1] + 1, ("turn", k), ("turn", q))
            at(b[1] + 2, ("turn", ropes))
        if g < 6:
            at(b[2] + 1, ("scores", h))
            at(b[2] + 2, ("scores", h + 1))
            at(b[2] + 3, ("probs", h))
            at(b[3], ("out", h), ("probs", h + 1))
            at(b[3] + 1, ("out", h + 1))
    o = AT1["o0"]
    at(o, ("scores", 28))
    at(o + 1, ("scores", 29))
    at(o + 2, ("probs", 28))
    at(o + 3, ("out", 28), ("probs", 29), ("scores", 30))
    at(o + 4, ("out", 29), ("probs", 30), ("scores", 31))
    at(o + 5, ("out", 30), ("probs", 31))
    at(o + 6, ("out", 31))
    for at_, chunks in ((AT0, MIX0), (AT1, MIX1)):
        for name, kind, loads in chunks:
            if kind == "rows":
                at(at_[name] + 2 * len(loads) - 1, ("rows", name))
            elif kind == "narrow":
                at(at_[name] + 1, ("narrow", name))
                at(at_[name] + 2, ("rows", name))
    return plan


STEPS = plan_steps()


def steps_after(n):
    return STEPS.get(n, [])


def build(nc, x, positions, ln_mix_g, ln_mlp_g, sf_w_in, sf_b_f, fox_q_g, fox_k_g, sf_w_o,
          mla_w_down, mla_q_a_g, mla_kv_a_g, mla_w_uq, mla_w_ukv, mla_q_g, mla_k_g, mla_w_o,
          mlp_w_up, mlp_w_down, out):
    matrices = {"w_in": sf_w_in[0], "w_o": sf_w_o[0], "w_down": mla_w_down[0], "w_ukv": mla_w_ukv[0],
                "w_uq": mla_w_uq[0], "mla_w_o": mla_w_o[0]}
    with ExitStack() as ctx:
        def sb(name, shape, dt=F32):
            return ctx.enter_context(nc.sbuf_tensor(name, shape, dt))

        def sem(name):
            return ctx.enter_context(nc.semaphore(name))

        xT = sb("xT", [P, KT, T])
        h = sb("h", [P, KT, 2, T], F32R)
        a = sb("a", [P, KT, 2, T], F32R)
        raw = sb("raw", [P, SLOTS, 4 * N])
        halves = sb("halves", [P, SLOTS, 2, 2 * N], F32R)
        nat = sb("nat", [P, 2, TT, N])
        mix = sb("mix", [P, 8192])
        heads = sb("heads", [P, 7, 3 * P])
        side = sb("side", [P, 4, P])
        ident = sb("ident", [P, P])
        ones = sb("ones", [P, P])
        tri_ge = sb("tri_ge", [P, P])
        tri_le = sb("tri_le", [P, P])
        ones_gt = sb("ones_gt", [P, 2 * P])
        sb_mask = sb("sb_mask", [P, 3 * P])
        sm_mask = sb("sm_mask", [P, 3 * P])
        gains = sb("gains", [P, 76])
        q_gain = sb("q_gain", [P, 2])
        rope_g = sb("rope_g", [P, 2, ROPE])
        b_f = sb("b_f", [P, NHG])
        fl = sb("fl", [P, 3, TT, NHG])
        log_f = sb("log_f", [P, TT, NHG])
        pos_i = sb("pos_i", [P, TT], I32)
        pos_f = sb("pos_f", [P, TT])
        inv_freq = sb("inv_freq", [P, HALF])
        rope_c = sb("rope_c", [P, 2, TT, ROPE])
        rope_s = sb("rope_s", [P, 2, TT, ROPE])
        kpe_ss = sb("kpe_ss", [P, TT])
        st = sb("st", [P, 4, 8])
        ss_x = sb("ss_x", [P, TT])
        r_tok = sb("r_tok", [P, TT])
        mx = sb("mx", [P, 2, 2])
        nmx = sb("nmx", [P, 2, 2])
        row_sum = sb("row_sum", [P, 2, 2])
        row_inv = sb("row_inv", [P, 2, 2])

        qT = mix[:, 0:2048].rearrange("p (b h t) -> p b h t", b=2, h=4)
        kT = mix[:, 2048:4096].rearrange("p (b h t) -> p b h t", b=2, h=4)
        v_tok = mix[:, 4096:6144].rearrange("p (b s n) -> p b s n", b=2, s=TT)
        qT1 = mix[:, 0:1024].rearrange("p (b h t) -> p b h t", b=2, h=2)
        kT1 = mix[:, 1024:2048].rearrange("p (b h t) -> p b h t", b=2, h=2)
        rT1 = mix[:, 2048:3072].rearrange("p (b w t) -> p b w t", b=2, w=2)
        kv_tok = mix[:, 3072:6144].rearrange("p (b s h w n) -> p b s h w n", b=3, s=TT, h=2, w=2)
        q_tok = mix[:, 6144:6912].rearrange("p (s h n) -> p s h n", s=TT, h=2)
        k_tok = mix[:, 6912:7424].rearrange("p (s h n) -> p s h n", s=TT, h=2)
        q_rot = mix[:, 7424:7936].rearrange("p (w s h n) -> p w s h n", w=2, s=TT, h=2)
        k_rot = mix[:, 7936:8192].rearrange("p (s h n) -> p s h n", s=TT, h=2)
        narrow_t = nat[:, 0, 0]
        sq_tok = nat[:, 0].rearrange("p s n -> p (s n)")[:, 0:4 * QKD].rearrange("p (m n) -> p m n", m=4)
        vec_rows = nat[0:76, 0, 0, 0:P]
        decay = side[:].rearrange("p (b s) t -> p b s t", b=2)
        kpe = side[:, 0].rearrange("p (s n) -> p s n", s=TT)
        kpe_r = side[:, 1].rearrange("p (s n) -> p s n", s=TT)
        kpe_t = side[:, 2].rearrange("p (s n) -> p s n", s=TT)
        r2 = heads[:, 0, 0:T]
        nacc = heads[:, 1, 0:T]
        ang = heads[:, 2, 0:2 * TT * HALF].rearrange("p (w s n) -> p w s n", w=2, s=TT)
        trig_n = heads[:, 3, 0:TT * HALF].rearrange("p (s n) -> p s n", s=TT)
        trig = heads[:, 4, 0:2 * TT * HALF].rearrange("p (w s n) -> p w s n", w=2, s=TT)
        sq_sum = mix[:, 0:1024].rearrange("p (k t) -> p k t", k=4)
        sq_new = mix[:, 2048:3072].rearrange("p (k t) -> p k t", k=4)
        s_buf = nat[:, 0].rearrange("p s (k t) -> p (s k) t", t=T)
        y_buf = nat[:, 1].rearrange("p s (k t) -> p (s k) t", t=T)
        zm, e0, sp, w_t = (lambda b: heads[:, b], heads[:, 2], lambda b: heads[:, 3 + b], lambda b: heads[:, 5 + b])

        def latent_tile(k):
            return a[:, 12 + k] if k < 4 else h[:, k]

        psum = ctx.enter_context(nc.psum_tensor("psum", [P, 8, N], F32))
        SCORES, PROBS, OUT, TURN = psum[:, 4], psum[:, 5], psum[:, 6], psum[:, 7]

        raw_loaded = [sem(f"raw_loaded{i}") for i in range(SLOTS)]
        x_loaded = [sem(f"x_loaded{i}") for i in range(TT)]
        pos_loaded, gains_loaded, vecs_loaded = sem("pos_loaded"), sem("gains_loaded"), sem("vecs_loaded")
        hi_done, lo_done = sem("hi_done"), sem("lo_done")
        pieces_used = sem("pieces_used")
        r_ready = sem("r_ready")
        rows_read, cols_read = sem("rows_read"), sem("cols_read")
        right_read = sem("right_read")
        consts = sem("consts")
        const_step = sem("const_step")
        x_turned, x_read = sem("x_turned"), sem("x_read")
        x_read_v = sem("x_read_v")
        gains_turned, gains_ready = sem("gains_turned"), sem("gains_ready")
        y_done, y_hi = sem("y_done"), sem("y_hi")
        split_done = sem("split_done")
        x_done = sem("x_done")
        sq_done, sq_added = sem("sq_done"), sem("sq_added")
        acc_ready = sem("acc_ready")
        norm_sum, norm_read = sem("norm_sum"), sem("norm_read")
        mlp_step = sem("mlp_step")
        rows_stat, rows_ln = sem("rows_stat"), sem("rows_ln")
        squared = sem("squared")
        narrow_out, narrow_done = sem("narrow_out"), sem("narrow_done")
        normed = sem("normed")
        trig_args, trig_done, rope_ready = sem("trig_args"), sem("trig_done"), sem("rope_ready")
        logf_in, logf_abs, logf_ln, logf_ready = sem("logf_in"), sem("logf_abs"), sem("logf_ln"), sem("logf_ready")
        turned, turn_read = sem("turned"), sem("turn_read")
        c_turned, c_hi, c_ready = sem("c_turned"), sem("c_hi"), sem("c_ready")
        q_scaled, q_roped = sem("q_scaled"), sem("q_roped")
        pool_step = sem("pool_step")
        scores_done, scores_read = sem("scores_done"), sem("scores_read")
        decay_ready = sem("decay_ready")
        max_ready = sem("max_ready")
        exp_done = sem("exp_done")
        probs_ready = sem("probs_ready")
        probs_turned, probs_read, probs_t = sem("probs_turned"), sem("probs_read"), sem("probs_t")
        out_done, out_hi, out_ready = sem("out_done"), sem("out_hi"), sem("out_ready")
        act_step, dve_step = sem("act_step"), sem("dve_step")
        x_final, out_turned, out_stored = sem("x_final"), sem("out_turned"), sem("out_stored")
        out_read, out_read_v = sem("out_read"), sem("out_read_v")

        block = ctx.enter_context(nc.Block())

        def flat(kts, width):
            return kts * width

        def narrow(n):
            return shape_of(n)[1] in (NHG, ROPE)

        def raw_piece(n):
            kts, width = shape_of(n)
            size = flat(kts, width)
            piece = raw[:, (n // 2) % SLOTS, (n % 2) * size:(n % 2 + 1) * size]
            return piece.rearrange("p (k n) -> p k n", k=kts) if narrow(n) else piece

        def narrow_piece(n):
            kts, width = shape_of(n)
            return halves[:, n % SLOTS].rearrange("p w n -> p (w n)")[:, 0:2 * kts * width]\
                .rearrange("p (k w n) -> p k w n", k=kts, w=2)

        def half_piece(n, which):
            kts, width = shape_of(n)
            if narrow(n):
                return narrow_piece(n)[:, :, which]
            return halves[:, n % SLOTS, which, 0:flat(kts, width)]

        gain_rows = [(ln_mix_g.rearrange("l (k p) -> (l k) p", p=P), 0, 32),
                     (ln_mlp_g.rearrange("l (k p) -> (l k) p", p=P), 32, 32),
                     (mla_q_a_g.rearrange("a (k p) -> (a k) p", p=P), 66, 4),
                     (mla_kv_a_g.rearrange("a (k p) -> (a k) p", p=P), 70, 4),
                     (fox_q_g, 64, 1), (fox_k_g, 65, 1), (mla_q_g[:, 0:NOPE], 74, 1), (mla_k_g[:, 0:NOPE], 75, 1)]

        @block.sync
        def _(sp_):
            def free_slot(load, extra=0):
                if load >= SLOTS:
                    sp_.wait_ge(lo_done, 2 * load - 2 * SLOTS + 2 + 2 * extra)
                    if not isinstance(extra, int):
                        sp_.nop()

            def straight(chunks, load):
                for _, _, loads in chunks:
                    for matrix, kts, row, col, width in loads:
                        if load in (2, 3):
                            sp_.wait_ge(x_turned, 4 * load - 4)
                            sp_.wait_ge(act_step, load - 1)
                            if load == 2:
                                for dst, src in ((rope_g[:, 0, :], mla_q_g[0, NOPE:QKD]),
                                                 (rope_g[:, 1, :], mla_k_g[0, NOPE:QKD]), (b_f[:], sf_b_f[0])):
                                    sp_.dma_start(dst, src.partition_broadcast(P)).then_inc(vecs_loaded, 16)
                        free_slot(load)
                        dst = raw[:, load % SLOTS, 0:kts * width].rearrange("p (k n) -> p k n", k=kts)
                        src = matrices[matrix][row:row + kts * P, col:col + width].rearrange("(k p) n -> p k n", p=P)
                        sp_.dma_start(dst, src).then_inc(raw_loaded[load % SLOTS], 16)
                        load += 1

            def mlp(layer, load0):
                w_up, w_down = mlp_w_up[layer], mlp_w_down[layer]
                with sp_.Fori(0, NB) as b:
                    for c in range(8):
                        for l in range(4):
                            load = load0 + 4 * c + l
                            free_slot(load, 32 * b)
                            dst = raw[:, load % SLOTS].rearrange("p (k n) -> p k n", k=4)
                            if c < 4:
                                src = w_up[4 * P * l:4 * P * (l + 1), bass.ds(b * D + c * N, N)]
                            else:
                                src = w_down[bass.ds(b * D + 4 * P * l, 4 * P), (c - 4) * N:(c - 3) * N]
                            sp_.dma_start(dst, src.rearrange("(k p) n -> p k n", p=P))\
                               .then_inc(raw_loaded[load % SLOTS], 16)

            for tt in range(TT):
                sp_.dma_start(raw[:, 2 + tt, :], x[0, tt * P:(tt + 1) * P, :]).then_inc(x_loaded[tt], 16)
            for src, row, count in gain_rows[0:4]:
                sp_.dma_start(vec_rows[row:row + count], src).then_inc(gains_loaded, 16)
            straight(MIX0, 0)
            mlp(0, P_MLP0 // 2)
            straight(MIX1, P_MIX1 // 2)
            mlp(1, P_MLP1 // 2)
            for c in range(4):
                sp_.wait_ge(out_read, c + 1)
                sp_.wait_ge(out_read_v, c + 1)
                sp_.dma_start(out[0, :, c * N:(c + 1) * N].rearrange("(s p) n -> p s n", p=P),
                              raw[:, c, 0:2 * N].rearrange("p (s n) -> p s n", s=TT)).then_inc(out_stored, 16)
            sp_.wait_ge(out_stored, 64)

        @block.gpsimd
        def _(pool):
            made = [0]

            def own(ins):
                made[0] += 1
                ins.then_inc(const_step, 1)
                pool.wait_ge(const_step, made[0])

            own(pool.memset(ident[:], 0.0))
            pool.affine_select(out=ident[:], in_=ident[:], compare_op=ALU.not_equal, fill=1.0, base=0,
                               pattern=[[-1, P]], channel_multiplier=1).then_inc(consts, 1)
            own(pool.memset(ones[:], 1.0))
            pool.memset(ones_gt[:, 0:P], 1.0)
            own(pool.memset(sb_mask[:], 0.0))
            own(pool.memset(sm_mask[:], 0.0))
            pool.affine_select(out=tri_ge[:], in_=ones[:], compare_op=ALU.is_ge, fill=0.0, base=0,
                               pattern=[[-1, P]], channel_multiplier=1)
            pool.affine_select(out=tri_le[:], in_=ones[:], compare_op=ALU.is_ge, fill=0.0, base=0,
                               pattern=[[1, P]], channel_multiplier=-1)
            pool.affine_select(out=ones_gt[:, P:2 * P], in_=ones[:], compare_op=ALU.is_gt, fill=0.0, base=0,
                               pattern=[[-1, P]], channel_multiplier=1)
            for c in (0, 2 * P):
                pool.affine_select(out=sb_mask[:, c:c + P], in_=sb_mask[:, c:c + P], compare_op=ALU.is_gt,
                                   fill=NEG, base=0, pattern=[[1, P]], channel_multiplier=-1)
                last = pool.affine_select(out=sm_mask[:, c:c + P], in_=sm_mask[:, c:c + P], compare_op=ALU.is_ge,
                                          fill=NEG, base=0, pattern=[[-1, P]], channel_multiplier=1)
            last.then_inc(consts, 1)

            pool.wait_ge(logf_ready, 1)
            for n in range(NHG):
                if n >= 2:
                    pool.wait_ge(scores_done, NHG + n - 1)
                for tt in range(TT):
                    ins = pool.tensor_scalar(decay[:, n % 2, tt], tri_le[:], log_f[:, tt, n:n + 1], None, ALU.mult)
                ins.then_inc(decay_ready, 1)

            pool.wait_ge(rope_ready, 1)
            step = [0]

            def mine(ins):
                step[0] += 1
                ins.then_inc(pool_step, 1)
                pool.wait_ge(pool_step, step[0])
            for g in range(8):
                pool.wait_ge(q_scaled, g + 1)
                for tt in range(TT):
                    q = q_tok[:, tt, :, NOPE:QKD]
                    cs = rope_c[:, 0, tt].unsqueeze(1).broadcast_to([P, 2, ROPE])
                    s1 = rope_s[:, 0, tt, 0:HALF].unsqueeze(1).broadcast_to([P, 2, HALF])
                    s2 = rope_s[:, 0, tt, HALF:ROPE].unsqueeze(1).broadcast_to([P, 2, HALF])
                    pool.tensor_tensor(q_rot[:, 0, tt], q, cs, ALU.mult)
                    pool.tensor_tensor(q_rot[:, 1, tt, :, 0:HALF], q[:, :, HALF:ROPE], s1, ALU.mult)
                    ins = pool.tensor_tensor(q_rot[:, 1, tt, :, HALF:ROPE], q[:, :, 0:HALF], s2, ALU.mult)
                mine(ins)
                pool.tensor_tensor(q_rot[:, 0], q_rot[:, 0], q_rot[:, 1], ALU.add).then_inc(q_roped, 1)
                pool.wait_ge(q_roped, g + 1)

        @block.scalar
        def _(act):
            own_steps = [0]

            def own(ins):
                own_steps[0] += 1
                ins.then_inc(act_step, 1)
                act.wait_ge(act_step, own_steps[0])

            def split_hi(n, extra=0):
                if n % 2 == 0:
                    act.wait_ge(raw_loaded[(n // 2) % SLOTS], 16 * (n // 2 // SLOTS + 1) + 16 // (2 * SLOTS) * extra)
                if n >= SLOTS:
                    act.wait_ge(pieces_used, n - SLOTS + 1 + extra)
                nc.scalar.copy(half_piece(n, 0), raw_piece(n)).then_inc(hi_done, 1)

            powers = [0]

            def power(m):
                powers[0] += 1
                act.wait_ge(rows_stat, powers[0])
                own(nc.scalar.activation(st[:, 3, 0:m], st[:, 1, 0:m], ACT.Ln))
                nc.scalar.activation(st[:, 2, 0:m], st[:, 3, 0:m], ACT.Exp, scale=-0.5).then_inc(rows_ln, 1)

            ys = [0]

            def round_y(dst):
                ys[0] += 1
                act.wait_ge(y_done, ys[0])
                nc.scalar.copy(dst, y_buf).then_inc(y_hi, 1)

            act.dma_start(pos_i[:], positions[0].rearrange("(s p) -> p s", p=P),
                          allow_slow_non_contiguous=True).then_inc(pos_loaded, 16)
            for src, row, count in gain_rows[4:]:
                act.dma_start(vec_rows[row:row + count], src).then_inc(gains_loaded, 16)
            act.preload_act_table_set("trig_and_small")

            for c in range(4):
                act.wait_ge(x_turned, c + 1)
                nc.scalar.copy(xT[:, 4 * c:4 * c + 4, 0:P], psum[:, 2 * c].rearrange("p (k t) -> p k t", k=4))\
                  .then_inc(x_read, 1)
            def square_x(tt):
                act.wait_ge(x_loaded[tt], 16)
                own(nc.scalar.activation(a[:, 8 * tt:8 * tt + 4].rearrange("p k s t -> p (k s t)"), raw[:, 2 + tt],
                                         ACT.Square, accum_out=ss_x[:, tt:tt + 1]))

            square_x(0)
            act.wait_ge(trig_args, 1)
            nc.scalar.activation(trig, ang, ACT.Sin).then_inc(trig_done, 1)
            act.preload_act_table_set("natural_log_exp_and_others")

            round_y(h[:, 0:4, 0, :])
            for n in (0, 1, 2):
                split_hi(n)
            round_y(h[:, 4:8, 0, :])
            split_hi(3)
            square_x(1)
            round_y(h[:, 8:12, 0, :])

            def evict(dst, src, scale=None):
                if scale is None:
                    return nc.scalar.copy(dst, src)
                return nc.scalar.activation(dst, src, ACT.Copy, scale=scale)

            def square_rows(pairs):
                for src, junk, total, scale in pairs:
                    ins = nc.scalar.activation(junk, src, ACT.Square, accum_out=total,
                                               **({} if scale is None else {"scale": scale}))
                ins.then_inc(squared, 1)

            def narrow_copy(name, last_piece, no):
                act.wait_ge(pieces_used, last_piece + 1)
                width = shape_of(last_piece)[1]
                nc.scalar.copy(narrow_t[0:2 * width], psum[0:2 * width, 2 * (no % 2)]).then_inc(narrow_out, 1)

            def rows(name, last_piece, no):
                if name in ("f", "kpe"):
                    act.wait_ge(narrow_done, 1 + (name == "kpe"))
                    act.wait_ge(r_ready, 1 + (name == "kpe"))
                    for tt in range(TT):
                        dst, width = (fl[:, 0, tt], NHG) if name == "f" else (kpe[:, tt], ROPE)
                        ins = evict(dst, psum[:, 2 * (no % 2) + 1, tt * width:(tt + 1) * width], r_tok[:, tt:tt + 1])
                else:
                    ins = wide_rows(name, last_piece, no)
                ins.then_inc(rows_read, 1)
                if name == "f":
                    act.wait_ge(logf_in, 1)
                    own(nc.scalar.activation(fl[:, 2], fl[:, 1], ACT.Abs))
                    own(nc.scalar.activation(fl[:, 0], fl[:, 2], ACT.Exp, scale=-1.0))
                    nc.scalar.activation(fl[:, 2], fl[:, 0], ACT.Ln, bias=1.0).then_inc(logf_ln, 1)
                if name in ("q2", "k2", "q3", "k3"):
                    power(8)
                elif name in ("ckv", "cq"):
                    power(TT)
                elif name[:2] == "uq":
                    power(8)

            def wide_rows(name, last_piece, no):
                act.wait_ge(pieces_used, last_piece + 1)
                act.wait_ge(r_ready, 1 + (no >= len(ROWS0)))
                banks = [psum[:, 2 * (no % 2) + tt] for tt in range(TT)]
                if name in ("ckv", "cq"):
                    square_rows([(banks[tt], mix[:, 7168 + tt * N:7168 + (tt + 1) * N], st[:, 0, tt:tt + 1],
                                  r_tok[:, tt:tt + 1]) for tt in range(TT)])
                elif name[:3] == "ukv":
                    square_rows([(banks[tt][:, 2 * e * HD:2 * e * HD + NOPE], nat[:, 1, tt, e * NOPE:(e + 1) * NOPE],
                                  st[:, 0, 4 + 2 * tt + e:5 + 2 * tt + e], None) for tt in range(TT) for e in range(2)])
                elif name[:2] == "uq":
                    square_rows([(banks[tt][:, e * QKD:(e + 1) * QKD], sq_tok[:, 2 * tt + e],
                                  st[:, 0, 2 * tt + e:1 + 2 * tt + e], None) for tt in range(TT) for e in range(2)])
                for tt in range(TT):
                    r = r_tok[:, tt:tt + 1]
                    if name[0] in "qk":
                        ins = evict(nat[:, "qk".index(name[0]), tt], banks[tt], r)
                    elif name[0] == "v":
                        ins = evict(v_tok[:, int(name[1]) % 2, tt], banks[tt], r)
                    elif name == "ckv":
                        ins = evict(nat[:, 0, tt], banks[tt], r)
                    elif name == "cq":
                        ins = evict(nat[:, 1, tt], banks[tt], r)
                    elif name[:3] == "ukv":
                        ins = evict(kv_tok[:, int(name[3]) % 3, tt].rearrange("p h w n -> p (h w n)"), banks[tt])
                    else:
                        ins = evict(q_tok[:, tt].rearrange("p h n -> p (h n)"), banks[tt][:, 0:2 * QKD])
                return ins

            def turn(t):
                act.wait_ge(turned, t + 1)
                if t < 16:
                    g, what, half = t // 4, (t % 4) // 2, t % 2
                    dst = (qT, kT)[what][:, g % 2, 2 * half:2 * half + 2]
                    scale = ((SB_SCALE, None), (q_gain[:, 0:1], gains[:, 65:66]))[g // 2][what]
                    ins = evict(dst, TURN.rearrange("p (h t) -> p h t", h=2), scale)
                else:
                    g, what = (t - 16) // 3, (t - 16) % 3
                    dst = (kT1, qT1, rT1)[what][:, g % 2]
                    scale = (gains[:, 75:76], q_gain[:, 1:2], None)[what]
                    ins = evict(dst, TURN.rearrange("p (h t) -> p h t", h=2), scale)
                ins.then_inc(turn_read, 1)

            def turn_c(n):
                act.wait_ge(c_turned, n + 1)
                for i in range(2):
                    k = 2 * n + i
                    col = (70 if n < 2 else 66) + k % 4
                    ins = nc.scalar.activation(latent_tile(k)[:, 0], psum[:, 7 - n % 2, i * T:(i + 1) * T], ACT.Copy,
                                               scale=gains[:, col:col + 1])
                ins.then_inc(c_hi, 1)

            def scores(n):
                b = n % 2
                if n < NHG:
                    act.wait_ge(scores_read, n + 1)
                    own(nc.scalar.activation(e0, zm(b), ACT.Abs))
                    own(nc.scalar.activation(w_t(b), e0, ACT.Exp, scale=-1.0))
                    nc.scalar.activation(e0, w_t(b), ACT.Ln, bias=1.0).then_inc(exp_done, 1)
                else:
                    act.wait_ge(max_ready, n - NHG + 1)
                    nc.scalar.activation(sp(b)[:, 0:P], zm(b)[:, 0:P], ACT.Exp, bias=nmx[:, b, 0:1],
                                         accum_out=row_sum[:, b, 0:1])
                    nc.scalar.activation(sp(b)[:, P:3 * P], zm(b)[:, P:3 * P], ACT.Exp, bias=nmx[:, b, 1:2],
                                         accum_out=row_sum[:, b, 1:2]).then_inc(exp_done, 1)

            def probs(n):
                b = n % 2
                if n < NHG:
                    act.wait_ge(probs_read, n + 1)
                    nc.scalar.activation(w_t(b), zm(b), ACT.Exp).then_inc(probs_t, 1)
                else:
                    act.wait_ge(probs_turned, n + 1)
                    nc.scalar.copy(w_t(b), PROBS[:, 0:3 * P]).then_inc(probs_t, 1)

            def head_out(n):
                act.wait_ge(out_done, n + 1)
                nc.scalar.copy(a[:, n % KT, 0], OUT[:, 0:T]).then_inc(out_hi, 1)

            def right_half(cols, end):
                act.wait_ge(pieces_used, end)
                nc.scalar.copy(s_buf, psum[:, 4 * (cols % 2):4 * (cols % 2) + 4, T:2 * T]).then_inc(right_read, 1)

            def next_norm(c, xs):
                norm = xs // 4
                round_y(h[:, 4 * c:4 * c + 4, 0, :])
                act.wait_ge(x_done, xs + 1)
                if c == 0 and norm:
                    act.wait_ge(acc_ready, norm)
                if c and 3 * norm + c - 1:
                    act.wait_ge(sq_added, 3 * norm + c - 1)
                nc.scalar.activation(sq_new if c else sq_sum, xT[:, 4 * c:4 * c + 4], ACT.Square).then_inc(sq_done, 1)

            def mixer(chunks, start, rows_no, cols0, xs0):
                n = start
                for name, kind, loads in chunks:
                    for j in range(2 * len(loads)):
                        ends_cols = kind == "cols" and j == 2 * len(loads) - 1
                        if not ends_cols:
                            split_hi(n + AHEAD)
                        for what, arg in steps_after(n):
                            if what == "rows":
                                rows(arg, n, rows_no[arg])
                            elif what == "narrow":
                                narrow_copy(arg, n, rows_no[arg])
                            elif what == "first_h":
                                round_y(h[:, 4 * arg:4 * arg + 4, 0, :])
                            elif what == "first_r":
                                power(TT)
                            elif what == "norm_rows":
                                power(TT)
                            else:
                                {"turn": turn, "turn_c": turn_c, "scores": scores, "probs": probs,
                                 "out": head_out}[what](arg)
                        n += 1
                    if kind == "cols":
                        c = int(name[1])
                        right_half(cols0 + c, n)
                        split_hi(n - 1 + AHEAD)
                        next_norm(c, xs0 + c)

            def mlp_block(base, cols0, blk, final, last_layer, y0):
                for c in range(8):
                    for j in range(7):
                        n = base + 8 * c + j + AHEAD
                        if not (last_layer and final and c == 7 and j >= 8 - AHEAD):
                            split_hi(n, 64 * blk)
                    right_half(cols0 + c, base + 8 * c + 8 + 64 * blk)
                    if not (last_layer and final and c == 7):
                        split_hi(base + 8 * c + 7 + AHEAD, 64 * blk)
                    if c < 4:
                        act.wait_ge(y_done, y0 + c + 1 + 4 * blk)
                        nc.scalar.copy(a[:, 4 * c:4 * c + 4, 0, :], y_buf).then_inc(y_hi, 1)
                    elif final and not last_layer:
                        ys[0] = y0 + 4 * NB + c - 4
                        next_norm(c - 4, 4 + c - 4)

            def mlp(base, cols0, last_layer):
                y0 = ys[0]
                with act.Fori(0, NB - 1) as blk:
                    mlp_block(base, cols0, blk, False, last_layer, y0)
                mlp_block(base, cols0, NB - 1, True, last_layer, y0)

            mixer(MIX0, P_MIX0, ROWS0, COLS_WO0, 0)
            mlp(P_MLP0, COLS_MLP0, False)
            mixer(MIX1, P_MIX1, ROWS1, COLS_WO1, 8)
            mlp(P_MLP1, COLS_MLP1, True)
            for c in range(4):
                act.wait_ge(out_turned, 2 * c + 1)
                nc.scalar.copy(raw[:, c, 0:N], psum[:, 2 * c]).then_inc(out_read, 1)

        @block.vector
        def _(dve):
            own_steps = [0]

            def own(ins):
                own_steps[0] += 1
                ins.then_inc(dve_step, 1)
                dve.wait_ge(dve_step, own_steps[0])

            v = nc.vector

            def split_lo(n, extra=0):
                dve.wait_ge(hi_done, n + 1 + extra)
                v.tensor_tensor(half_piece(n, 1), raw_piece(n), half_piece(n, 0).bitcast(F32), ALU.subtract)\
                 .then_inc(lo_done, 1)

            stats = [0]

            def power(m, inv_count):
                v.tensor_scalar(st[:, 1, 0:m], st[:, 0, 0:m], inv_count, EPS, ALU.mult, ALU.add).then_inc(rows_stat, 1)
                stats[0] += 1
                dve.wait_ge(rows_stat, stats[0])
                dve.wait_ge(rows_ln, stats[0])
                own(v.tensor_tensor(st[:, 3, 0:m], st[:, 2, 0:m], st[:, 2, 0:m], ALU.mult))
                own(v.tensor_tensor(st[:, 3, 0:m], st[:, 3, 0:m], st[:, 1, 0:m], ALU.mult))
                own(v.tensor_scalar(st[:, 3, 0:m], st[:, 3, 0:m], -0.5, 1.5, ALU.mult, ALU.add))

            splits = [0]
            ys = [0]

            def split_y(dst_lo, dst_hi):
                ys[0] += 1
                dve.wait_ge(y_hi, ys[0])
                v.tensor_tensor(dst_lo, y_buf, dst_hi.bitcast(F32), ALU.subtract).then_inc(split_done, 1)

            def times_gain(c, gain_col):
                g = gains[:, gain_col + 4 * c:gain_col + 4 * c + 4].unsqueeze(2).broadcast_to([P, 4, T])
                if ys[0]:
                    dve.wait_ge(split_done, ys[0])
                v.tensor_tensor(y_buf, xT[:, 4 * c:4 * c + 4], g, ALU.mult).then_inc(y_done, 1)
                dve.wait_ge(y_done, ys[0] + 1)

            def split_h(c):
                split_y(h[:, 4 * c:4 * c + 4, 1, :], h[:, 4 * c:4 * c + 4, 0, :])

            for i in range(HALF):
                v.memset(inv_freq[:, i:i + 1], float(np.float32(THETA ** (-i / HALF))))
            dve.wait_ge(pos_loaded, 16)
            own(v.tensor_copy(pos_f[:], pos_i[:]))
            for tt in range(TT):
                ins = v.tensor_scalar(ang[:, 0, tt], inv_freq[:], pos_f[:, tt:tt + 1], None, ALU.mult)
            own(ins)
            magic = 1.5 * 2.0 ** 23
            parts, rest = [], 2 * math.pi
            for bits in (5, 14, 25, 40):
                part = math.floor(rest * 2.0 ** bits) / 2.0 ** bits
                parts.append(part)
                rest -= part
            for stride in (4096.0, 1.0):
                own(v.tensor_scalar(trig_n, ang[:, 0], 1.0 / (2 * math.pi * stride), magic, ALU.mult, ALU.add))
                own(v.tensor_scalar(trig_n, trig_n, -magic, None, ALU.add))
                for part in parts:
                    own(v.scalar_tensor_tensor(out=ang[:, 0], in0=trig_n, scalar=-part * stride, in1=ang[:, 0],
                                               op0=ALU.mult, op1=ALU.add))
            own(v.tensor_scalar(ang[:, 1], ang[:, 0], math.pi / 2, None, ALU.add))
            own(v.tensor_scalar(trig_n, ang[:, 1], math.pi, -2 * math.pi, ALU.is_gt, ALU.mult))
            own(v.tensor_tensor(ang[:, 1], ang[:, 1], trig_n, ALU.add))
            limit = float(np.nextafter(np.float32(math.pi), np.float32(0)))
            v.tensor_scalar(ang, ang, limit, -limit, ALU.min, ALU.max).then_inc(trig_args, 1)

            dve.wait_ge(gains_turned, 1)
            own(v.tensor_copy(gains[:], psum[:, 7, 0:76]))
            v.tensor_scalar(q_gain[:, 0:1], gains[:, 64:65], SB_SCALE, None, ALU.mult)
            v.tensor_scalar(q_gain[:, 1:2], gains[:, 74:75], MLA_SCALE, None, ALU.mult).then_inc(gains_ready, 1)

            def read_x(c):
                dve.wait_ge(x_turned, 4 + c + 1)
                v.tensor_copy(xT[:, 4 * c:4 * c + 4, P:T], psum[:, 2 * c + 1].rearrange("p (k t) -> p k t", k=4))\
                 .then_inc(x_read_v, 1)

            read_x(0)
            for c, before, after in ((0, (), (0, 1)), (1, (2,), ()), (2, (3,), ())):
                dve.wait_ge(x_read, c + 1)
                dve.wait_ge(x_read_v, c + 1)
                times_gain(c, 0)
                read_x(c + 1)
                for n in before:
                    split_lo(n)
                split_h(c)
                for n in after:
                    split_lo(n)
            dve.wait_ge(x_read_v, 4)

            def first_r():
                dve.wait_ge(trig_done, 1)
                dve.wait_ge(vecs_loaded, 16 * 3)
                for i, scale in ((0, MLA_SCALE), (1, 1.0)):
                    g1 = rope_g[:, i, 0:HALF].unsqueeze(1).broadcast_to([P, TT, HALF])
                    g2 = rope_g[:, i, HALF:ROPE].unsqueeze(1).broadcast_to([P, TT, HALF])
                    for dst, j, s, g in ((rope_c[:, i, :, 0:HALF], 1, scale, g1), (rope_c[:, i, :, HALF:ROPE], 1, scale, g2),
                                         (rope_s[:, i, :, 0:HALF], 0, -scale, g2), (rope_s[:, i, :, HALF:ROPE], 0, scale, g1)):
                        ins = v.scalar_tensor_tensor(out=dst, in0=trig[:, j], scalar=s, in1=g, op0=ALU.mult, op1=ALU.mult)
                ins.then_inc(rope_ready, 1)
                dve.wait_ge(rope_ready, 1)

                dve.wait_ge(act_step, 2)
                own(v.tensor_copy(st[:, 0, 0:TT], ss_x[:]))
                power(TT, 1.0 / D)
                v.tensor_tensor(r_tok[:], st[:, 3, 0:TT], st[:, 2, 0:TT], ALU.mult).then_inc(r_ready, 1)

            normed_no = [0]

            def rows(name, no):
                if name == "f":
                    dve.wait_ge(rows_read, no + 1)
                    bias = b_f[:].unsqueeze(1).broadcast_to([P, TT, NHG])
                    v.tensor_tensor(fl[:, 1], fl[:, 0], bias, ALU.add).then_inc(logf_in, 1)
                    dve.wait_ge(logf_in, 1)
                    dve.wait_ge(logf_ln, 1)
                    v.scalar_tensor_tensor(out=log_f[:], in0=fl[:, 1], scalar=0.0, in1=fl[:, 2],
                                           op0=ALU.min, op1=ALU.subtract).then_inc(logf_ready, 1)
                elif name in ("q2", "k2", "q3", "k3"):
                    w = nat[:, "qk".index(name[0])].rearrange("p s (h n) -> p (s h) n", n=HD)
                    sq = mix[:, 6144:7168].rearrange("p (m n) -> p m n", m=8)
                    dve.wait_ge(rows_read, no + 1)
                    own(v.tensor_tensor(sq, w, w, ALU.mult))
                    own(v.tensor_reduce(st[:, 0, 0:8], sq, AX_X, ALU.add))
                    power(8, 1.0 / HD)
                    own(v.tensor_tensor(st[:, 3], st[:, 3], st[:, 2], ALU.mult))
                    v.tensor_tensor(w, w, st[:, 3].unsqueeze(2).broadcast_to([P, 8, HD]), ALU.mult)\
                     .then_inc(normed, 1)
                    normed_no[0] += 1
                    dve.wait_ge(normed, normed_no[0])
                elif name in ("ckv", "cq"):
                    w = nat[:, ("ckv", "cq").index(name)]
                    dve.wait_ge(squared, 1 + (name == "cq"))
                    power(TT, 1.0 / RANK)
                    own(v.tensor_tensor(st[:, 3, 0:TT], st[:, 3, 0:TT], st[:, 2, 0:TT], ALU.mult))
                    dve.wait_ge(rows_read, no + 1)
                    v.tensor_tensor(w, w, st[:, 3, 0:TT].unsqueeze(2).broadcast_to([P, TT, N]), ALU.mult)\
                     .then_inc(normed, 1)
                    normed_no[0] += 1
                    dve.wait_ge(normed, normed_no[0])
                elif name == "kpe":
                    dve.wait_ge(rows_read, no + 1)
                    own(v.tensor_tensor(kpe_t, kpe, kpe, ALU.mult))
                    own(v.tensor_reduce(kpe_ss[:], kpe_t, AX_X, ALU.add))
                    v.tensor_tensor(kpe_r, kpe, rope_c[:, 1], ALU.mult)
                    v.tensor_tensor(kpe_t[:, :, 0:HALF], kpe[:, :, HALF:ROPE], rope_s[:, 1, :, 0:HALF], ALU.mult)
                    own(v.tensor_tensor(kpe_t[:, :, HALF:ROPE], kpe[:, :, 0:HALF], rope_s[:, 1, :, HALF:ROPE], ALU.mult))
                    own(v.tensor_tensor(kpe_r, kpe_r, kpe_t, ALU.add))
                elif name[:2] == "uq":
                    g = int(name[2])
                    q = q_tok.rearrange("p s h n -> p (s h) n")
                    dve.wait_ge(squared, 2 + 2 * g + 2)
                    own(v.tensor_tensor(st[:, 0, 4:8].rearrange("p (s h) -> p s h", s=TT),
                                        st[:, 0, 4:8].rearrange("p (s h) -> p s h", s=TT),
                                        kpe_ss[:].unsqueeze(2).broadcast_to([P, TT, 2]), ALU.add))
                    power(8, 1.0 / QKD)
                    own(v.tensor_tensor(st[:, 3], st[:, 3], st[:, 2], ALU.mult))
                    dve.wait_ge(rows_read, no + 1)
                    v.tensor_tensor(q, q, st[:, 3, 0:4].unsqueeze(2).broadcast_to([P, 4, QKD]), ALU.mult)\
                     .then_inc(q_scaled, 1)
                    rk = st[:, 3, 4:8].rearrange("p (s h) -> p s h", s=TT)
                    v.tensor_tensor(k_rot, kpe_r.unsqueeze(2).broadcast_to([P, TT, 2, ROPE]),
                                    rk.unsqueeze(3).broadcast_to([P, TT, 2, ROPE]), ALU.mult)
                    v.tensor_tensor(k_tok, kv_tok[:, g % 3, :, :, 0], rk.unsqueeze(3).broadcast_to([P, TT, 2, NOPE]),
                                    ALU.mult).then_inc(normed, 1)
                    normed_no[0] += 1
                    dve.wait_ge(normed, normed_no[0])

            def norm_rows():
                dve.wait_ge(norm_sum, 1 + NB)
                own(v.tensor_copy(st[:, 0, 0:TT], OUT[:, 0:TT]))
                power(TT, 1.0 / D)
                v.tensor_tensor(r_tok[:], st[:, 3, 0:TT], st[:, 2, 0:TT], ALU.mult).then_inc(r_ready, 1)

            def turn_c(n):
                dve.wait_ge(c_hi, n + 1)
                for i in range(2):
                    k = 2 * n + i
                    col = (70 if n < 2 else 66) + k % 4
                    tile = latent_tile(k)
                    ins = v.scalar_tensor_tensor(out=tile[:, 1], in0=psum[:, 7 - n % 2, i * T:(i + 1) * T],
                                                 scalar=gains[:, col:col + 1], in1=tile[:, 0].bitcast(F32),
                                                 op0=ALU.mult, op1=ALU.subtract)
                ins.then_inc(c_ready, 1)

            def scores(n):
                b = n % 2
                dve.wait_ge(scores_done, n + 1)
                if n < NHG:
                    v.tensor_tensor(zm(b), SCORES[:, 0:3 * P], sb_mask[:], ALU.add).then_inc(scores_read, 1)
                    dve.wait_ge(scores_read, n + 1)
                    dve.wait_ge(exp_done, n + 1)
                    v.scalar_tensor_tensor(out=sp(b), in0=zm(b), scalar=0.0, in1=e0, op0=ALU.max, op1=ALU.add)\
                     .then_inc(probs_ready, 1)
                else:
                    for i, c0, c1 in ((0, 0, P), (1, P, 3 * P)):
                        ins = v.tensor_tensor_reduce(out=zm(b)[:, c0:c1], in0=SCORES[:, c0:c1], in1=sm_mask[:, c0:c1],
                                                     scale=1.0, scalar=-3.0e38, op0=ALU.add, op1=ALU.max,
                                                     accum_out=mx[:, b, i:i + 1])
                    ins.then_inc(scores_read, 1)
                    dve.wait_ge(scores_read, n + 1)
                    v.tensor_scalar(nmx[:, b], mx[:, b], -1.0, None, ALU.mult).then_inc(max_ready, 1)
                    dve.wait_ge(exp_done, n + 1)
                    own(v.reciprocal(row_inv[:, b], row_sum[:, b]))
                    v.tensor_scalar(sp(b)[:, 0:P], sp(b)[:, 0:P], row_inv[:, b, 0:1], None, ALU.mult)
                    v.tensor_scalar(sp(b)[:, P:3 * P], sp(b)[:, P:3 * P], row_inv[:, b, 1:2], None, ALU.mult)\
                     .then_inc(probs_ready, 1)

            def probs(n):
                if n < NHG:
                    b = n % 2
                    dve.wait_ge(probs_turned, n + 1)
                    v.tensor_tensor(zm(b), zm(b), PROBS[:, 0:3 * P], ALU.subtract).then_inc(probs_read, 1)

            def head_out(n):
                dve.wait_ge(out_hi, n + 1)
                v.tensor_tensor(a[:, n % KT, 1], OUT[:, 0:T], a[:, n % KT, 0].bitcast(F32), ALU.subtract)\
                 .then_inc(out_ready, 1)

            def next_norm(c, xs, gain_col, piece, extra=0):
                times_gain(c, gain_col)
                split_lo(piece, extra)
                split_h(c)
                norm = xs // 4
                dve.wait_ge(sq_done, xs + 1)
                if c:
                    v.tensor_tensor(sq_sum, sq_sum, sq_new, ALU.add).then_inc(sq_added, 1)
                    dve.wait_ge(sq_added, 3 * norm + c)
                if c == 3:
                    own(v.tensor_tensor(sq_sum[:, 0:2], sq_sum[:, 0:2], sq_sum[:, 2:4], ALU.add))
                    v.tensor_tensor(nacc, sq_sum[:, 0], sq_sum[:, 1], ALU.add).then_inc(acc_ready, 1)

            def mixer(chunks, start, rows_no, cols0, xs0, gain_col):
                n = start
                for name, kind, loads in chunks:
                    for j in range(2 * len(loads)):
                        if not (kind == "cols" and j == 2 * len(loads) - 1):
                            split_lo(n + AHEAD)
                        for what, arg in steps_after(n):
                            if what == "rows":
                                rows(arg, rows_no[arg])
                            elif what == "first_h":
                                times_gain(arg, 0)
                                split_h(arg)
                            elif what == "first_r":
                                first_r()
                            elif what == "norm_rows":
                                norm_rows()
                            elif what not in ("turn", "narrow"):
                                {"turn_c": turn_c, "scores": scores, "probs": probs, "out": head_out}[what](arg)
                        n += 1
                    if kind == "cols":
                        c = int(name[1])
                        xc = xT[:, 4 * c:4 * c + 4]
                        bank = 4 * ((cols0 + c) % 2)
                        dve.wait_ge(right_read, cols0 + c + 1)
                        v.tensor_tensor(y_buf, psum[:, bank:bank + 4, 0:T], s_buf, ALU.add).then_inc(cols_read, 1)
                        dve.wait_ge(cols_read, cols0 + c + 1)
                        v.tensor_tensor(xc, xc, y_buf, ALU.add).then_inc(x_done, 1)
                        dve.wait_ge(x_done, xs0 + c + 1)
                        next_norm(c, xs0 + c, gain_col, n - 1 + AHEAD)

            def mlp_block(base, cols0, blk, final, layer, y0):
                last_layer = layer == 1
                for c in range(8):
                    for j in range(7):
                        n = base + 8 * c + j + AHEAD
                        if not (last_layer and final and c == 7 and j >= 8 - AHEAD):
                            split_lo(n, 64 * blk)
                        if c == 4 and j == 5:
                            dve.wait_ge(norm_sum, (NB + 1) * layer + 1 + blk)
                            v.tensor_scalar(r2, psum[:, 4, 0:T], 1.0 / D, EPS, ALU.mult, ALU.add)\
                             .then_inc(norm_read, 1)
                            dve.wait_ge(norm_read, NB * layer + 1 + blk)
                            v.reciprocal(r2, r2).then_inc(mlp_step, 1)
                            dve.wait_ge(mlp_step, 5 * NB * layer + 1 + 5 * blk)
                    bank = 4 * ((cols0 + c) % 2)
                    dve.wait_ge(right_read, cols0 + c + 1 + 8 * blk)
                    v.tensor_tensor(s_buf, psum[:, bank:bank + 4, 0:T], s_buf, ALU.add).then_inc(cols_read, 1)
                    dve.wait_ge(cols_read, cols0 + c + 1 + 8 * blk)
                    if c < 4:
                        v.scalar_tensor_tensor(out=y_buf, in0=s_buf, scalar=0.0, in1=s_buf, op0=ALU.max,
                                               op1=ALU.mult).then_inc(y_done, 1)
                        split_lo(base + 8 * c + 7 + AHEAD, 64 * blk)
                        dve.wait_ge(y_hi, y0 + c + 1 + 4 * blk)
                        v.tensor_tensor(a[:, 4 * c:4 * c + 4, 1, :], y_buf, a[:, 4 * c:4 * c + 4, 0, :].bitcast(F32),
                                        ALU.subtract).then_inc(split_done, 1)
                    else:
                        xc = xT[:, 4 * c - 16:4 * c - 12]
                        v.tensor_tensor(y_buf, s_buf, r2.unsqueeze(1).broadcast_to([P, 4, T]), ALU.mult)\
                         .then_inc(mlp_step, 1)
                        dve.wait_ge(mlp_step, 5 * NB * layer + c - 2 + 5 * blk)
                        last = v.tensor_tensor(xc, xc, y_buf, ALU.add)
                        if final and not last_layer:
                            last.then_inc(x_done, 1)
                            dve.wait_ge(x_done, 4 + c - 4 + 1)
                            ys[0] = y0 + 4 * NB + c - 4
                            next_norm(c - 4, 4 + c - 4, 16, base + 8 * c + 7 + AHEAD, 64 * blk)
                        elif final:
                            last.then_inc(x_final, 1)
                            if c < 7:
                                split_lo(base + 8 * c + 7 + AHEAD, 64 * blk)
                        else:
                            split_lo(base + 8 * c + 7 + AHEAD, 64 * blk)

            def mlp(base, cols0, layer):
                y0 = ys[0]
                with dve.Fori(0, NB - 1) as blk:
                    mlp_block(base, cols0, blk, False, layer, y0)
                mlp_block(base, cols0, NB - 1, True, layer, y0)

            mixer(MIX0, P_MIX0, ROWS0, COLS_WO0, 0, 32)
            mlp(P_MLP0, COLS_MLP0, 0)
            mixer(MIX1, P_MIX1, ROWS1, COLS_WO1, 8, 48)
            mlp(P_MLP1, COLS_MLP1, 1)
            for c in range(4):
                dve.wait_ge(out_turned, 2 * c + 2)
                v.tensor_copy(raw[:, c, N:2 * N], psum[:, 2 * c + 1]).then_inc(out_read_v, 1)

        @block.tensor
        def _(pe):
            mm = nc.tensor.matmul

            def piece_rows(n, kt0, total_kts, no, src):
                kts, width = shape_of(n)
                hi = half_piece(n, 0).rearrange("p (k n) -> p k n", k=kts)
                lo = half_piece(n, 1).rearrange("p (k n) -> p k n", k=kts)
                for i in range(kts):
                    k = kt0 + i
                    for tt in range(TT):
                        bank = psum[:, 2 * (no % 2) + tt, 0:width]
                        x_hi = src(k, 0)[:, tt * P:(tt + 1) * P]
                        x_lo = src(k, 1)[:, tt * P:(tt + 1) * P]
                        mm(bank, x_hi, hi[:, i], start=(k == 0), stop=False)
                        mm(bank, x_hi, lo[:, i], start=False, stop=False)
                        last = mm(bank, x_lo, hi[:, i], start=False, stop=(k == total_kts - 1))
                return last

            def piece_narrow(n, kt0, no):
                for i in range(shape_of(n)[0]):
                    k = kt0 + i
                    w = narrow_piece(n)[:, i].rearrange("p w n -> p (w n)")
                    last = mm(psum[0:w.shape[1], 2 * (no % 2)], w, h[:, k].rearrange("p s t -> p (s t)"),
                              start=(k == 0), stop=(k == KT - 1))
                return last

            def narrow_back(name, no):
                width = NHG if name == "f" else ROPE
                pe.wait_ge(narrow_out, 1 + (name == "kpe"))
                terms = [(s, w) for s in range(2) for w in range(2)]
                for tt in range(TT):
                    for s, w in terms:
                        ins = mm(psum[:, 2 * (no % 2) + 1, tt * width:(tt + 1) * width],
                                 narrow_t[0:2 * width, s * T + tt * P:s * T + (tt + 1) * P],
                                 ident[0:2 * width, w * width:(w + 1) * width],
                                 start=((s, w) == terms[0]), stop=((s, w) == terms[-1]))
                ins.then_inc(narrow_done, 1)

            def piece_cols(n, j, set_, src):
                for i in range(2):
                    k = 2 * j + i
                    for m in range(4):
                        bank = psum[:, 4 * set_ + m]
                        cols = slice(i * N + m * P, i * N + (m + 1) * P)
                        for which in ((0, 1) if k == 0 else (1, 0)):
                            if which == 0:
                                last = mm(bank, half_piece(n, 0)[:, cols], src[:, k].rearrange("p s t -> p (s t)"),
                                          start=(k == 0), stop=(k == KT - 1))
                            else:
                                last = mm(bank[:, T:2 * T], half_piece(n, 1)[:, cols], src[:, k, 0],
                                          start=False, stop=False)
                return last

            pe.wait_ge(consts, 1)
            for tt in range(TT):
                pe.wait_ge(x_loaded[tt], 16)
                for c in range(4):
                    if (tt, c) == (1, 3):
                        pe.wait_ge(gains_ready, 1)
                    for i in range(4):
                        k = 4 * c + i
                        ins = nc.tensor.transpose(psum[:, 2 * c + tt, i * P:(i + 1) * P],
                                                  raw[:, 2 + tt, k * P:(k + 1) * P], ident[:])
                    ins.then_inc(x_turned, 1)
                if tt == 0:
                    pe.wait_ge(gains_loaded, 16 * len(gain_rows))
                    nc.tensor.transpose(psum[:, 7, 0:76], vec_rows, ident[0:76, 0:76]).then_inc(gains_turned, 1)

            def turn(t):
                if t < 16:
                    g, what, half = t // 4, (t % 4) // 2, t % 2
                    if g < 2:
                        pe.wait_ge(rows_read, 3 * g + what + 1)
                    else:
                        pe.wait_ge(normed, 2 * (g - 2) + what + 1)
                    srcs = [nat[:, what, tt, (2 * half + e) * HD:(2 * half + e + 1) * HD] for e in range(2) for tt in range(TT)]
                else:
                    g, what = (t - 16) // 3, (t - 16) % 3
                    pe.wait_ge(normed, 6 + g + 1)
                    if what == 2:
                        pe.wait_ge(q_roped, g + 1)
                        srcs = [w[:, tt].rearrange("p h n -> p (h n)") for w in (q_rot[:, 0], k_rot) for tt in range(TT)]
                    else:
                        w = (k_tok, q_tok)[what]
                        srcs = [w[:, tt, e, 0:NOPE] for e in range(2) for tt in range(TT)]
                if t:
                    pe.wait_ge(turn_read, t)
                for i, s in enumerate(srcs):
                    ins = nc.tensor.transpose(TURN[:, i * P:(i + 1) * P], s, ident[:])
                ins.then_inc(turned, 1)

            def turn_c(n):
                pe.wait_ge(normed, 5 + n // 2)
                if n >= 2:
                    pe.wait_ge(c_ready, n - 1)
                w = nat[:, n // 2]
                for i in range(2):
                    for tt in range(TT):
                        k = 2 * (n % 2) + i
                        ins = nc.tensor.transpose(psum[:, 7 - n % 2, i * T + tt * P:i * T + (tt + 1) * P],
                                                  w[:, tt, k * P:(k + 1) * P], ident[:])
                ins.then_inc(c_turned, 1)

            def scores(n):
                if n:
                    pe.wait_ge(scores_read, n)
                if n < 16:
                    g, e = n // 4, n % 4
                    pe.wait_ge(turn_read, 4 * g + 4)
                    q, k = qT[:, g % 2, e], kT[:, g % 2, e]
                else:
                    g, e = (n - 16) // 2, n % 2
                    pe.wait_ge(turn_read, 16 + 3 * g + 3)
                    q, k = qT1[:, g % 2, e], kT1[:, g % 2, e]
                    qr, kr = rT1[64 * e:64 * e + 64, g % 2, 0], rT1[64 * e:64 * e + 64, g % 2, 1]
                if n < NHG:
                    mm(SCORES[:, 0:2 * P], k[:, 0:P], q, start=True, stop=True)
                    mm(SCORES[:, 2 * P:3 * P], k[:, P:T], q[:, P:T], start=True, stop=True).then_inc(scores_done, 1)
                    return
                first, second = SCORES[:, 0:P], SCORES[:, P:3 * P]
                if n < 16:
                    pe.wait_ge(decay_ready, n - NHG + 1)
                    d = decay[:, n % 2]
                    gt = ones_gt[:, P:2 * P]
                    mm(first, q[:, 0:P], k[:, 0:P], start=True, stop=False)
                    mm(first, d[:, 0], gt, start=False, stop=True)
                    mm(second, q[:, P:T], k, start=True, stop=False)
                    mm(second[:, 0:P], log_f[:, 0, n - NHG:n - NHG + 1].broadcast_to([P, P]), gt, start=False, stop=False)
                    mm(second, d[:, 1], ones_gt[:], start=False, stop=True).then_inc(scores_done, 1)
                else:
                    mm(first, q[:, 0:P], k[:, 0:P], start=True, stop=False)
                    mm(first, qr[:, 0:P], kr[:, 0:P], start=False, stop=True)
                    mm(second, q[:, P:T], k, start=True, stop=False)
                    mm(second, qr[:, P:T], kr, start=False, stop=True).then_inc(scores_done, 1)

            def probs(n):
                b = n % 2
                pe.wait_ge(probs_ready, n + 1)
                if n:
                    pe.wait_ge(probs_t, n)
                if n < NHG:
                    mm(PROBS[:, 0:3 * P], tri_ge[:], sp(b), start=True, stop=False)
                    mm(PROBS[:, P:2 * P], ones[:], sp(b)[:, 2 * P:3 * P], start=False, stop=True)\
                        .then_inc(probs_turned, 1)
                else:
                    for i in range(3):
                        ins = nc.tensor.transpose(PROBS[:, i * P:(i + 1) * P], sp(b)[:, i * P:(i + 1) * P], ident[:])
                    ins.then_inc(probs_turned, 1)

            def head_out(n):
                b = n % 2
                pe.wait_ge(probs_t, n + 1)
                if n:
                    pe.wait_ge(out_ready, n)
                if n < 16:
                    g, e = n // 4, n % 4
                    pe.wait_ge(rows_read, ROWS0[f"v{g}"] + 1)
                    vs = [v_tok[:, g % 2, tt, e * HD:(e + 1) * HD] for tt in range(TT)]
                else:
                    g, e = (n - 16) // 2, n % 2
                    vs = [kv_tok[:, g % 3, tt, e, 1] for tt in range(TT)]
                mm(OUT[:, 0:T], vs[0], w_t(b)[:, 0:2 * P], start=True, stop=False)
                mm(OUT[:, P:T], vs[1], w_t(b)[:, 2 * P:3 * P], start=False, stop=True).then_inc(out_done, 1)

            def norm_rows():
                pe.wait_ge(acc_ready, 2)
                pe.wait_ge(cols_read, COLS_WO1)
                for tt in range(TT):
                    ins = mm(OUT[:, tt:tt + 1], nacc[:, tt * P:(tt + 1) * P], ones[:, 0:1], start=True, stop=True)
                ins.then_inc(norm_sum, 1)

            def mixer(chunks, start, rows_no, cols0, splits0, heads0):
                n = start
                for name, kind, loads in chunks:
                    count = 2 * len(loads)
                    latent = name[:2] in ("uk", "uq")
                    total = 4 if latent else KT
                    if kind != "cols":
                        no = rows_no[name]
                        if no >= 2:
                            pe.wait_ge(rows_read, no - 1)
                        if name == "ckv":
                            pe.wait_ge(cols_read, cols0 - 1)
                    else:
                        c = int(name[1])
                        if c == 0:
                            pe.wait_ge(rows_read, len(ROWS0) if heads0 == 0 else len(ROWS0) + len(ROWS1))
                        elif c >= 2:
                            pe.wait_ge(cols_read, cols0 + c - 1)
                    for j in range(count):
                        kts, _ = shape_of(n)
                        pe.wait_ge(lo_done, n + 1)
                        if kind == "cols":
                            if c == 0:
                                pe.wait_ge(out_ready, heads0 + 2 * j + 2)
                            last = piece_cols(n, j, (cols0 + c) % 2, a)
                        elif latent:
                            src = 0 if name[:3] == "ukv" else 4
                            pe.wait_ge(c_ready, 2 if src == 0 else 4)
                            last = piece_rows(n, j * kts, total, no, lambda k, s, src=src: latent_tile(src + k)[:, s])
                        else:
                            pe.wait_ge(split_done, splits0 + min(4, (kts * (j + 1) + 3) // 4))
                            if kind == "rows":
                                last = piece_rows(n, j * kts, total, no, lambda k, s: h[:, k, s])
                            else:
                                last = piece_narrow(n, j * kts, no)
                        last.then_inc(pieces_used, 1)
                        for what, arg in steps_after(n):
                            if what == "norm_rows":
                                norm_rows()
                            elif what == "rows" and arg in ("f", "kpe"):
                                narrow_back(arg, rows_no[arg])
                            elif what not in ("rows", "narrow", "first_h", "first_r"):
                                {"turn": turn, "turn_c": turn_c, "scores": scores, "probs": probs,
                                 "out": head_out}[what](arg)
                        n += 1

            def mlp(base, cols0, layer, splits0):
                with pe.Fori(0, NB) as blk:
                    for c in range(8):
                        pe.wait_ge(cols_read, cols0 + c - 1 + 8 * blk)
                        if c == 5:
                            pe.wait_ge(norm_read, NB * layer + 1 + blk)
                        for j in range(8):
                            n = base + 8 * c + j
                            pe.wait_ge(lo_done, n + 1 + 64 * blk)
                            if c == 0:
                                pe.wait_ge(split_done, splits0 + j // 2 + 1 + 4 * blk)
                            if c == 4:
                                pe.wait_ge(split_done, splits0 + 4 + j // 2 + 1 + 4 * blk)
                            last = piece_cols(n, j, (cols0 + c) % 2, h if c < 4 else a)
                            last.then_inc(pieces_used, 1)
                            if c == 4 and j == 5:
                                pe.wait_ge(acc_ready, 2 * layer + 1)
                                pe.wait_ge(cols_read, cols0 + c + 8 * blk)
                                mm(psum[:, 4, 0:T], ones[:], nacc, start=True, stop=True).then_inc(norm_sum, 1)

            pe.wait_ge(consts, 2)
            pe.wait_ge(x_read, 1)
            pe.wait_ge(x_read_v, 1)
            mixer(MIX0, P_MIX0, ROWS0, COLS_WO0, 0, 0)
            mlp(P_MLP0, COLS_MLP0, 0, 4)
            mixer(MIX1, P_MIX1, ROWS1, COLS_WO1, 8 + 4 * NB, 16)
            mlp(P_MLP1, COLS_MLP1, 1, 8 + 4 * NB + 4)
            pe.wait_ge(cols_read, COLS_MLP1 + 8 * NB)
            for c in range(4):
                pe.wait_ge(x_final, c + 1)
                for tt in range(TT):
                    for i in range(4):
                        ins = nc.tensor.transpose(psum[:, 2 * c + tt, i * P:(i + 1) * P],
                                                  xT[:, 4 * c + i, tt * P:(tt + 1) * P], ident[:])
                    ins.then_inc(out_turned, 1)


_INS = ["x", "positions", "ln_mix_g", "ln_mlp_g", "sf_w_in", "sf_b_f", "fox_q_g", "fox_k_g", "sf_w_o",
        "mla_w_down", "mla_q_a_g", "mla_kv_a_g", "mla_w_uq", "mla_w_ukv", "mla_q_g", "mla_k_g",
        "mla_w_o", "mlp_w_up", "mlp_w_down"]


def kernel(**inputs):
    import numpy as _np
    import concourse.bacc as _bacc
    from concourse import mybir as _mybir
    from concourse.bass_utils import run_bass_kernel_spmd as _run

    nc = _bacc.Bacc("TRN2", target_bir_lowering=False, num_devices=1)
    arrays, args = {}, []
    for name in _INS:
        arr = _np.ascontiguousarray(inputs[name])
        arrays[f"in_{name}"] = arr
        args.append(nc.dram_tensor(f"in_{name}", arr.shape, _mybir.dt.from_np(arr.dtype), kind="ExternalInput").ap())
    out = nc.dram_tensor("out_x", (1, T, D), F32, kind="ExternalOutput").ap()
    build(nc, *args, out)
    r = _run(nc, [arrays], core_ids=[0])
    return r.results[0]["out_x"]
```

```python
from contextlib import ExitStack
import math

import numpy as np
import concourse.bass as bass
from concourse import mybir

F32 = mybir.dt.float32
F32R = mybir.dt.float32r
I32 = mybir.dt.int32
ALU = mybir.AluOpType
ACT = mybir.ActivationFunctionType
AX_X = mybir.AxisListType.X

P = 128
T = 256
TT = T // P
D = 2048
KT = D // P
HD = 128
NHG = 8
D_FF = 8192
NB = D_FF // D
RANK = 512
NOPE, ROPE = 128, 64
HALF = ROPE // 2
QKD = NOPE + ROPE
EPS = 1e-6
THETA = 10000.0
NEG = -1e30
SB_SCALE = HD ** -0.5
MLA_SCALE = QKD ** -0.5
N = 512
AHEAD = 4
SLOTS = 4

GROUPS = 4


def plan_chunks():
    def full(matrix, col, width=N, k_tiles=KT):
        return [(matrix, 4, 4 * P * l, col, width) for l in range(k_tiles // 4)]
    first = []
    for g in range(GROUPS):
        if g == 2:
            first.append(("f", "narrow", [("w_in", KT, 0, 6 * NHG * HD, NHG)]))
        for j, what in enumerate("qkv"):
            first.append((f"{what}{g}", "rows", full("w_in", (3 * (g // 2) + j) * NHG * HD + (g % 2) * N)))
    for c in range(4):
        first.append((f"o{c}", "cols", full("w_o", c * N)))
    second = [("ckv", "rows", full("w_down", RANK)),
              ("cq", "rows", full("w_down", 0)),
              ("kpe", "narrow", [("w_down", KT, 0, 2 * RANK, ROPE)])]
    for g in range(8):
        second.append((f"ukv{g}", "rows", full("w_ukv", g * N, N, 4)))
        second.append((f"uq{g}", "rows", full("w_uq", g * 2 * QKD, 2 * QKD, 4)))
    for c in range(4):
        second.append((f"o{c}", "cols", full("mla_w_o", c * N)))
    return first, second


MIX0, MIX1 = plan_chunks()
MLP_PIECES = NB * 64
P_MIX0 = 0
P_MLP0 = 2 * sum(len(c[2]) for c in MIX0)
P_MIX1 = P_MLP0 + MLP_PIECES
P_MLP1 = P_MIX1 + 2 * sum(len(c[2]) for c in MIX1)
P_END = P_MLP1 + MLP_PIECES


def pieces_of(chunks, start):
    out, n = {}, start
    for _, _, loads in chunks:
        for _, kts, _, _, width in loads:
            out[n] = out[n + 1] = (kts // 2, width)
            n += 2
    return out


SHAPES = {**pieces_of(MIX0, P_MIX0), **pieces_of(MIX1, P_MIX1)}


def shape_of(n):
    return SHAPES.get(n, (2, N))


def chunk_starts(chunks, start):
    out, n = {}, start
    for name, _, loads in chunks:
        out[name] = n
        n += 2 * len(loads)
    return out


AT0, AT1 = chunk_starts(MIX0, P_MIX0), chunk_starts(MIX1, P_MIX1)

ROWS0 = {c[0]: n for n, c in enumerate(x for x in MIX0 if x[1] != "cols")}
ROWS1 = {c[0]: n + len(ROWS0) for n, c in enumerate(x for x in MIX1 if x[1] != "cols")}
COLS_WO0, COLS_MLP0, COLS_WO1, COLS_MLP1 = 0, 4, 4 + 8 * NB, 8 + 8 * NB


def plan_steps():
    plan = {}

    def at(n, *steps):
        plan.setdefault(n, []).extend(steps)
    base = [AT0[f"q{g}"] for g in range(GROUPS)]
    for g in range(GROUPS):
        for e in range(4 if g else 0):
            h = 4 * (g - 1) + e
            for what, j in (("scores", 0), ("probs", 2), ("out", 4)):
                at(base[g] + 6 * e + j, (what, h))
        at(base[g] + 12, ("turn", 4 * g))
        at(base[g] + 14, ("turn", 4 * g + 1))
        at(base[g] + 20, ("turn", 4 * g + 2))
        at(base[g] + 22, ("turn", 4 * g + 3))
    o = AT0["o0"]
    for e in range(4):
        at(o + e + 2, ("probs", 12 + e))
    for e in range(4):
        at(min(o + e + 3, o + 5), ("out", 12 + e))
    for e in range(4):
        at(o + e, ("scores", 12 + e))
    at(1, ("first_h", 3))
    at(2, ("square_x", 0))
    at(4, ("square_x", 1))
    at(5, ("first_r", 0))
    at(6, ("gains", 0))
    at(9, ("angles", 0))
    at(11, ("sines", 0))
    at(AT1["ckv"] + 1, ("acc", 0))
    at(AT1["ckv"] + 4, ("norm_rows", 0))
    at(AT1["cq"] + 3, ("turn_c", 0))
    at(AT1["cq"] + 5, ("turn_c", 1))
    at(AT1["ukv0"], ("turn_c", 2), ("turn_c", 3))
    for g in range(8):
        b = [AT1[f"ukv{g + i}"] if g + i < 8 else AT1["o0"] for i in range(2)]
        k, q, ropes = (16 + 3 * g + i for i in range(3))
        if g < 7:
            at(b[1] + 1, ("turn", k))
            at(b[1] + 2, ("turn", q))
            at(b[1] + 3, ("turn", ropes))
    for g in range(6):
        b = [AT1[f"ukv{g + i}"] if g + i < 8 else AT1["o0"] + 4 * (g + i - 8) for i in range(4)]
        h = 16 + 2 * g
        at(b[2] + 1, ("scores", h))
        at(b[2] + 2, ("scores", h + 1))
        at(b[2] + 3, ("probs", h))
        at(b[3], ("out", h), ("probs", h + 1))
        at(b[3] + 1, ("out", h + 1))
    o = AT1["o0"]
    at(o, ("scores", 28), ("turn", 37))
    at(o + 1, ("turn", 38), ("scores", 29))
    at(o + 2, ("turn", 39), ("probs", 28))
    at(o + 3, ("out", 28), ("probs", 29), ("scores", 30))
    at(o + 4, ("out", 29), ("probs", 30), ("scores", 31))
    at(o + 5, ("probs", 31), ("out", 30), ("out", 31))
    for at_, chunks in ((AT0, MIX0), (AT1, MIX1)):
        for name, kind, loads in chunks:
            if kind == "rows":
                at(at_[name] + 2 * len(loads) - 1, ("rows", name))
            elif kind == "narrow":
                at(at_[name] + 1, ("narrow", name))
                at(at_[name] + 2, ("rows", name))
    for n in (AT0["o0"] - 1, AT0["o0"] + 5, AT1["o0"] - 1, AT1["o0"] + 5):
        at(n, ("split", 0))
    plan[AT1["o0"] - 1].sort(key=lambda step: ("turn", "rows", "probs", "split").index(step[0]))
    for n in [*range(P_MIX0, P_MLP0), *range(P_MIX1, P_MLP1)]:
        if not any(what == "split" for what, _ in plan.get(n, [])):
            plan.setdefault(n, []).insert(0, ("split", 0))
    return plan


STEPS = plan_steps()


def steps_after(n):
    return STEPS.get(n, [])


def build(nc, x, positions, ln_mix_g, ln_mlp_g, sf_w_in, sf_b_f, fox_q_g, fox_k_g, sf_w_o,
          mla_w_down, mla_q_a_g, mla_kv_a_g, mla_w_uq, mla_w_ukv, mla_q_g, mla_k_g, mla_w_o,
          mlp_w_up, mlp_w_down, out):
    matrices = {"w_in": sf_w_in[0], "w_o": sf_w_o[0], "w_down": mla_w_down[0], "w_ukv": mla_w_ukv[0],
                "w_uq": mla_w_uq[0], "mla_w_o": mla_w_o[0]}
    with ExitStack() as ctx:
        def sb(name, shape, dt=F32):
            return ctx.enter_context(nc.sbuf_tensor(name, shape, dt))

        def sem(name):
            return ctx.enter_context(nc.semaphore(name))

        xT = sb("xT", [P, KT, T])
        h = sb("h", [P, KT, 2, T], F32R)
        a = sb("a", [P, KT, 2, T], F32R)
        raw = sb("raw", [P, SLOTS, 4 * N])
        halves = sb("halves", [P, SLOTS, 2, 2 * N], F32R)
        nat = sb("nat", [P, 2, TT, N])
        mix = sb("mix", [P, 8192])
        heads = sb("heads", [P, 7, 3 * P])
        side = sb("side", [P, 4, P])
        ident = sb("ident", [P, P])
        ones = sb("ones", [P, P])
        tri_ge = sb("tri_ge", [P, P])
        tri_le = sb("tri_le", [P, P])
        ones_gt = sb("ones_gt", [P, 2 * P])
        sb_mask = sb("sb_mask", [P, 3 * P])
        sm_mask = sb("sm_mask", [P, 3 * P])
        gains = sb("gains", [P, 76])
        q_gain = sb("q_gain", [P, 2])
        rope_g = sb("rope_g", [P, 2, ROPE])
        b_f = sb("b_f", [P, NHG])
        fl = sb("fl", [P, 3, TT, NHG])
        log_f = sb("log_f", [P, TT, NHG])
        pos_i = sb("pos_i", [P, TT], I32)
        pos_f = sb("pos_f", [P, TT])
        inv_freq = sb("inv_freq", [P, HALF])
        rope_c = sb("rope_c", [P, 2, TT, ROPE])
        rope_s = sb("rope_s", [P, 2, TT, ROPE])
        kpe_ss = sb("kpe_ss", [P, TT])
        st = sb("st", [P, 4, 8])
        ss_x = sb("ss_x", [P, TT])
        r_tok = sb("r_tok", [P, TT])
        mx = sb("mx", [P, 2, 2])
        nmx = sb("nmx", [P, 2, 2])
        row_sum = sb("row_sum", [P, 2, 2])
        row_inv = sb("row_inv", [P, 2, 2])

        qT = mix[:, 0:2048].rearrange("p (b h t) -> p b h t", b=2, h=4)
        kT = mix[:, 2048:4096].rearrange("p (b h t) -> p b h t", b=2, h=4)
        v_tok = mix[:, 4096:6144].rearrange("p (b s n) -> p b s n", b=2, s=TT)
        qT1 = mix[:, 0:1024].rearrange("p (b h t) -> p b h t", b=2, h=2)
        kT1 = mix[:, 1024:2048].rearrange("p (b h t) -> p b h t", b=2, h=2)
        rT1 = mix[:, 2048:3072].rearrange("p (b w t) -> p b w t", b=2, w=2)
        kv_tok = mix[:, 3072:6144].rearrange("p (b s h w n) -> p b s h w n", b=3, s=TT, h=2, w=2)
        q_tok = mix[:, 6144:6912].rearrange("p (s h n) -> p s h n", s=TT, h=2)
        k_tok = mix[:, 6912:7424].rearrange("p (s h n) -> p s h n", s=TT, h=2)
        q_rot = mix[:, 7424:7936].rearrange("p (w s h n) -> p w s h n", w=2, s=TT, h=2)
        k_rot = mix[:, 7936:8192].rearrange("p (s h n) -> p s h n", s=TT, h=2)
        o_buf = nat[:, 1, :, T:2 * T]
        narrow_t = nat[:, 0, 0]
        sq_tok = nat[:, 0].rearrange("p s n -> p (s n)")[:, 0:4 * QKD].rearrange("p (m n) -> p m n", m=4)
        gain_in = nat[0:32, 0, 0, 0:P], nat[0:44, 0, 1, 0:P]
        x_in = mix[:, 0:TT * D].rearrange("p (s n) -> p s n", s=TT)
        decay = side[:].rearrange("p (b s) t -> p b s t", b=2)
        kpe = side[:, 0].rearrange("p (s n) -> p s n", s=TT)
        kpe_r = side[:, 1].rearrange("p (s n) -> p s n", s=TT)
        kpe_t = side[:, 2].rearrange("p (s n) -> p s n", s=TT)
        r2 = heads[:, 0, 0:T]
        nacc = heads[:, 1, 0:T]
        ang = heads[:, 2, 0:2 * TT * HALF].rearrange("p (w s n) -> p w s n", w=2, s=TT)
        trig_n = heads[:, 3, 0:TT * HALF].rearrange("p (s n) -> p s n", s=TT)
        trig = heads[:, 4, 0:2 * TT * HALF].rearrange("p (w s n) -> p w s n", w=2, s=TT)
        sq_sum = mix[:, 0:1024].rearrange("p (k t) -> p k t", k=4)
        sq_new = mix[:, 2048:3072].rearrange("p (k t) -> p k t", k=4)
        s_buf = nat[:, 0].rearrange("p s (k t) -> p (s k) t", t=T)
        y_buf = nat[:, 1].rearrange("p s (k t) -> p (s k) t", t=T)
        zm, e0, sp, w_t = (lambda b: heads[:, b], heads[:, 2], lambda b: heads[:, 3 + b], lambda b: heads[:, 5 + b])

        def out_on_pool(n):
            return 16 <= n < 30

        def latent_tile(k):
            return a[:, 12 + k] if k < 4 else h[:, k]

        psum = ctx.enter_context(nc.psum_tensor("psum", [P, 8, N], F32))
        SCORES, PROBS, OUT, TURN = psum[:, 4], psum[:, 5], psum[:, 6], psum[:, 7]

        raw_loaded = [sem(f"raw_loaded{i}") for i in range(SLOTS)]
        x_loaded = [[sem(f"x_loaded{i}{j}") for j in range(TT)] for i in range(2)]
        first_loaded = sem("first_loaded")
        gain0_loaded = sem("gain0_loaded")
        pos_loaded, gains_loaded, vecs_loaded = sem("pos_loaded"), sem("gains_loaded"), sem("vecs_loaded")
        hi_done, lo_done = sem("hi_done"), sem("lo_done")
        pieces_used = sem("pieces_used")
        r_ready = sem("r_ready")
        rows_read, cols_read = sem("rows_read"), sem("cols_read")
        right_read = sem("right_read")
        consts = sem("consts")
        const_step = sem("const_step")
        x_turned, x_read = sem("x_turned"), sem("x_read")
        x_read_v = sem("x_read_v")
        gains_turned, gains_ready = sem("gains_turned"), sem("gains_ready")
        y_done, y_hi = sem("y_done"), sem("y_hi")
        split_done = sem("split_done")
        x_done = sem("x_done")
        sq_done, sq_added = sem("sq_done"), sem("sq_added")
        acc_ready = sem("acc_ready")
        norm_sum, norm_read = sem("norm_sum"), sem("norm_read")
        mlp_step = sem("mlp_step")
        rows_stat, rows_ln = sem("rows_stat"), sem("rows_ln")
        squared = sem("squared")
        narrow_out, narrow_done = sem("narrow_out"), sem("narrow_done")
        normed = sem("normed")
        trig_args, trig_done, rope_ready = sem("trig_args"), sem("trig_done"), sem("rope_ready")
        logf_in, logf_abs, logf_ln, logf_ready = sem("logf_in"), sem("logf_abs"), sem("logf_ln"), sem("logf_ready")
        turned, turn_read = sem("turned"), sem("turn_read")
        c_turned, c_hi, c_ready = sem("c_turned"), sem("c_hi"), sem("c_ready")
        q_scaled, q_roped = sem("q_scaled"), sem("q_roped")
        pool_step = sem("pool_step")
        scores_done, scores_read = sem("scores_done"), sem("scores_read")
        decay_ready = sem("decay_ready")
        max_ready = sem("max_ready")
        exp_done = sem("exp_done")
        probs_ready = sem("probs_ready")
        probs_turned, probs_read, probs_t = sem("probs_turned"), sem("probs_read"), sem("probs_t")
        out_done, out_hi, out_ready = sem("out_done"), sem("out_hi"), sem("out_ready")
        out_copied = sem("out_copied")
        rk_ready, k_scaled = sem("rk_ready"), sem("k_scaled")
        act_step, dve_step = sem("act_step"), sem("dve_step")
        x_final, out_turned, out_stored = sem("x_final"), sem("out_turned"), sem("out_stored")
        out_read, out_read_v = sem("out_read"), sem("out_read_v")

        block = ctx.enter_context(nc.Block())

        def flat(kts, width):
            return kts * width

        def narrow(n):
            return shape_of(n)[1] in (NHG, ROPE)

        def raw_piece(n):
            kts, width = shape_of(n)
            size = flat(kts, width)
            piece = raw[:, (n // 2) % SLOTS, (n % 2) * size:(n % 2 + 1) * size]
            return piece.rearrange("p (k n) -> p k n", k=kts) if narrow(n) else piece

        def narrow_piece(n):
            kts, width = shape_of(n)
            return halves[:, n % SLOTS].rearrange("p w n -> p (w n)")[:, 0:2 * kts * width]\
                .rearrange("p (k w n) -> p k w n", k=kts, w=2)

        def half_piece(n, which):
            kts, width = shape_of(n)
            if narrow(n):
                return narrow_piece(n)[:, :, which]
            return halves[:, n % SLOTS, which, 0:flat(kts, width)]

        gain_rows = [(ln_mlp_g.rearrange("l (k p) -> (l k) p", p=P), 0, 32),
                     (mla_q_a_g.rearrange("a (k p) -> (a k) p", p=P), 34, 4),
                     (mla_kv_a_g.rearrange("a (k p) -> (a k) p", p=P), 38, 4),
                     (fox_q_g, 32, 1), (fox_k_g, 33, 1), (mla_q_g[:, 0:NOPE], 42, 1), (mla_k_g[:, 0:NOPE], 43, 1)]

        @block.sync
        def _(sp_):
            def free_slot(load, extra=0):
                if load >= SLOTS:
                    sp_.wait_ge(lo_done, 2 * load - 2 * SLOTS + 2 + 2 * extra)
                    if not isinstance(extra, int):
                        sp_.nop()

            def straight(chunks, load):
                for _, _, loads in chunks:
                    for matrix, kts, row, col, width in loads:
                        free_slot(load)
                        dst = raw[:, load % SLOTS, 0:kts * width].rearrange("p (k n) -> p k n", k=kts)
                        src = matrices[matrix][row:row + kts * P, col:col + width].rearrange("(k p) n -> p k n", p=P)
                        if load == 0:
                            sp_.dma_start(dst[:, 0:2], src[:, 0:2]).then_inc(first_loaded, 16)
                            load_x(1)
                            sp_.dma_start(dst[:, 2:4], src[:, 2:4]).then_inc(raw_loaded[0], 16)
                        else:
                            sp_.dma_start(dst, src).then_inc(raw_loaded[load % SLOTS], 16)
                        load += 1
                        if load == 2:
                            for src, first, count in gain_rows:
                                sp_.dma_start(gain_in[1][first:first + count], src).then_inc(gains_loaded, 16)
                            sp_.dma_start(pos_i[:], positions[0].rearrange("(s p) -> p s", p=P),
                                          allow_slow_non_contiguous=True).then_inc(pos_loaded, 16)
                            for dst, src in ((rope_g[:, 0, :], mla_q_g[0, NOPE:QKD]),
                                             (rope_g[:, 1, :], mla_k_g[0, NOPE:QKD]), (b_f[:], sf_b_f[0])):
                                sp_.dma_start(dst, src.partition_broadcast(P)).then_inc(vecs_loaded, 16)

            def mlp(layer, load0):
                w_up, w_down = mlp_w_up[layer], mlp_w_down[layer]
                with sp_.Fori(0, NB) as b:
                    for c in range(8):
                        for l in range(4):
                            load = load0 + 4 * c + l
                            free_slot(load, 32 * b)
                            dst = raw[:, load % SLOTS].rearrange("p (k n) -> p k n", k=4)
                            if c < 4:
                                src = w_up[4 * P * l:4 * P * (l + 1), bass.ds(b * D + c * N, N)]
                            else:
                                src = w_down[bass.ds(b * D + 4 * P * l, 4 * P), (c - 4) * N:(c - 3) * N]
                            sp_.dma_start(dst, src.rearrange("(k p) n -> p k n", p=P))\
                               .then_inc(raw_loaded[load % SLOTS], 16)

            def load_x(half):
                for tt in range(TT):
                    cols = slice(half * D // 2, (half + 1) * D // 2)
                    sp_.dma_start(x_in[:, tt, cols], x[0, tt * P:(tt + 1) * P, cols]).then_inc(x_loaded[half][tt], 16)

            load_x(0)
            straight(MIX0, 0)
            mlp(0, P_MLP0 // 2)
            straight(MIX1, P_MIX1 // 2)
            mlp(1, P_MLP1 // 2)
            for c in range(4):
                sp_.wait_ge(out_read, min(2 * c + 2, 7))
                if c == 3:
                    sp_.wait_ge(out_read_v, 1)
                sp_.dma_start(out[0, :, c * N:(c + 1) * N].rearrange("(s p) n -> p s n", p=P),
                              raw[:, c, 0:2 * N].rearrange("p (s n) -> p s n", s=TT)).then_inc(out_stored, 16)
            sp_.wait_ge(out_stored, 64)

        @block.gpsimd
        def _(pool):
            made = [0]

            def own(ins):
                made[0] += 1
                ins.then_inc(const_step, 1)
                pool.wait_ge(const_step, made[0])

            own(pool.memset(ident[:], 0.0))
            pool.affine_select(out=ident[:], in_=ident[:], compare_op=ALU.not_equal, fill=1.0, base=0,
                               pattern=[[-1, P]], channel_multiplier=1).then_inc(consts, 1)
            own(pool.memset(ones[:], 1.0))
            pool.memset(ones_gt[:, 0:P], 1.0)
            own(pool.memset(sb_mask[:], 0.0))
            own(pool.memset(sm_mask[:], 0.0))
            pool.affine_select(out=tri_ge[:], in_=ones[:], compare_op=ALU.is_ge, fill=0.0, base=0,
                               pattern=[[-1, P]], channel_multiplier=1)
            pool.affine_select(out=tri_le[:], in_=ones[:], compare_op=ALU.is_ge, fill=0.0, base=0,
                               pattern=[[1, P]], channel_multiplier=-1)
            pool.affine_select(out=ones_gt[:, P:2 * P], in_=ones[:], compare_op=ALU.is_gt, fill=0.0, base=0,
                               pattern=[[-1, P]], channel_multiplier=1)
            for c in (0, 2 * P):
                pool.affine_select(out=sb_mask[:, c:c + P], in_=sb_mask[:, c:c + P], compare_op=ALU.is_gt,
                                   fill=NEG, base=0, pattern=[[1, P]], channel_multiplier=-1)
                last = pool.affine_select(out=sm_mask[:, c:c + P], in_=sm_mask[:, c:c + P], compare_op=ALU.is_ge,
                                          fill=NEG, base=0, pattern=[[-1, P]], channel_multiplier=1)
            last.then_inc(consts, 1)

            pool.wait_ge(logf_ready, 1)
            for n in range(NHG):
                if n >= 2:
                    pool.wait_ge(scores_done, NHG + n - 1)
                for tt in range(TT):
                    ins = pool.tensor_scalar(decay[:, n % 2, tt], tri_le[:], log_f[:, tt, n:n + 1], None, ALU.mult)
                ins.then_inc(decay_ready, 1)

            pool.wait_ge(rope_ready, 1)
            step = [0]

            def mine(ins):
                step[0] += 1
                ins.then_inc(pool_step, 1)
                pool.wait_ge(pool_step, step[0])

            def split_out(n):
                pool.wait_ge(out_copied, n - 15)
                mine(pool.tensor_copy(a[:, n % KT, 0], o_buf[:, n % 2]))
                pool.tensor_tensor(a[:, n % KT, 1], o_buf[:, n % 2], a[:, n % KT, 0].bitcast(F32), ALU.subtract)\
                    .then_inc(out_ready, 1)

            for g in range(8):
                pool.wait_ge(rk_ready, g + 1)
                rk = st[:, 3, 4:8].rearrange("p (s h) -> p s h", s=TT).unsqueeze(3)
                pool.tensor_tensor(k_tok, kv_tok[:, g % 3, :, :, 0], rk.broadcast_to([P, TT, 2, NOPE]), ALU.mult)\
                    .then_inc(k_scaled, 1)
                if g:
                    pool.wait_ge(turned, 16 + 3 * g)
                pool.tensor_tensor(k_rot, kpe_r.unsqueeze(2).broadcast_to([P, TT, 2, ROPE]),
                                   rk.broadcast_to([P, TT, 2, ROPE]), ALU.mult)
                pool.wait_ge(q_scaled, g + 1)
                for tt in range(TT):
                    q = q_tok[:, tt, :, NOPE:QKD]
                    cs = rope_c[:, 0, tt].unsqueeze(1).broadcast_to([P, 2, ROPE])
                    s1 = rope_s[:, 0, tt, 0:HALF].unsqueeze(1).broadcast_to([P, 2, HALF])
                    s2 = rope_s[:, 0, tt, HALF:ROPE].unsqueeze(1).broadcast_to([P, 2, HALF])
                    pool.tensor_tensor(q_rot[:, 0, tt], q, cs, ALU.mult)
                    pool.tensor_tensor(q_rot[:, 1, tt, :, 0:HALF], q[:, :, HALF:ROPE], s1, ALU.mult)
                    ins = pool.tensor_tensor(q_rot[:, 1, tt, :, HALF:ROPE], q[:, :, 0:HALF], s2, ALU.mult)
                mine(ins)
                pool.tensor_tensor(q_rot[:, 0], q_rot[:, 0], q_rot[:, 1], ALU.add).then_inc(q_roped, 1)
                pool.wait_ge(q_roped, g + 1)
                if g >= 2:
                    split_out(16 + 2 * (g - 2))
                    split_out(16 + 2 * (g - 2) + 1)
            for n in (28, 29):
                split_out(n)

        @block.scalar
        def _(act):
            own_steps = [0]

            def own(ins):
                own_steps[0] += 1
                ins.then_inc(act_step, 1)
                act.wait_ge(act_step, own_steps[0])

            def split_hi(n, extra=0):
                if n == 0:
                    act.wait_ge(first_loaded, 16)
                elif n % 2 == 0 or n == 1:
                    act.wait_ge(raw_loaded[(n // 2) % SLOTS], 16 * (n // 2 // SLOTS + 1) + 16 // (2 * SLOTS) * extra)
                if n >= SLOTS:
                    act.wait_ge(pieces_used, n - SLOTS + 1 + extra)
                nc.scalar.copy(half_piece(n, 0), raw_piece(n)).then_inc(hi_done, 1)

            powers = [0]

            def power(m):
                powers[0] += 1
                act.wait_ge(rows_stat, powers[0])
                own(nc.scalar.activation(st[:, 3, 0:m], st[:, 1, 0:m], ACT.Ln))
                nc.scalar.activation(st[:, 2, 0:m], st[:, 3, 0:m], ACT.Exp, scale=-0.5).then_inc(rows_ln, 1)

            ys = [0]

            def round_y(dst):
                ys[0] += 1
                act.wait_ge(y_done, ys[0])
                nc.scalar.copy(dst, y_buf).then_inc(y_hi, 1)

            act.dma_start(gain_in[0], ln_mix_g.rearrange("l (k p) -> (l k) p", p=P)).then_inc(gain0_loaded, 16)
            act.preload_act_table_set("natural_log_exp_and_others")

            def read_x(c):
                act.wait_ge(x_turned, 2 * c + 1)
                nc.scalar.copy(xT[:, 4 * c:4 * c + 4, 0:P], psum[:, 2 * c].rearrange("p (k t) -> p k t", k=4))\
                  .then_inc(x_read, 1)

            def square_x(tt):
                for half in range(2):
                    act.wait_ge(x_loaded[half][tt], 16)
                own(nc.scalar.activation(a[:, 8 * tt:8 * tt + 4].rearrange("p k s t -> p (k s t)"), x_in[:, tt],
                                         ACT.Square, accum_out=ss_x[:, tt:tt + 1]))

            read_x(0)
            read_x(1)
            round_y(h[:, 0:4, 0, :])
            split_hi(0)
            read_x(2)
            split_hi(1)
            round_y(h[:, 4:8, 0, :])
            split_hi(2)
            read_x(3)
            split_hi(3)
            round_y(h[:, 8:12, 0, :])

            def evict(dst, src, scale=None):
                if scale is None:
                    return nc.scalar.copy(dst, src)
                return nc.scalar.activation(dst, src, ACT.Copy, scale=scale)

            def square_rows(pairs):
                for src, junk, total, scale in pairs:
                    ins = nc.scalar.activation(junk, src, ACT.Square, accum_out=total,
                                               **({} if scale is None else {"scale": scale}))
                ins.then_inc(squared, 1)

            def narrow_copy(name, last_piece, no):
                act.wait_ge(pieces_used, last_piece + 1)
                width = shape_of(last_piece)[1]
                nc.scalar.copy(narrow_t[0:2 * width], psum[0:2 * width, 2 * (no % 2)]).then_inc(narrow_out, 1)

            def rows(name, last_piece, no):
                if name in ("f", "kpe"):
                    act.wait_ge(narrow_done, 1 + (name == "kpe"))
                    act.wait_ge(r_ready, 1 + (name == "kpe"))
                    for tt in range(TT):
                        dst, width = (fl[:, 0, tt], NHG) if name == "f" else (kpe[:, tt], ROPE)
                        ins = evict(dst, psum[:, 2 * (no % 2) + 1, tt * width:(tt + 1) * width], r_tok[:, tt:tt + 1])
                else:
                    ins = wide_rows(name, last_piece, no)
                ins.then_inc(rows_read, 1)
                if name == "uq7":
                    act.wait_ge(rows_read, no + 1)
                    square_rows([(q_tok[:, tt, e], sq_tok[:, 2 * tt + e], st[:, 0, 2 * tt + e:1 + 2 * tt + e], None)
                                 for tt in range(TT) for e in range(2)])
                if name == "f":
                    act.wait_ge(logf_in, 1)
                    own(nc.scalar.activation(fl[:, 2], fl[:, 1], ACT.Abs))
                    own(nc.scalar.activation(fl[:, 0], fl[:, 2], ACT.Exp, scale=-1.0))
                    nc.scalar.activation(fl[:, 2], fl[:, 0], ACT.Ln, bias=1.0).then_inc(logf_ln, 1)
                if name in ("q2", "k2", "q3", "k3"):
                    power(8)
                elif name in ("ckv", "cq"):
                    power(TT)
                elif name[:2] == "uq":
                    power(8)

            def wide_rows(name, last_piece, no):
                act.wait_ge(pieces_used, last_piece + 1)
                act.wait_ge(r_ready, 1 + (no >= len(ROWS0)))
                banks = [psum[:, 2 * (no % 2) + tt] for tt in range(TT)]
                if name in ("ckv", "cq"):
                    square_rows([(banks[tt], mix[:, 7168 + tt * N:7168 + (tt + 1) * N], st[:, 0, tt:tt + 1],
                                  r_tok[:, tt:tt + 1]) for tt in range(TT)])
                elif name[:3] == "ukv":
                    square_rows([(banks[tt][:, 2 * e * HD:2 * e * HD + NOPE], nat[:, 1, tt, e * NOPE:(e + 1) * NOPE],
                                  st[:, 0, 4 + 2 * tt + e:5 + 2 * tt + e], None) for tt in range(TT) for e in range(2)])
                elif name[:2] == "uq":
                    if int(name[2]):
                        act.wait_ge(turned, 16 + 3 * int(name[2]))
                    if name != "uq7":
                        square_rows([(banks[tt][:, e * QKD:(e + 1) * QKD], sq_tok[:, 2 * tt + e],
                                      st[:, 0, 2 * tt + e:1 + 2 * tt + e], None) for tt in range(TT) for e in range(2)])
                elif name in ("q2", "k2", "q3", "k3"):
                    square_rows([(banks[tt][:, e * HD:(e + 1) * HD], mix[:, 6144 + (4 * tt + e) * HD:6144 + (4 * tt + e + 1) * HD],
                                  st[:, 0, 4 * tt + e:4 * tt + e + 1], r_tok[:, tt:tt + 1]) for tt in range(TT) for e in range(4)])
                for tt in range(TT):
                    r = r_tok[:, tt:tt + 1]
                    if name[0] in "qk":
                        ins = evict(nat[:, "qk".index(name[0]), tt], banks[tt], r)
                    elif name[0] == "v":
                        ins = evict(v_tok[:, int(name[1]) % 2, tt], banks[tt], r)
                    elif name == "ckv":
                        ins = evict(nat[:, 0, tt], banks[tt], r)
                    elif name == "cq":
                        ins = evict(nat[:, 1, tt], banks[tt], r)
                    elif name[:3] == "ukv":
                        ins = evict(kv_tok[:, int(name[3]) % 3, tt].rearrange("p h w n -> p (h w n)"), banks[tt])
                    else:
                        ins = evict(q_tok[:, tt].rearrange("p h n -> p (h n)"), banks[tt][:, 0:2 * QKD])
                return ins

            def turn(t):
                if t < 16:
                    act.wait_ge(turned, t + 1)
                    g, what, half = t // 4, (t % 4) // 2, t % 2
                    dst = (qT, kT)[what][:, g % 2, 2 * half:2 * half + 2]
                    scale = ((SB_SCALE, None), (q_gain[:, 0:1], gains[:, 65:66]))[g // 2][what]
                    evict(dst, TURN.rearrange("p (h t) -> p h t", h=2), scale).then_inc(turn_read, 1)

            def turn_c(n):
                act.wait_ge(c_turned, n + 1)
                for i in range(2):
                    k = 2 * n + i
                    col = (70 if n < 2 else 66) + k % 4
                    ins = nc.scalar.activation(latent_tile(k)[:, 0], psum[:, 7 - n % 2, i * T:(i + 1) * T], ACT.Copy,
                                               scale=gains[:, col:col + 1])
                ins.then_inc(c_hi, 1)

            def scores(n):
                b = n % 2
                if n < NHG:
                    act.wait_ge(scores_read, n + 1)
                    own(nc.scalar.activation(e0, zm(b), ACT.Abs))
                    own(nc.scalar.activation(w_t(b), e0, ACT.Exp, scale=-1.0))
                    nc.scalar.activation(e0, w_t(b), ACT.Ln, bias=1.0).then_inc(exp_done, 1)
                else:
                    act.wait_ge(max_ready, n - NHG + 1)
                    nc.scalar.activation(sp(b)[:, 0:P], zm(b)[:, 0:P], ACT.Exp, bias=nmx[:, b, 0:1],
                                         accum_out=row_sum[:, b, 0:1])
                    nc.scalar.activation(sp(b)[:, P:3 * P], zm(b)[:, P:3 * P], ACT.Exp, bias=nmx[:, b, 1:2],
                                         accum_out=row_sum[:, b, 1:2]).then_inc(exp_done, 1)

            def probs(n):
                b = n % 2
                if n < NHG:
                    act.wait_ge(probs_read, n + 1)
                    nc.scalar.activation(w_t(b), zm(b), ACT.Exp).then_inc(probs_t, 1)
                else:
                    act.wait_ge(probs_turned, n + 1)
                    nc.scalar.copy(w_t(b), PROBS[:, 0:3 * P]).then_inc(probs_t, 1)

            def head_out(n):
                act.wait_ge(out_done, n + 1)
                if not out_on_pool(n):
                    nc.scalar.copy(a[:, n % KT, 0], OUT[:, 0:T]).then_inc(out_hi, 1)
                else:
                    if n >= 18:
                        act.wait_ge(out_ready, n - 1)
                    nc.scalar.copy(o_buf[:, n % 2], OUT[:, 0:T]).then_inc(out_copied, 1)

            def right_half(cols, end):
                act.wait_ge(pieces_used, end)
                nc.scalar.copy(s_buf, psum[:, 4 * (cols % 2):4 * (cols % 2) + 4, T:2 * T]).then_inc(right_read, 1)

            def next_norm(c, xs):
                norm = xs // 4
                round_y(h[:, 4 * c:4 * c + 4, 0, :])
                act.wait_ge(x_done, xs + 1)
                if c == 0 and norm:
                    act.wait_ge(acc_ready, norm)
                if c and 3 * norm + c - 1:
                    act.wait_ge(sq_added, 3 * norm + c - 1)
                nc.scalar.activation(sq_new if c else sq_sum, xT[:, 4 * c:4 * c + 4], ACT.Square).then_inc(sq_done, 1)

            def mixer(chunks, start, rows_no, cols0, xs0):
                n = start
                for name, kind, loads in chunks:
                    for j in range(2 * len(loads)):
                        for what, arg in steps_after(n):
                            if what == "split":
                                if not (kind == "cols" and j == 2 * len(loads) - 1):
                                    split_hi(n + AHEAD)
                            elif what == "rows":
                                rows(arg, n, rows_no[arg])
                            elif what == "narrow":
                                narrow_copy(arg, n, rows_no[arg])
                            elif what == "first_h":
                                round_y(h[:, 4 * arg:4 * arg + 4, 0, :])
                            elif what == "first_r":
                                power(TT)
                            elif what == "square_x":
                                square_x(arg)
                            elif what == "sines":
                                act.wait_ge(trig_args, 1)
                                nc.scalar.activation(trig, ang, ACT.Sin).then_inc(trig_done, 1)
                                act.preload_act_table_set("natural_log_exp_and_others")
                            elif what in ("gains", "angles", "acc"):
                                pass
                            elif what == "norm_rows":
                                power(TT)
                            else:
                                {"turn": turn, "turn_c": turn_c, "scores": scores, "probs": probs,
                                 "out": head_out}[what](arg)
                        n += 1
                    if kind == "cols":
                        c = int(name[1])
                        right_half(cols0 + c, n)
                        split_hi(n - 1 + AHEAD)
                        next_norm(c, xs0 + c)

            def mlp_block(base, cols0, blk, final, last_layer, y0):
                for c in range(8):
                    for j in range(7):
                        n = base + 8 * c + j + AHEAD
                        if not (last_layer and final and c == 7 and j >= 8 - AHEAD):
                            split_hi(n, 64 * blk)
                    right_half(cols0 + c, base + 8 * c + 8 + 64 * blk)
                    if not (last_layer and final and c == 7):
                        split_hi(base + 8 * c + 7 + AHEAD, 64 * blk)
                    if c < 4:
                        act.wait_ge(y_done, y0 + c + 1 + 4 * blk)
                        nc.scalar.copy(a[:, 4 * c:4 * c + 4, 0, :], y_buf).then_inc(y_hi, 1)
                    elif final and not last_layer:
                        ys[0] = y0 + 4 * NB + c - 4
                        next_norm(c - 4, 4 + c - 4)

            def mlp(base, cols0, last_layer):
                y0 = ys[0]
                with act.Fori(0, NB - 1) as blk:
                    mlp_block(base, cols0, blk, False, last_layer, y0)
                mlp_block(base, cols0, NB - 1, True, last_layer, y0)

            mixer(MIX0, P_MIX0, ROWS0, COLS_WO0, 0)
            mlp(P_MLP0, COLS_MLP0, False)
            mixer(MIX1, P_MIX1, ROWS1, COLS_WO1, 8)
            mlp(P_MLP1, COLS_MLP1, True)
            for c in range(4):
                for tt in range(2 if c < 3 else 1):
                    act.wait_ge(out_turned, 2 * c + tt + 1)
                    nc.scalar.copy(raw[:, c, tt * N:(tt + 1) * N], psum[:, 2 * c + tt]).then_inc(out_read, 1)

        @block.vector
        def _(dve):
            own_steps = [0]

            def own(ins):
                own_steps[0] += 1
                ins.then_inc(dve_step, 1)
                dve.wait_ge(dve_step, own_steps[0])

            v = nc.vector

            def split_lo(n, extra=0):
                dve.wait_ge(hi_done, n + 1 + extra)
                v.tensor_tensor(half_piece(n, 1), raw_piece(n), half_piece(n, 0).bitcast(F32), ALU.subtract)\
                 .then_inc(lo_done, 1)

            stats = [0]

            def power(m, inv_count):
                v.tensor_scalar(st[:, 1, 0:m], st[:, 0, 0:m], inv_count, EPS, ALU.mult, ALU.add).then_inc(rows_stat, 1)
                stats[0] += 1
                dve.wait_ge(rows_stat, stats[0])
                dve.wait_ge(rows_ln, stats[0])
                own(v.tensor_tensor(st[:, 3, 0:m], st[:, 2, 0:m], st[:, 2, 0:m], ALU.mult))
                own(v.tensor_tensor(st[:, 3, 0:m], st[:, 3, 0:m], st[:, 1, 0:m], ALU.mult))
                own(v.tensor_scalar(st[:, 3, 0:m], st[:, 3, 0:m], -0.5, 1.5, ALU.mult, ALU.add))

            splits = [0]
            ys = [0]

            def split_y(dst_lo, dst_hi):
                ys[0] += 1
                dve.wait_ge(y_hi, ys[0])
                v.tensor_tensor(dst_lo, y_buf, dst_hi.bitcast(F32), ALU.subtract).then_inc(split_done, 1)

            def times_gain(c, gain_col):
                g = gains[:, gain_col + 4 * c:gain_col + 4 * c + 4].unsqueeze(2).broadcast_to([P, 4, T])
                if ys[0]:
                    dve.wait_ge(split_done, ys[0])
                v.tensor_tensor(y_buf, xT[:, 4 * c:4 * c + 4], g, ALU.mult).then_inc(y_done, 1)
                dve.wait_ge(y_done, ys[0] + 1)

            def split_h(c):
                split_y(h[:, 4 * c:4 * c + 4, 1, :], h[:, 4 * c:4 * c + 4, 0, :])

            for i in range(HALF):
                v.memset(inv_freq[:, i:i + 1], float(np.float32(THETA ** (-i / HALF))))
            def angles():
                dve.wait_ge(pos_loaded, 16)
                own(v.tensor_copy(pos_f[:], pos_i[:]))
                for tt in range(TT):
                    ins = v.tensor_scalar(ang[:, 0, tt], inv_freq[:], pos_f[:, tt:tt + 1], None, ALU.mult)
                own(ins)
                magic = 1.5 * 2.0 ** 23
                parts, rest = [], 2 * math.pi
                for bits in (5, 14, 25, 40):
                    part = math.floor(rest * 2.0 ** bits) / 2.0 ** bits
                    parts.append(part)
                    rest -= part
                for stride in (4096.0, 1.0):
                    own(v.tensor_scalar(trig_n, ang[:, 0], 1.0 / (2 * math.pi * stride), magic, ALU.mult, ALU.add))
                    own(v.tensor_scalar(trig_n, trig_n, -magic, None, ALU.add))
                    for part in parts:
                        own(v.scalar_tensor_tensor(out=ang[:, 0], in0=trig_n, scalar=-part * stride, in1=ang[:, 0],
                                                   op0=ALU.mult, op1=ALU.add))
                own(v.tensor_scalar(ang[:, 1], ang[:, 0], math.pi / 2, None, ALU.add))
                own(v.tensor_scalar(trig_n, ang[:, 1], math.pi, -2 * math.pi, ALU.is_gt, ALU.mult))
                own(v.tensor_tensor(ang[:, 1], ang[:, 1], trig_n, ALU.add))
                limit = float(np.nextafter(np.float32(math.pi), np.float32(0)))
                v.tensor_scalar(ang, ang, limit, -limit, ALU.min, ALU.max).then_inc(trig_args, 1)

            dve.wait_ge(gains_turned, 1)
            v.tensor_copy(gains[:, 0:32], psum[:, 7, 0:32]).then_inc(gains_ready, 1)
            dve.wait_ge(gains_ready, 1)

            def other_gains():
                dve.wait_ge(gains_turned, 2)
                own(v.tensor_copy(gains[:, 32:76], psum[:, 7, 0:44]))
                v.tensor_scalar(q_gain[:, 0:1], gains[:, 64:65], SB_SCALE, None, ALU.mult)
                v.tensor_scalar(q_gain[:, 1:2], gains[:, 74:75], MLA_SCALE, None, ALU.mult).then_inc(gains_ready, 1)

            def read_x(c):
                dve.wait_ge(x_turned, 2 * c + 2)
                v.tensor_copy(xT[:, 4 * c:4 * c + 4, P:T], psum[:, 2 * c + 1].rearrange("p (k t) -> p k t", k=4))\
                 .then_inc(x_read_v, 1)

            def first_h(c):
                dve.wait_ge(x_read, c + 1)
                dve.wait_ge(x_read_v, c + 1)
                times_gain(c, 0)

            read_x(0)
            first_h(0)
            read_x(1)
            split_h(0)
            split_lo(0)
            first_h(1)
            split_lo(1)
            read_x(2)
            split_h(1)
            split_lo(2)
            first_h(2)
            read_x(3)
            split_lo(3)
            split_h(2)


            def rope_tables():
                dve.wait_ge(trig_done, 1)
                dve.wait_ge(vecs_loaded, 16 * 3)
                for i, scale in ((0, MLA_SCALE), (1, 1.0)):
                    g1 = rope_g[:, i, 0:HALF].unsqueeze(1).broadcast_to([P, TT, HALF])
                    g2 = rope_g[:, i, HALF:ROPE].unsqueeze(1).broadcast_to([P, TT, HALF])
                    for dst, j, s, g in ((rope_c[:, i, :, 0:HALF], 1, scale, g1), (rope_c[:, i, :, HALF:ROPE], 1, scale, g2),
                                         (rope_s[:, i, :, 0:HALF], 0, -scale, g2), (rope_s[:, i, :, HALF:ROPE], 0, scale, g1)):
                        ins = v.scalar_tensor_tensor(out=dst, in0=trig[:, j], scalar=s, in1=g, op0=ALU.mult, op1=ALU.mult)
                ins.then_inc(rope_ready, 1)
                dve.wait_ge(rope_ready, 1)

            def first_r():
                dve.wait_ge(act_step, 2)
                own(v.tensor_copy(st[:, 0, 0:TT], ss_x[:]))
                power(TT, 1.0 / D)
                v.tensor_tensor(r_tok[:], st[:, 3, 0:TT], st[:, 2, 0:TT], ALU.mult).then_inc(r_ready, 1)

            normed_no = [0]

            def rows(name, no):
                if name == "f":
                    dve.wait_ge(rows_read, no + 1)
                    bias = b_f[:].unsqueeze(1).broadcast_to([P, TT, NHG])
                    v.tensor_tensor(fl[:, 1], fl[:, 0], bias, ALU.add).then_inc(logf_in, 1)
                    dve.wait_ge(logf_in, 1)
                    dve.wait_ge(logf_ln, 1)
                    v.scalar_tensor_tensor(out=log_f[:], in0=fl[:, 1], scalar=0.0, in1=fl[:, 2],
                                           op0=ALU.min, op1=ALU.subtract).then_inc(logf_ready, 1)
                elif name in ("q2", "k2", "q3", "k3"):
                    w = nat[:, "qk".index(name[0])].rearrange("p s (h n) -> p (s h) n", n=HD)
                    dve.wait_ge(squared, 1 + ("q2", "k2", "q3", "k3").index(name))
                    power(8, 1.0 / HD)
                    dve.wait_ge(rows_read, no + 1)
                    own(v.tensor_tensor(st[:, 3], st[:, 3], st[:, 2], ALU.mult))
                    v.tensor_tensor(w, w, st[:, 3].unsqueeze(2).broadcast_to([P, 8, HD]), ALU.mult)\
                     .then_inc(normed, 1)
                    normed_no[0] += 1
                    dve.wait_ge(normed, normed_no[0])
                elif name in ("ckv", "cq"):
                    w = nat[:, ("ckv", "cq").index(name)]
                    dve.wait_ge(squared, 5 + (name == "cq"))
                    power(TT, 1.0 / RANK)
                    own(v.tensor_tensor(st[:, 3, 0:TT], st[:, 3, 0:TT], st[:, 2, 0:TT], ALU.mult))
                    dve.wait_ge(rows_read, no + 1)
                    v.tensor_tensor(w, w, st[:, 3, 0:TT].unsqueeze(2).broadcast_to([P, TT, N]), ALU.mult)\
                     .then_inc(normed, 1)
                    normed_no[0] += 1
                    dve.wait_ge(normed, normed_no[0])
                elif name == "kpe":
                    dve.wait_ge(rows_read, no + 1)
                    own(v.tensor_tensor(kpe_t, kpe, kpe, ALU.mult))
                    own(v.tensor_reduce(kpe_ss[:], kpe_t, AX_X, ALU.add))
                    v.tensor_tensor(kpe_r, kpe, rope_c[:, 1], ALU.mult)
                    v.tensor_tensor(kpe_t[:, :, 0:HALF], kpe[:, :, HALF:ROPE], rope_s[:, 1, :, 0:HALF], ALU.mult)
                    own(v.tensor_tensor(kpe_t[:, :, HALF:ROPE], kpe[:, :, 0:HALF], rope_s[:, 1, :, HALF:ROPE], ALU.mult))
                    own(v.tensor_tensor(kpe_r, kpe_r, kpe_t, ALU.add))
                elif name[:2] == "uq":
                    g = int(name[2])
                    q = q_tok.rearrange("p s h n -> p (s h) n")
                    dve.wait_ge(squared, 6 + 2 * g + 2)
                    own(v.tensor_tensor(st[:, 0, 4:8].rearrange("p (s h) -> p s h", s=TT),
                                        st[:, 0, 4:8].rearrange("p (s h) -> p s h", s=TT),
                                        kpe_ss[:].unsqueeze(2).broadcast_to([P, TT, 2]), ALU.add))
                    power(8, 1.0 / QKD)
                    v.tensor_tensor(st[:, 3], st[:, 3], st[:, 2], ALU.mult).then_inc(rk_ready, 1)
                    dve.wait_ge(rk_ready, g + 1)
                    dve.wait_ge(rows_read, no + 1)
                    v.tensor_tensor(q, q, st[:, 3, 0:4].unsqueeze(2).broadcast_to([P, 4, QKD]), ALU.mult)\
                     .then_inc(q_scaled, 1)

            def norm_rows():
                dve.wait_ge(norm_sum, 1 + NB)
                own(v.tensor_copy(st[:, 0, 0:TT], OUT[:, 0:TT]))
                power(TT, 1.0 / D)
                v.tensor_tensor(r_tok[:], st[:, 3, 0:TT], st[:, 2, 0:TT], ALU.mult).then_inc(r_ready, 1)

            def turn(t):
                dve.wait_ge(turned, t + 1)
                g, what = (t - 16) // 3, (t - 16) % 3
                dst = (kT1, qT1, rT1)[what][:, g % 2]
                src = TURN.rearrange("p (h t) -> p h t", h=2)
                if what == 2:
                    ins = v.tensor_copy(dst, src)
                else:
                    ins = v.tensor_scalar(dst, src, (gains[:, 75:76], q_gain[:, 1:2])[what], None, ALU.mult)
                ins.then_inc(turn_read, 1)

            def turn_c(n):
                dve.wait_ge(c_hi, n + 1)
                for i in range(2):
                    k = 2 * n + i
                    col = (70 if n < 2 else 66) + k % 4
                    tile = latent_tile(k)
                    ins = v.scalar_tensor_tensor(out=tile[:, 1], in0=psum[:, 7 - n % 2, i * T:(i + 1) * T],
                                                 scalar=gains[:, col:col + 1], in1=tile[:, 0].bitcast(F32),
                                                 op0=ALU.mult, op1=ALU.subtract)
                ins.then_inc(c_ready, 1)

            def scores(n, piece):
                b = n % 2
                dve.wait_ge(scores_done, n + 1)
                if n < NHG:
                    v.tensor_tensor(zm(b), SCORES[:, 0:3 * P], sb_mask[:], ALU.add).then_inc(scores_read, 1)
                    dve.wait_ge(scores_read, n + 1)
                    split_lo(piece)
                    dve.wait_ge(exp_done, n + 1)
                    v.scalar_tensor_tensor(out=sp(b), in0=zm(b), scalar=0.0, in1=e0, op0=ALU.max, op1=ALU.add)\
                     .then_inc(probs_ready, 1)
                else:
                    for i, c0, c1 in ((0, 0, P), (1, P, 3 * P)):
                        ins = v.tensor_tensor_reduce(out=zm(b)[:, c0:c1], in0=SCORES[:, c0:c1], in1=sm_mask[:, c0:c1],
                                                     scale=1.0, scalar=-3.0e38, op0=ALU.add, op1=ALU.max,
                                                     accum_out=mx[:, b, i:i + 1])
                    ins.then_inc(scores_read, 1)
                    dve.wait_ge(scores_read, n + 1)
                    v.tensor_scalar(nmx[:, b], mx[:, b], -1.0, None, ALU.mult).then_inc(max_ready, 1)
                    split_lo(piece)
                    dve.wait_ge(exp_done, n + 1)
                    own(v.reciprocal(row_inv[:, b], row_sum[:, b]))
                    v.tensor_scalar(sp(b)[:, 0:P], sp(b)[:, 0:P], row_inv[:, b, 0:1], None, ALU.mult)
                    v.tensor_scalar(sp(b)[:, P:3 * P], sp(b)[:, P:3 * P], row_inv[:, b, 1:2], None, ALU.mult)\
                     .then_inc(probs_ready, 1)

            def probs(n):
                if n < NHG:
                    b = n % 2
                    dve.wait_ge(probs_turned, n + 1)
                    v.tensor_tensor(zm(b), zm(b), PROBS[:, 0:3 * P], ALU.subtract).then_inc(probs_read, 1)

            def head_out(n):
                if not out_on_pool(n):
                    dve.wait_ge(out_hi, n + 1 if n < 16 else n - 13)
                    v.tensor_tensor(a[:, n % KT, 1], OUT[:, 0:T], a[:, n % KT, 0].bitcast(F32), ALU.subtract)\
                     .then_inc(out_ready, 1)

            def next_norm(c, xs, gain_col, piece, extra=0):
                times_gain(c, gain_col)
                split_lo(piece, extra)
                split_h(c)
                if xs != 7:
                    add_squares(c, xs)

            def add_squares(c, xs):
                norm = xs // 4
                dve.wait_ge(sq_done, xs + 1)
                if c:
                    v.tensor_tensor(sq_sum, sq_sum, sq_new, ALU.add).then_inc(sq_added, 1)
                    dve.wait_ge(sq_added, 3 * norm + c)
                if c == 3:
                    own(v.tensor_tensor(sq_sum[:, 0:2], sq_sum[:, 0:2], sq_sum[:, 2:4], ALU.add))
                    v.tensor_tensor(nacc, sq_sum[:, 0], sq_sum[:, 1], ALU.add).then_inc(acc_ready, 1)

            def mixer(chunks, start, rows_no, cols0, xs0, gain_col):
                n = start
                for name, kind, loads in chunks:
                    for j in range(2 * len(loads)):
                        fill = any(what == "scores" for what, _ in steps_after(n))
                        for what, arg in steps_after(n):
                            if what == "split":
                                if not (fill or (kind == "cols" and j == 2 * len(loads) - 1)):
                                    split_lo(n + AHEAD)
                            elif what == "scores":
                                scores(arg, n + AHEAD)
                            elif what == "rows":
                                rows(arg, rows_no[arg])
                            elif what == "first_h":
                                first_h(arg)
                                split_h(arg)
                            elif what == "gains":
                                other_gains()
                            elif what == "acc":
                                add_squares(3, 7)
                            elif what == "angles":
                                angles()
                            elif what == "sines":
                                rope_tables()
                            elif what == "first_r":
                                first_r()
                            elif what == "norm_rows":
                                norm_rows()
                            elif what == "turn":
                                if arg >= 16:
                                    turn(arg)
                            elif what not in ("narrow", "square_x"):
                                {"turn_c": turn_c, "probs": probs, "out": head_out}[what](arg)
                        n += 1
                    if kind == "cols":
                        c = int(name[1])
                        xc = xT[:, 4 * c:4 * c + 4]
                        bank = 4 * ((cols0 + c) % 2)
                        dve.wait_ge(right_read, cols0 + c + 1)
                        v.tensor_tensor(y_buf, psum[:, bank:bank + 4, 0:T], s_buf, ALU.add).then_inc(cols_read, 1)
                        dve.wait_ge(cols_read, cols0 + c + 1)
                        v.tensor_tensor(xc, xc, y_buf, ALU.add).then_inc(x_done, 1)
                        dve.wait_ge(x_done, xs0 + c + 1)
                        next_norm(c, xs0 + c, gain_col, n - 1 + AHEAD)

            def mlp_block(base, cols0, blk, final, layer, y0):
                last_layer = layer == 1
                for c in range(8):
                    for j in range(7):
                        n = base + 8 * c + j + AHEAD
                        if not (last_layer and final and c == 7 and j >= 8 - AHEAD):
                            split_lo(n, 64 * blk)
                        if c == 4 and j == 5:
                            dve.wait_ge(norm_sum, (NB + 1) * layer + 1 + blk)
                            v.tensor_scalar(r2, psum[:, 4, 0:T], 1.0 / D, EPS, ALU.mult, ALU.add)\
                             .then_inc(norm_read, 1)
                            dve.wait_ge(norm_read, NB * layer + 1 + blk)
                            v.reciprocal(r2, r2).then_inc(mlp_step, 1)
                            dve.wait_ge(mlp_step, 5 * NB * layer + 1 + 5 * blk)
                    bank = 4 * ((cols0 + c) % 2)
                    dve.wait_ge(right_read, cols0 + c + 1 + 8 * blk)
                    v.tensor_tensor(s_buf, psum[:, bank:bank + 4, 0:T], s_buf, ALU.add).then_inc(cols_read, 1)
                    dve.wait_ge(cols_read, cols0 + c + 1 + 8 * blk)
                    if c < 4:
                        v.scalar_tensor_tensor(out=y_buf, in0=s_buf, scalar=0.0, in1=s_buf, op0=ALU.max,
                                               op1=ALU.mult).then_inc(y_done, 1)
                        split_lo(base + 8 * c + 7 + AHEAD, 64 * blk)
                        dve.wait_ge(y_hi, y0 + c + 1 + 4 * blk)
                        v.tensor_tensor(a[:, 4 * c:4 * c + 4, 1, :], y_buf, a[:, 4 * c:4 * c + 4, 0, :].bitcast(F32),
                                        ALU.subtract).then_inc(split_done, 1)
                    else:
                        xc = xT[:, 4 * c - 16:4 * c - 12]
                        v.tensor_tensor(y_buf, s_buf, r2.unsqueeze(1).broadcast_to([P, 4, T]), ALU.mult)\
                         .then_inc(mlp_step, 1)
                        dve.wait_ge(mlp_step, 5 * NB * layer + c - 2 + 5 * blk)
                        if final and last_layer and c == 7:
                            for part in (slice(0, 2), slice(2, 4)):
                                v.tensor_tensor(xc[:, part], xc[:, part], y_buf[:, part], ALU.add).then_inc(x_final, 1)
                            continue
                        last = v.tensor_tensor(xc, xc, y_buf, ALU.add)
                        if final and not last_layer:
                            last.then_inc(x_done, 1)
                            dve.wait_ge(x_done, 4 + c - 4 + 1)
                            ys[0] = y0 + 4 * NB + c - 4
                            next_norm(c - 4, 4 + c - 4, 16, base + 8 * c + 7 + AHEAD, 64 * blk)
                        elif final:
                            last.then_inc(x_final, 1)
                            split_lo(base + 8 * c + 7 + AHEAD, 64 * blk)
                        else:
                            split_lo(base + 8 * c + 7 + AHEAD, 64 * blk)

            def mlp(base, cols0, layer):
                y0 = ys[0]
                with dve.Fori(0, NB - 1) as blk:
                    mlp_block(base, cols0, blk, False, layer, y0)
                mlp_block(base, cols0, NB - 1, True, layer, y0)

            mixer(MIX0, P_MIX0, ROWS0, COLS_WO0, 0, 32)
            mlp(P_MLP0, COLS_MLP0, 0)
            mixer(MIX1, P_MIX1, ROWS1, COLS_WO1, 8, 48)
            mlp(P_MLP1, COLS_MLP1, 1)
            dve.wait_ge(out_turned, 8)
            v.tensor_copy(raw[:, 3, N:2 * N], psum[:, 7]).then_inc(out_read_v, 1)

        @block.tensor
        def _(pe):
            mm = nc.tensor.matmul

            def piece_rows(n, kt0, total_kts, no, src):
                kts, width = shape_of(n)
                hi = half_piece(n, 0).rearrange("p (k n) -> p k n", k=kts)
                lo = half_piece(n, 1).rearrange("p (k n) -> p k n", k=kts)
                for i in range(kts):
                    k = kt0 + i
                    for tt in range(TT):
                        bank = psum[:, 2 * (no % 2) + tt, 0:width]
                        x_hi = src(k, 0)[:, tt * P:(tt + 1) * P]
                        x_lo = src(k, 1)[:, tt * P:(tt + 1) * P]
                        mm(bank, x_hi, hi[:, i], start=(k == 0), stop=False)
                        mm(bank, x_hi, lo[:, i], start=False, stop=False)
                        last = mm(bank, x_lo, hi[:, i], start=False, stop=(k == total_kts - 1))
                return last

            def piece_narrow(n, kt0, no):
                for i in range(shape_of(n)[0]):
                    k = kt0 + i
                    w = narrow_piece(n)[:, i].rearrange("p w n -> p (w n)")
                    last = mm(psum[0:w.shape[1], 2 * (no % 2)], w, h[:, k].rearrange("p s t -> p (s t)"),
                              start=(k == 0), stop=(k == KT - 1))
                return last

            def narrow_back(name, no):
                width = NHG if name == "f" else ROPE
                pe.wait_ge(narrow_out, 1 + (name == "kpe"))
                terms = [(s, w) for s in range(2) for w in range(2)]
                for tt in range(TT):
                    for s, w in terms:
                        ins = mm(psum[:, 2 * (no % 2) + 1, tt * width:(tt + 1) * width],
                                 narrow_t[0:2 * width, s * T + tt * P:s * T + (tt + 1) * P],
                                 ident[0:2 * width, w * width:(w + 1) * width],
                                 start=((s, w) == terms[0]), stop=((s, w) == terms[-1]))
                ins.then_inc(narrow_done, 1)

            def piece_cols(n, j, set_, src):
                for i in range(2):
                    k = 2 * j + i
                    for m in range(4):
                        bank = psum[:, 4 * set_ + m]
                        cols = slice(i * N + m * P, i * N + (m + 1) * P)
                        for which in ((0, 1) if k == 0 else (1, 0)):
                            if which == 0:
                                last = mm(bank, half_piece(n, 0)[:, cols], src[:, k].rearrange("p s t -> p (s t)"),
                                          start=(k == 0), stop=(k == KT - 1))
                            else:
                                last = mm(bank[:, T:2 * T], half_piece(n, 1)[:, cols], src[:, k, 0],
                                          start=False, stop=False)
                return last

            pe.wait_ge(consts, 1)
            pe.wait_ge(gain0_loaded, 16)
            nc.tensor.transpose(psum[:, 7, 0:32], gain_in[0], ident[0:32, 0:32]).then_inc(gains_turned, 1)
            for c in range(4):
                for tt in range(TT):
                    pe.wait_ge(x_loaded[c // 2][tt], 16)
                    if (c, tt) == (3, 1):
                        pe.wait_ge(gains_ready, 1)
                    for i in range(4):
                        k = 4 * c + i
                        ins = nc.tensor.transpose(psum[:, 2 * c + tt, i * P:(i + 1) * P],
                                                  x_in[:, tt, k * P:(k + 1) * P], ident[:])
                    ins.then_inc(x_turned, 1)

            def other_gains():
                pe.wait_ge(gains_loaded, 16 * len(gain_rows))
                pe.wait_ge(x_read_v, 4)
                nc.tensor.transpose(psum[:, 7, 0:44], gain_in[1], ident[0:44, 0:44]).then_inc(gains_turned, 1)

            def turn(t):
                if t < 16:
                    g, what, half = t // 4, (t % 4) // 2, t % 2
                    if g < 2:
                        pe.wait_ge(rows_read, 3 * g + what + 1)
                    else:
                        pe.wait_ge(normed, 2 * (g - 2) + what + 1)
                    srcs = [nat[:, what, tt, (2 * half + e) * HD:(2 * half + e + 1) * HD] for e in range(2) for tt in range(TT)]
                else:
                    g, what = (t - 16) // 3, (t - 16) % 3
                    pe.wait_ge((k_scaled, q_scaled, q_roped)[what], g + 1)
                    if what == 2:
                        srcs = [w[:, tt].rearrange("p h n -> p (h n)") for w in (q_rot[:, 0], k_rot) for tt in range(TT)]
                    else:
                        w = (k_tok, q_tok)[what]
                        srcs = [w[:, tt, e, 0:NOPE] for e in range(2) for tt in range(TT)]
                if t:
                    pe.wait_ge(turn_read, t)
                for i, s in enumerate(srcs):
                    ins = nc.tensor.transpose(TURN[:, i * P:(i + 1) * P], s, ident[:])
                ins.then_inc(turned, 1)

            def turn_c(n):
                pe.wait_ge(normed, 5 + n // 2)
                if n >= 2:
                    pe.wait_ge(c_ready, n - 1)
                w = nat[:, n // 2]
                for i in range(2):
                    for tt in range(TT):
                        k = 2 * (n % 2) + i
                        ins = nc.tensor.transpose(psum[:, 7 - n % 2, i * T + tt * P:i * T + (tt + 1) * P],
                                                  w[:, tt, k * P:(k + 1) * P], ident[:])
                ins.then_inc(c_turned, 1)

            def scores(n):
                if n:
                    pe.wait_ge(scores_read, n)
                if n < 16:
                    g, e = n // 4, n % 4
                    pe.wait_ge(turn_read, 4 * g + 4)
                    q, k = qT[:, g % 2, e], kT[:, g % 2, e]
                else:
                    g, e = (n - 16) // 2, n % 2
                    pe.wait_ge(turn_read, 16 + 3 * g + 3)
                    q, k = qT1[:, g % 2, e], kT1[:, g % 2, e]
                    qr, kr = rT1[64 * e:64 * e + 64, g % 2, 0], rT1[64 * e:64 * e + 64, g % 2, 1]
                if n < NHG:
                    mm(SCORES[:, 0:2 * P], k[:, 0:P], q, start=True, stop=True)
                    mm(SCORES[:, 2 * P:3 * P], k[:, P:T], q[:, P:T], start=True, stop=True).then_inc(scores_done, 1)
                    return
                first, second = SCORES[:, 0:P], SCORES[:, P:3 * P]
                if n < 16:
                    pe.wait_ge(decay_ready, n - NHG + 1)
                    d = decay[:, n % 2]
                    gt = ones_gt[:, P:2 * P]
                    mm(first, q[:, 0:P], k[:, 0:P], start=True, stop=False)
                    mm(first, d[:, 0], gt, start=False, stop=True)
                    mm(second, q[:, P:T], k, start=True, stop=False)
                    mm(second[:, 0:P], log_f[:, 0, n - NHG:n - NHG + 1].broadcast_to([P, P]), gt, start=False, stop=False)
                    mm(second, d[:, 1], ones_gt[:], start=False, stop=True).then_inc(scores_done, 1)
                else:
                    mm(first, q[:, 0:P], k[:, 0:P], start=True, stop=False)
                    mm(first, qr[:, 0:P], kr[:, 0:P], start=False, stop=True)
                    mm(second, q[:, P:T], k, start=True, stop=False)
                    mm(second, qr[:, P:T], kr, start=False, stop=True).then_inc(scores_done, 1)

            def probs(n):
                b = n % 2
                pe.wait_ge(probs_ready, n + 1)
                if n:
                    pe.wait_ge(probs_t, n)
                if n < NHG:
                    mm(PROBS[:, 0:3 * P], tri_ge[:], sp(b), start=True, stop=False)
                    mm(PROBS[:, P:2 * P], ones[:], sp(b)[:, 2 * P:3 * P], start=False, stop=True)\
                        .then_inc(probs_turned, 1)
                else:
                    for i in range(3):
                        ins = nc.tensor.transpose(PROBS[:, i * P:(i + 1) * P], sp(b)[:, i * P:(i + 1) * P], ident[:])
                    ins.then_inc(probs_turned, 1)

            def head_out(n):
                b = n % 2
                pe.wait_ge(probs_t, n + 1)
                if n and out_on_pool(n - 1):
                    pe.wait_ge(out_copied, n - 16)
                elif n:
                    pe.wait_ge(out_ready, n)
                if n < 16:
                    g, e = n // 4, n % 4
                    pe.wait_ge(rows_read, ROWS0[f"v{g}"] + 1)
                    vs = [v_tok[:, g % 2, tt, e * HD:(e + 1) * HD] for tt in range(TT)]
                else:
                    g, e = (n - 16) // 2, n % 2
                    vs = [kv_tok[:, g % 3, tt, e, 1] for tt in range(TT)]
                mm(OUT[:, 0:T], vs[0], w_t(b)[:, 0:2 * P], start=True, stop=False)
                mm(OUT[:, P:T], vs[1], w_t(b)[:, 2 * P:3 * P], start=False, stop=True).then_inc(out_done, 1)

            def norm_rows():
                pe.wait_ge(acc_ready, 2)
                pe.wait_ge(cols_read, COLS_WO1)
                for tt in range(TT):
                    ins = mm(OUT[:, tt:tt + 1], nacc[:, tt * P:(tt + 1) * P], ones[:, 0:1], start=True, stop=True)
                ins.then_inc(norm_sum, 1)

            def mixer(chunks, start, rows_no, cols0, splits0, heads0):
                n = start
                for name, kind, loads in chunks:
                    count = 2 * len(loads)
                    latent = name[:2] in ("uk", "uq")
                    total = 4 if latent else KT
                    if kind != "cols":
                        no = rows_no[name]
                        if no >= 2:
                            pe.wait_ge(rows_read, no - 1)
                        if name == "ckv":
                            pe.wait_ge(cols_read, cols0 - 1)
                    else:
                        c = int(name[1])
                        if c == 0:
                            pe.wait_ge(rows_read, len(ROWS0) if heads0 == 0 else len(ROWS0) + len(ROWS1))
                        elif c >= 2:
                            pe.wait_ge(cols_read, cols0 + c - 1)
                    for j in range(count):
                        kts, _ = shape_of(n)
                        pe.wait_ge(lo_done, n + 1)
                        if kind == "cols":
                            if c == 0:
                                pe.wait_ge(out_ready, heads0 + 2 * j + 2)
                            last = piece_cols(n, j, (cols0 + c) % 2, a)
                        elif latent:
                            src = 0 if name[:3] == "ukv" else 4
                            pe.wait_ge(c_ready, 2 if src == 0 else 4)
                            last = piece_rows(n, j * kts, total, no, lambda k, s, src=src: latent_tile(src + k)[:, s])
                        else:
                            pe.wait_ge(split_done, splits0 + min(4, (kts * (j + 1) + 3) // 4))
                            if kind == "rows":
                                last = piece_rows(n, j * kts, total, no, lambda k, s: h[:, k, s])
                            else:
                                last = piece_narrow(n, j * kts, no)
                        last.then_inc(pieces_used, 1)
                        for what, arg in steps_after(n):
                            if what == "norm_rows":
                                norm_rows()
                            elif what == "gains":
                                other_gains()
                            elif what == "rows" and arg in ("f", "kpe"):
                                narrow_back(arg, rows_no[arg])
                            elif what in ("turn", "turn_c", "scores", "probs", "out"):
                                {"turn": turn, "turn_c": turn_c, "scores": scores, "probs": probs,
                                 "out": head_out}[what](arg)
                        n += 1

            def mlp(base, cols0, layer, splits0):
                with pe.Fori(0, NB) as blk:
                    for c in range(8):
                        pe.wait_ge(cols_read, cols0 + c - 1 + 8 * blk)
                        if c == 5:
                            pe.wait_ge(norm_read, NB * layer + 1 + blk)
                        for j in range(8):
                            n = base + 8 * c + j
                            pe.wait_ge(lo_done, n + 1 + 64 * blk)
                            if c == 0:
                                pe.wait_ge(split_done, splits0 + j // 2 + 1 + 4 * blk)
                            if c == 4:
                                pe.wait_ge(split_done, splits0 + 4 + j // 2 + 1 + 4 * blk)
                            last = piece_cols(n, j, (cols0 + c) % 2, h if c < 4 else a)
                            last.then_inc(pieces_used, 1)
                            if c == 4 and j == 5:
                                pe.wait_ge(acc_ready, 2 * layer + 1)
                                pe.wait_ge(cols_read, cols0 + c + 8 * blk)
                                mm(psum[:, 4, 0:T], ones[:], nacc, start=True, stop=True).then_inc(norm_sum, 1)

            pe.wait_ge(consts, 2)
            pe.wait_ge(x_read, 1)
            pe.wait_ge(x_read_v, 1)
            mixer(MIX0, P_MIX0, ROWS0, COLS_WO0, 0, 0)
            mlp(P_MLP0, COLS_MLP0, 0, 4)
            mixer(MIX1, P_MIX1, ROWS1, COLS_WO1, 8 + 4 * NB, 16)
            mlp(P_MLP1, COLS_MLP1, 1, 8 + 4 * NB + 4)
            for c in range(4):
                pe.wait_ge(cols_read, COLS_MLP1 + 8 * NB - (1 if c < 2 else 0))
                for part in range(2):
                    pe.wait_ge(x_final, c + 1 + (part if c == 3 else 0))
                    for tt in range(TT):
                        for i in (2 * part, 2 * part + 1):
                            ins = nc.tensor.transpose(psum[:, 2 * c + tt, i * P:(i + 1) * P],
                                                      xT[:, 4 * c + i, tt * P:(tt + 1) * P], ident[:])
                        if part:
                            ins.then_inc(out_turned, 1)


_INS = ["x", "positions", "ln_mix_g", "ln_mlp_g", "sf_w_in", "sf_b_f", "fox_q_g", "fox_k_g", "sf_w_o",
        "mla_w_down", "mla_q_a_g", "mla_kv_a_g", "mla_w_uq", "mla_w_ukv", "mla_q_g", "mla_k_g",
        "mla_w_o", "mlp_w_up", "mlp_w_down"]


def kernel(**inputs):
    import numpy as _np
    import concourse.bacc as _bacc
    from concourse import mybir as _mybir
    from concourse.bass_utils import run_bass_kernel_spmd as _run

    nc = _bacc.Bacc("TRN2", target_bir_lowering=False, num_devices=1)
    arrays, args = {}, []
    for name in _INS:
        arr = _np.ascontiguousarray(inputs[name])
        arrays[f"in_{name}"] = arr
        args.append(nc.dram_tensor(f"in_{name}", arr.shape, _mybir.dt.from_np(arr.dtype), kind="ExternalInput").ap())
    out = nc.dram_tensor("out_x", (1, T, D), F32, kind="ExternalOutput").ap()
    build(nc, *args, out)
    r = _run(nc, [arrays], core_ids=[0])
    return r.results[0]["out_x"]
```
